# Optimizing a Trainium2 kernel written in Bass

```python
import jax, jax.numpy as jnp
from jax import lax
import numpy as np

D_MODEL = 1024
BATCH = 1
SEQ = 512
DEPTH = 2

GRID_W = 64
CTX_LEN = 256
EPS = 1e-6
LN_EPS = 64e-5
MIX_W = D_MODEL
CHUNK = 128
A_GROUPS = 4
A_WIDTH = MIX_W // 2
A_GDIM = A_WIDTH // A_GROUPS
B_HEAD = 64
B_WIDTH = MIX_W // 2
B_HEADS = B_WIDTH // B_HEAD
DECAY_LORA = 64
AAA_LORA = 64
GATE_LORA = 128
C_WIDTH = MIX_W
C_HEADS = 4
C_HEAD = C_WIDTH // C_HEADS
QKV_BLOCK = 4
C_CHUNK = 128
D_FF = 2816
N_EVEN = (DEPTH + 1) // 2
N_ODD = DEPTH // 2
AB_IN = 2 * A_WIDTH + 3 * B_WIDTH + 2 * DECAY_LORA + 2 * AAA_LORA + GATE_LORA
C_IN = 2 * C_WIDTH + 4 * C_HEADS


def rmsnorm(x, g):
    xf = x.astype(jnp.float32)
    y = xf * lax.rsqrt(jnp.mean(xf * xf, axis=-1, keepdims=True) + EPS)
    return (y * g).astype(x.dtype)

def modulate(h, shift, scale):
    return h * (1 + scale) + shift

def ada_mod(cvec, w, b):
    m = jax.nn.silu(cvec) @ w + b
    m = m.reshape(cvec.shape[:-1] + (6, D_MODEL))
    if cvec.ndim == 2:
        return [m[:, i, None, :] for i in range(6)]
    return [m[i] for i in range(6)]

def dwconv1d(x, w):
    xp = jnp.pad(x, ((0, 0), (1, 1), (0, 0)))
    return xp[:, :-2] * w[0] + xp[:, 1:-1] * w[1] + xp[:, 2:] * w[2]

def dwconv_grid(x, w, rows):
    bn, t, ch = x.shape
    y = lax.conv_general_dilated(x.reshape(bn, rows, GRID_W, ch), w[:, :, None, :],
                                 window_strides=(1, 1), padding='SAME',
                                 dimension_numbers=('NHWC', 'HWIO', 'NHWC'),
                                 feature_group_count=ch)
    return y.reshape(bn, t, ch)

def conv_ffn(h, w_up, conv_w, conv_b, w_down, rows):
    a, b = jnp.split(h @ w_up, 2, axis=-1)
    a = dwconv1d(a, conv_w[1]) if rows is None else dwconv_grid(a, conv_w, rows)
    return (jax.nn.gelu(a + conv_b) * b) @ w_down

def spatial_gate(p, w_s, b_s, g_v):
    bn, t, _ = p.shape
    u, v = jnp.split(jax.nn.gelu(p[..., :2 * A_WIDTH]), 2, axis=-1)
    v = rmsnorm(v.reshape(bn, t // CHUNK, CHUNK, A_GROUPS, A_GDIM), g_v)
    z = jnp.einsum('gpq,bnqgc->bnpgc', w_s, v) + b_s.T[None, None, :, :, None]
    return u * z.reshape(bn, t, A_WIDTH)

def rwkv_prep(p, b_shift, b_w0, b_w_up, b_a0, b_a_up, b_g_up, b_kk, b_ka):
    bn, t, _ = p.shape
    o = 2 * A_WIDTH
    r, k, v = jnp.split(dwconv1d(p[..., o:o + 3 * B_WIDTH], b_shift), 3, axis=-1)
    o += 3 * B_WIDTH
    wd = p[..., o:o + 2 * DECAY_LORA].reshape(bn, t, 2, DECAY_LORA)
    o += 2 * DECAY_LORA
    ad = p[..., o:o + 2 * AAA_LORA].reshape(bn, t, 2, AAA_LORA)
    o += 2 * AAA_LORA
    gd = p[..., o:o + GATE_LORA]
    logw = -jax.nn.softplus(-(b_w0 + jnp.einsum('btdr,drc->btdc', jnp.tanh(wd), b_w_up))) - 0.5
    decay = jnp.exp(-jnp.exp(logw.astype(jnp.float32)))
    a = jax.nn.sigmoid(b_a0 + jnp.einsum('btdr,drc->btdc', ad, b_a_up))
    g = jax.nn.sigmoid(gd) @ b_g_up
    hs = lambda u: u.reshape(u.shape[:-1] + (B_HEADS, B_HEAD))
    kk = hs(k * b_kk).astype(jnp.float32)
    kk = (kk * lax.rsqrt(jnp.maximum(jnp.sum(kk * kk, axis=-1, keepdims=True), 1e-12))).astype(k.dtype)
    k_dir = k[:, :, None, :] * (1 + (a - 1) * b_ka)
    return hs(r), hs(decay), hs(k_dir), hs(v), kk, hs(a), g

def rwkv_dir_inputs(prep, d):
    r, w, kd, v, kk, a, _ = prep
    seq = (r, w[:, :, d], kd[:, :, d], v, kk, kk * a[:, :, d])
    return tuple(u[:, ::-1] for u in seq) if d == 1 else seq

def rwkv7_scan(r, w, k, v, kk, b, s0):
    dt = r.dtype
    def step(s, inp):
        r_t, w_t, k_t, v_t, kk_t, b_t = inp
        sa = jnp.einsum('bhvk,bhk->bhv', s, kk_t)
        s = s * w_t[:, :, None, :] - sa[..., None] * b_t[:, :, None, :] + v_t[..., None] * k_t[:, :, None, :]
        return s, jnp.einsum('bhvk,bhk->bhv', s, r_t)
    xs = tuple(jnp.moveaxis(u.astype(jnp.float32), 1, 0) for u in (r, w, k, v, kk, b))
    s, ys = lax.scan(step, s0, xs)
    return jnp.moveaxis(ys, 0, 1).astype(dt), s

def rwkv_out(y, prep, b_rk, ln_g, ln_b):
    r, _, kd, v, _, _, g = prep
    yf = y.astype(jnp.float32)
    mu = jnp.mean(yf, axis=-1, keepdims=True)
    var = jnp.mean(jnp.square(yf - mu), axis=-1, keepdims=True)
    yn = ((yf - mu) * lax.rsqrt(var + LN_EPS)).astype(r.dtype) * ln_g + ln_b
    bonus = jnp.sum(jnp.sum(r[:, :, None] * kd * b_rk, axis=-1, keepdims=True), axis=2) * v
    out = (yn + bonus) * g.reshape(v.shape)
    return out.reshape(v.shape[0], v.shape[1], B_WIDTH)

def rwkv_bidir(pc, pl, need_ctx, b_shift, b_w0, b_w_up, b_a0, b_a_up, b_g_up, b_kk, b_ka, b_rk, b_ln_g, b_ln_b):
    prep_c = rwkv_prep(pc, b_shift, b_w0, b_w_up, b_a0, b_a_up, b_g_up, b_kk, b_ka)
    prep_l = rwkv_prep(pl, b_shift, b_w0, b_w_up, b_a0, b_a_up, b_g_up, b_kk, b_ka)
    bn = pl.shape[0]
    ys_c, ys_l = [], []
    for d in range(2):
        s0 = jnp.zeros((bn, B_HEADS, B_HEAD, B_HEAD), jnp.float32)
        y_c, s_c = rwkv7_scan(*rwkv_dir_inputs(prep_c, d), s0)
        y_l, _ = rwkv7_scan(*rwkv_dir_inputs(prep_l, d), s_c)
        if d == 1:
            y_c, y_l = y_c[:, ::-1], y_l[:, ::-1]
        ys_c.append(y_c)
        ys_l.append(y_l)
    out_l = rwkv_out(ys_l[0] + ys_l[1], prep_l, b_rk, b_ln_g, b_ln_b)
    out_c = rwkv_out(ys_c[0] + ys_c[1], prep_c, b_rk, b_ln_g, b_ln_b) if need_ctx else None
    return out_c, out_l

def mixer_ab(hc, hl, need_ctx, w_in, w_out, a_ws, a_bs, a_gv, b_shift, b_w0, b_w_up, b_a0, b_a_up,
             b_g_up, b_kk, b_ka, b_rk, b_ln_g, b_ln_b):
    pc, pl = hc @ w_in, hl @ w_in
    bc, bl = rwkv_bidir(pc, pl, need_ctx, b_shift, b_w0, b_w_up, b_a0, b_a_up, b_g_up, b_kk, b_ka,
                        b_rk, b_ln_g, b_ln_b)
    yl = jnp.concatenate([spatial_gate(pl, a_ws, a_bs, a_gv), bl], axis=-1) @ w_out
    yc = jnp.concatenate([spatial_gate(pc, a_ws, a_bs, a_gv), bc], axis=-1) @ w_out if need_ctx else None
    return yc, yl

def mlstm_prep(p, conv, conv_b, wq, wk, wv, bi, bf):
    bn, t, _ = p.shape
    xm, z = p[..., :C_WIDTH], p[..., C_WIDTH:2 * C_WIDTH]
    gates = p[..., 2 * C_WIDTH:].reshape(bn, t, 2, 2, C_HEADS)
    xcv = jax.nn.silu(dwconv1d(xm, conv) + conv_b)
    def blockdiag(u, w):
        return jnp.einsum('btgi,gio->btgo', u.reshape(bn, t, C_WIDTH // QKV_BLOCK, QKV_BLOCK), w).reshape(bn, t, C_WIDTH)
    def heads(u):
        return u.reshape(bn, t, C_HEADS, C_HEAD).transpose(0, 2, 1, 3)
    q = heads(blockdiag(xcv, wq))
    k = heads(blockdiag(xcv, wk)) * (C_HEAD ** -0.5)
    v = heads(blockdiag(xm, wv))
    logi = jnp.transpose(gates[:, :, 0] + bi, (2, 0, 3, 1))
    logf = jax.nn.log_sigmoid(jnp.transpose(gates[:, :, 1] + bf, (2, 0, 3, 1)))
    return q, k, v, logi, logf, xcv, z

def mlstm_dir_inputs(prep, d):
    q, k, v, logi, logf = prep[:5]
    seq = (q, k, v, logi[d], logf[d])
    return tuple(u[:, :, ::-1] for u in seq) if d == 1 else seq

def mlstm_chunk_scan(q, k, v, logi, logf, state):
    bn, nh, t, dh = q.shape
    nc = t // C_CHUNK
    dt = q.dtype
    tril = jnp.tril(jnp.ones((C_CHUNK, C_CHUNK), dtype=bool))
    def chunks(u):
        u = u.astype(jnp.float32)
        return jnp.moveaxis(u.reshape((bn, nh, nc, C_CHUNK) + u.shape[3:]), 2, 0)
    def step(carry, inp):
        cmat, nvec, m = carry
        qc, kc, vc, li, lf = inp
        b = jnp.cumsum(lf, axis=-1)
        logd = jnp.where(tril, b[..., :, None] - b[..., None, :] + li[..., None, :], -jnp.inf)
        inter = b + m[..., None]
        m_row = jnp.maximum(inter, jnp.max(logd, axis=-1))
        s = jnp.einsum('bhjd,bhsd->bhjs', qc, kc) * jnp.exp(logd - m_row[..., None])
        w_inter = jnp.exp(inter - m_row)
        num = jnp.einsum('bhjs,bhsv->bhjv', s, vc) + w_inter[..., None] * jnp.einsum('bhvd,bhjd->bhjv', cmat, qc)
        den = jnp.sum(s, axis=-1) + w_inter * jnp.einsum('bhd,bhjd->bhj', nvec, qc)
        h = num / jnp.maximum(jnp.abs(den), jnp.exp(-m_row))[..., None]
        b_last = b[..., -1]
        log_in = b_last[..., None] - b + li
        m_new = jnp.maximum(b_last + m, jnp.max(log_in, axis=-1))
        carry_scale = jnp.exp(b_last + m - m_new)
        kw = kc * jnp.exp(log_in - m_new[..., None])[..., None]
        cmat = carry_scale[..., None, None] * cmat + jnp.einsum('bhsv,bhsd->bhvd', vc, kw)
        nvec = carry_scale[..., None] * nvec + jnp.sum(kw, axis=-2)
        return (cmat, nvec, m_new), h
    state, hs = lax.scan(step, state, tuple(chunks(u) for u in (q, k, v, logi, logf)))
    h = jnp.moveaxis(hs, 0, 2).reshape(bn, nh, t, v.shape[-1])
    return h.astype(dt), state

def mlstm_out(h, xcv, z, c_norm, c_skip, w_out):
    bn, nh, t, dh = h.shape
    hn = rmsnorm(h.transpose(0, 2, 1, 3), c_norm).reshape(bn, t, C_WIDTH)
    return ((hn + c_skip * xcv) * jax.nn.sigmoid(z)) @ w_out

def mixer_mlstm(hc, hl, need_ctx, w_in, w_out, conv, conv_b, wq, wk, wv, bi, bf, c_norm, c_skip):
    prep_c = mlstm_prep(hc @ w_in, conv, conv_b, wq, wk, wv, bi, bf)
    prep_l = mlstm_prep(hl @ w_in, conv, conv_b, wq, wk, wv, bi, bf)
    bn = hl.shape[0]
    hs_c, hs_l = [], []
    for d in range(2):
        init = (jnp.zeros((bn, C_HEADS, C_HEAD, C_HEAD), jnp.float32),
                jnp.zeros((bn, C_HEADS, C_HEAD), jnp.float32),
                jnp.zeros((bn, C_HEADS), jnp.float32))
        h_c, st = mlstm_chunk_scan(*mlstm_dir_inputs(prep_c, d), init)
        h_l, _ = mlstm_chunk_scan(*mlstm_dir_inputs(prep_l, d), st)
        if d == 1:
            h_c, h_l = h_c[:, :, ::-1], h_l[:, :, ::-1]
        hs_c.append(h_c)
        hs_l.append(h_l)
    yl = mlstm_out(hs_l[0] + hs_l[1], prep_l[5], prep_l[6], c_norm, c_skip, w_out)
    yc = mlstm_out(hs_c[0] + hs_c[1], prep_c[5], prep_c[6], c_norm, c_skip, w_out) if need_ctx else None
    return yc, yl

def first_inputs(seed: int = 0) -> dict:
    key = jax.random.key(seed)
    ks = iter(jax.random.split(key, 64))
    def nrm(shape, s):
        return jax.random.normal(next(ks), shape, jnp.float32) * s
    D = D_MODEL
    return {
        'x': nrm((BATCH, SEQ, D), 1.0),
        'c': nrm((BATCH, D), 1.0),
        'ctx': nrm((BATCH, CTX_LEN, D), 1.0),
        'c_ctx': nrm((D,), 1.0),
        'ada_w': nrm((DEPTH, D, 6 * D), D ** -0.5),
        'ada_b': nrm((DEPTH, 6 * D), 0.02),
        'norm_mix_pre': 1.0 + nrm((DEPTH, D), 0.05),
        'norm_mix_post': 1.0 + nrm((DEPTH, D), 0.05),
        'norm_ffn_pre': 1.0 + nrm((DEPTH, D), 0.05),
        'norm_ffn_post': 1.0 + nrm((DEPTH, D), 0.05),
        'ffn_up': nrm((DEPTH, D, 2 * D_FF), D ** -0.5),
        'ffn_conv': nrm((DEPTH, 3, 3, D_FF), 1.0 / 3.0),
        'ffn_conv_b': nrm((DEPTH, D_FF), 0.02),
        'ffn_down': nrm((DEPTH, D_FF, D), D_FF ** -0.5),
        'ab_w_in': nrm((N_EVEN, D, AB_IN), D ** -0.5),
        'ab_w_out': nrm((N_EVEN, MIX_W, D), MIX_W ** -0.5),
        'a_ws': nrm((N_EVEN, A_GROUPS, CHUNK, CHUNK), CHUNK ** -0.5),
        'a_bs': 1.0 + nrm((N_EVEN, A_GROUPS, CHUNK), 0.1),
        'a_gv': 1.0 + nrm((N_EVEN, A_GROUPS, A_GDIM), 0.05),
        'b_shift': nrm((N_EVEN, 3, 3 * B_WIDTH), 0.5),
        'b_w0': jnp.linspace(-6.0, -1.0, B_WIDTH, dtype=jnp.float32) + nrm((N_EVEN, 2, B_WIDTH), 0.1),
        'b_w_up': nrm((N_EVEN, 2, DECAY_LORA, B_WIDTH), 0.5 * DECAY_LORA ** -0.5),
        'b_a0': nrm((N_EVEN, 2, B_WIDTH), 0.1),
        'b_a_up': nrm((N_EVEN, 2, AAA_LORA, B_WIDTH), AAA_LORA ** -0.5),
        'b_g_up': nrm((N_EVEN, GATE_LORA, B_WIDTH), GATE_LORA ** -0.5),
        'b_kk': 0.85 + nrm((N_EVEN, B_WIDTH), 0.05),
        'b_ka': 1.0 + nrm((N_EVEN, B_WIDTH), 0.05),
        'b_rk': nrm((N_EVEN, B_HEADS, B_HEAD), 0.1),
        'b_ln_g': 1.0 + nrm((N_EVEN, B_HEADS, B_HEAD), 0.05),
        'b_ln_b': nrm((N_EVEN, B_HEADS, B_HEAD), 0.02),
        'c_w_in': nrm((N_ODD, D, C_IN), D ** -0.5),
        'c_w_out': nrm((N_ODD, C_WIDTH, D), C_WIDTH ** -0.5),
        'c_conv': nrm((N_ODD, 3, C_WIDTH), 0.5),
        'c_conv_b': nrm((N_ODD, C_WIDTH), 0.02),
        'c_wq': nrm((N_ODD, C_WIDTH // QKV_BLOCK, QKV_BLOCK, QKV_BLOCK), QKV_BLOCK ** -0.5),
        'c_wk': nrm((N_ODD, C_WIDTH // QKV_BLOCK, QKV_BLOCK, QKV_BLOCK), QKV_BLOCK ** -0.5),
        'c_wv': nrm((N_ODD, C_WIDTH // QKV_BLOCK, QKV_BLOCK, QKV_BLOCK), QKV_BLOCK ** -0.5),
        'c_bi': nrm((N_ODD, 2, C_HEADS), 0.1),
        'c_bf': jnp.linspace(3.0, 6.0, C_HEADS, dtype=jnp.float32) + nrm((N_ODD, 2, C_HEADS), 0.1),
        'c_norm': 1.0 + nrm((N_ODD, C_HEADS, C_HEAD), 0.05),
        'c_skip': 1.0 + nrm((N_ODD, C_WIDTH), 0.05),
    }

def first_block(x, c, ctx, c_ctx, ada_w, ada_b, norm_mix_pre, norm_mix_post, norm_ffn_pre, norm_ffn_post,
              ffn_up, ffn_conv, ffn_conv_b, ffn_down, ab_w_in, ab_w_out, a_ws, a_bs, a_gv, b_shift, b_w0,
              b_w_up, b_a0, b_a_up, b_g_up, b_kk, b_ka, b_rk, b_ln_g, b_ln_b, c_w_in, c_w_out, c_conv,
              c_conv_b, c_wq, c_wk, c_wv, c_bi, c_bf, c_norm, c_skip):
    rows = x.shape[1] // GRID_W
    xl, xc = x, ctx
    for layer in range(DEPTH):
        need_ctx = layer < DEPTH - 1
        i = layer // 2
        ml = ada_mod(c, ada_w[layer], ada_b[layer])
        mc = ada_mod(c_ctx, ada_w[layer], ada_b[layer])
        hl = modulate(rmsnorm(xl, norm_mix_pre[layer]), ml[0], ml[1])
        hc = modulate(rmsnorm(xc, norm_mix_pre[layer]), mc[0], mc[1])
        if layer % 2 == 0:
            yc, yl = mixer_ab(hc, hl, need_ctx, ab_w_in[i], ab_w_out[i], a_ws[i], a_bs[i], a_gv[i],
                              b_shift[i], b_w0[i], b_w_up[i], b_a0[i], b_a_up[i], b_g_up[i], b_kk[i],
                              b_ka[i], b_rk[i], b_ln_g[i], b_ln_b[i])
        else:
            yc, yl = mixer_mlstm(hc, hl, need_ctx, c_w_in[i], c_w_out[i], c_conv[i], c_conv_b[i],
                                 c_wq[i], c_wk[i], c_wv[i], c_bi[i], c_bf[i], c_norm[i], c_skip[i])
        xl = xl + ml[2] * rmsnorm(yl, norm_mix_post[layer])
        hl = modulate(rmsnorm(xl, norm_ffn_pre[layer]), ml[3], ml[4])
        xl = xl + ml[5] * rmsnorm(conv_ffn(hl, ffn_up[layer], ffn_conv[layer], ffn_conv_b[layer],
                                           ffn_down[layer], rows), norm_ffn_post[layer])
        if need_ctx:
            xc = xc + mc[2] * rmsnorm(yc, norm_mix_post[layer])
            hc = modulate(rmsnorm(xc, norm_ffn_pre[layer]), mc[3], mc[4])
            xc = xc + mc[5] * rmsnorm(conv_ffn(hc, ffn_up[layer], ffn_conv[layer], ffn_conv_b[layer],
                                               ffn_down[layer], None), norm_ffn_post[layer])
    return xl


_first_inputs = first_inputs


def first_inputs(seed=0):
    import zlib

    import numpy as np

    out = dict(_first_inputs(seed))
    spreads = {}
    factors = {'ffn_conv_b': 4.47,
     'a_gv': 2.835,
     'b_w_up': 2.8,
     'b_a0': 5.301,
     'b_ln_g': 3.787,
     'b_ln_b': 24.932,
     'c_conv_b': 3.583,
     'c_bi': 64.0,
     'c_norm': 10.528,
     'c_skip': 15.883,
     'a_bs': 3.361}
    for name, (base, spread) in spreads.items():
        noise = np.random.default_rng([zlib.crc32(name.encode()), seed]).standard_normal(out[name].shape)
        drawn = base * np.exp(spread * noise) if base else spread * noise
        out[name] = __import__('jax').numpy.asarray(drawn.astype(out[name].dtype))
    for name, factor in factors.items():
        out[name] = (out[name] * factor).astype(out[name].dtype)
    return out


_narrow_inputs = first_inputs


def first_inputs(seed=0):
    out = dict(_narrow_inputs(seed))
    wider = {'a_gv': 3.5, 'b_ln_g': 3.59, 'c_norm': 3.95, 'c_skip': 4.02}
    for name, times in wider.items():
        mean = out[name].mean()
        out[name] = (mean + times * (out[name] - mean)).astype(out[name].dtype)
    return out


DN_HEADS = 4
DN_DK = 128
DN_DV = 128
DN_QK = DN_HEADS * DN_DK
DN_V = DN_HEADS * DN_DV
DN_CONV = 5
CHUNK_2 = 64
N_DIR = 2
CF_WIDTH = 512
CF_CONV = 31
N_BRANCH = 2

SIZES = (2 * DN_QK + DN_V,
         DN_V,
         N_DIR * DN_HEADS,
         N_DIR * DN_HEADS,
         CF_WIDTH,
         CF_WIDTH,
         CF_WIDTH,
         N_BRANCH * D_MODEL)
D_IN = sum(SIZES)


def rms_norm(x, w):
    xf = x.astype(jnp.float32)
    y = xf * lax.rsqrt(jnp.mean(xf * xf, axis=-1, keepdims=True) + EPS)
    return (y * w.astype(jnp.float32)).astype(x.dtype)

def layer_norm(x, w, b):
    xf = x.astype(jnp.float32)
    mu = jnp.mean(xf, axis=-1, keepdims=True)
    xc = xf - mu
    y = xc * lax.rsqrt(jnp.mean(xc * xc, axis=-1, keepdims=True) + EPS)
    return (y * w.astype(jnp.float32) + b.astype(jnp.float32)).astype(x.dtype)

def l2_normalize(t):
    return t * lax.rsqrt(jnp.sum(t * t, axis=-1, keepdims=True) + EPS)

def depthwise_conv_centred(u, w):
    k = w.shape[0]
    return lax.conv_general_dilated(
        u, w[:, None, :].astype(u.dtype), window_strides=(1,),
        padding=[(k // 2, k // 2)], dimension_numbers=('NWC', 'WIO', 'NWC'),
        feature_group_count=u.shape[-1])

def gated_delta_chunked(q, k, v, g, beta):
    bsz, seq, nh, dk = q.shape
    dv = v.shape[-1]
    n = seq // CHUNK_2
    q = q.reshape(bsz, n, CHUNK_2, nh, dk).transpose(0, 3, 1, 2, 4) * (dk ** -0.5)
    k = k.reshape(bsz, n, CHUNK_2, nh, dk).transpose(0, 3, 1, 2, 4)
    v = v.reshape(bsz, n, CHUNK_2, nh, dv).transpose(0, 3, 1, 2, 4)
    g = jnp.cumsum(g.reshape(bsz, n, CHUNK_2, nh).transpose(0, 3, 1, 2), axis=-1)
    beta = beta.reshape(bsz, n, CHUNK_2, nh).transpose(0, 3, 1, 2)

    incl = jnp.tril(jnp.ones((CHUNK_2, CHUNK_2), dtype=bool))
    strict = jnp.tril(jnp.ones((CHUNK_2, CHUNK_2), dtype=bool), k=-1)
    diff = g[..., :, None] - g[..., None, :]
    decay = jnp.where(incl, jnp.exp(jnp.where(incl, diff, 0.0)), 0.0)

    k_beta = k * beta[..., None]
    lmat = jnp.where(strict, jnp.einsum('bhncd,bhnsd->bhncs', k_beta, k) * decay, 0.0)
    eye = jnp.eye(CHUNK_2, dtype=jnp.float32)
    rhs = jnp.concatenate([v * beta[..., None], k_beta * jnp.exp(g)[..., None]], axis=-1)
    sol = lax.linalg.triangular_solve(eye + lmat, rhs, left_side=True, lower=True,
                                      unit_diagonal=True)
    value, k_cum = sol[..., :dv], sol[..., dv:]

    attn = jnp.einsum('bhncd,bhnsd->bhncs', q, k) * decay
    q_dec = q * jnp.exp(g)[..., None]
    g_last = g[..., -1]
    k_dec = k * jnp.exp(g_last[..., None] - g)[..., None]

    xs = (jnp.moveaxis(value, 2, 0), jnp.moveaxis(k_cum, 2, 0), jnp.moveaxis(attn, 2, 0),
          jnp.moveaxis(q_dec, 2, 0), jnp.moveaxis(k_dec, 2, 0),
          jnp.moveaxis(jnp.exp(g_last), 2, 0))

    def step(state, inp):
        val_n, kc_n, a_n, qd_n, kd_n, dl_n = inp
        v_new = val_n - jnp.einsum('bhcd,bhde->bhce', kc_n, state)
        o_n = jnp.einsum('bhcd,bhde->bhce', qd_n, state) + jnp.einsum('bhcs,bhse->bhce', a_n, v_new)
        state = state * dl_n[..., None, None] + jnp.einsum('bhcd,bhce->bhde', kd_n, v_new)
        return state, o_n

    s0 = jnp.zeros((bsz, nh, dk, dv), dtype=jnp.float32)
    _, o = lax.scan(step, s0, xs)
    return o.transpose(1, 0, 3, 2, 4).reshape(bsz, seq, nh, dv)

def hybrid_mixer(h, w_in, qkv_conv_w, a_log, dt_bias, dn_norm_w, w_dn_out,
                 cf_conv_w, cf_conv_b, cf_ln_w, cf_ln_b, w_cf_out, gate_b, w_out):
    bsz, seq, _ = h.shape
    pts = []
    acc = 0
    for s in SIZES[:-1]:
        acc += s
        pts.append(acc)
    proj = h @ w_in
    qkv, z_a, a_lg, b_lg, cf_val, cf_glu, z_b, gate_lg = jnp.split(proj, pts, axis=-1)

    qkv = jax.nn.silu(depthwise_conv_centred(qkv, qkv_conv_w))
    q = qkv[..., :DN_QK].astype(jnp.float32).reshape(bsz, seq, DN_HEADS, DN_DK)
    k = qkv[..., DN_QK:2 * DN_QK].astype(jnp.float32).reshape(bsz, seq, DN_HEADS, DN_DK)
    v = qkv[..., 2 * DN_QK:].astype(jnp.float32).reshape(bsz, seq, DN_HEADS, DN_DV)
    q = l2_normalize(q)
    k = l2_normalize(k)
    a_lg = a_lg.astype(jnp.float32).reshape(bsz, seq, N_DIR, DN_HEADS)
    g = -jnp.exp(a_log.astype(jnp.float32)) * jax.nn.softplus(a_lg + dt_bias.astype(jnp.float32))
    beta = jax.nn.sigmoid(b_lg.astype(jnp.float32).reshape(bsz, seq, N_DIR, DN_HEADS))
    o_fwd = gated_delta_chunked(q, k, v, g[:, :, 0], beta[:, :, 0])
    flip = lambda t: jnp.flip(t, axis=1)
    o_bwd = flip(gated_delta_chunked(flip(q), flip(k), flip(v), flip(g[:, :, 1]), flip(beta[:, :, 1])))
    o = o_fwd + o_bwd
    o = o * lax.rsqrt(jnp.mean(o * o, axis=-1, keepdims=True) + EPS) * dn_norm_w.astype(jnp.float32)
    o = o * jax.nn.silu(z_a.astype(jnp.float32).reshape(bsz, seq, DN_HEADS, DN_DV))
    y_a = o.reshape(bsz, seq, DN_V).astype(h.dtype) @ w_dn_out

    u = cf_val * jax.nn.sigmoid(cf_glu)
    u = depthwise_conv_centred(u, cf_conv_w) + cf_conv_b
    u = jax.nn.silu(layer_norm(u, cf_ln_w, cf_ln_b))
    y_b = (u * jax.nn.silu(z_b)) @ w_cf_out

    gate = jax.nn.sigmoid(gate_lg + gate_b).reshape(bsz, seq, N_BRANCH, D_MODEL)
    y = gate[:, :, 0] * y_a + gate[:, :, 1] * y_b
    return y @ w_out

def second_inputs(seed: int = 0) -> dict:
    key = jax.random.key(seed)
    ks = jax.random.split(key, 17)
    nrm = jax.random.normal
    x = nrm(ks[0], (BATCH, SEQ, D_MODEL), jnp.float32)
    norm_w = 1.0 + 0.05 * nrm(ks[1], (DEPTH, D_MODEL), jnp.float32)
    w_in = nrm(ks[2], (DEPTH, D_MODEL, D_IN), jnp.float32) * D_MODEL ** -0.5
    qkv_conv_w = nrm(ks[3], (DEPTH, DN_CONV, 2 * DN_QK + DN_V), jnp.float32) * DN_CONV ** -0.5
    a_log = jnp.log(jax.random.uniform(ks[4], (DEPTH, N_DIR, DN_HEADS), jnp.float32, 1.0, 16.0))
    dt = jnp.exp(jax.random.uniform(ks[5], (DEPTH, N_DIR, DN_HEADS), jnp.float32,
                                    float(np.log(1e-3)), float(np.log(1e-1))))
    dt_bias = dt + jnp.log(-jnp.expm1(-dt))
    dn_norm_w = 1.0 + 0.05 * nrm(ks[6], (DEPTH, DN_DV), jnp.float32)
    w_dn_out = nrm(ks[7], (DEPTH, DN_V, D_MODEL), jnp.float32) * DN_V ** -0.5
    cf_conv_w = nrm(ks[8], (DEPTH, CF_CONV, CF_WIDTH), jnp.float32) * CF_CONV ** -0.5
    cf_conv_b = 0.02 * nrm(ks[9], (DEPTH, CF_WIDTH), jnp.float32)
    cf_ln_w = 1.0 + 0.05 * nrm(ks[10], (DEPTH, CF_WIDTH), jnp.float32)
    cf_ln_b = 0.02 * nrm(ks[11], (DEPTH, CF_WIDTH), jnp.float32)
    w_cf_out = nrm(ks[12], (DEPTH, CF_WIDTH, D_MODEL), jnp.float32) * CF_WIDTH ** -0.5
    gate_b = 0.02 * nrm(ks[13], (DEPTH, N_BRANCH * D_MODEL), jnp.float32)
    w_out = nrm(ks[14], (DEPTH, D_MODEL, D_MODEL), jnp.float32) * D_MODEL ** -0.5
    final_norm_w = 1.0 + 0.05 * nrm(ks[15], (D_MODEL,), jnp.float32)
    return {'x': x, 'norm_w': norm_w, 'w_in': w_in, 'qkv_conv_w': qkv_conv_w,
            'a_log': a_log, 'dt_bias': dt_bias, 'dn_norm_w': dn_norm_w, 'w_dn_out': w_dn_out,
            'cf_conv_w': cf_conv_w, 'cf_conv_b': cf_conv_b, 'cf_ln_w': cf_ln_w, 'cf_ln_b': cf_ln_b,
            'w_cf_out': w_cf_out, 'gate_b': gate_b, 'w_out': w_out, 'final_norm_w': final_norm_w}

def second_block(x, norm_w, w_in, qkv_conv_w, a_log, dt_bias, dn_norm_w, w_dn_out,
              cf_conv_w, cf_conv_b, cf_ln_w, cf_ln_b, w_cf_out, gate_b, w_out, final_norm_w):
    for l in range(DEPTH):
        h = rms_norm(x, norm_w[l])
        x = x + hybrid_mixer(h, w_in[l], qkv_conv_w[l], a_log[l], dt_bias[l], dn_norm_w[l],
                             w_dn_out[l], cf_conv_w[l], cf_conv_b[l], cf_ln_w[l], cf_ln_b[l],
                             w_cf_out[l], gate_b[l], w_out[l])
    return rms_norm(x, final_norm_w)


def setup_inputs(seed=0):
    out = dict(first_inputs(seed))
    for name, value in second_inputs(seed + 1).items():
        if name != "x":
            out[name + "_2"] = value
    return out


def reference(
    x, c, ctx, c_ctx, ada_w, ada_b, norm_mix_pre, norm_mix_post, norm_ffn_pre, norm_ffn_post,
    ffn_up, ffn_conv, ffn_conv_b, ffn_down, ab_w_in, ab_w_out, a_ws, a_bs, a_gv, b_shift, b_w0,
    b_w_up, b_a0, b_a_up, b_g_up, b_kk, b_ka, b_rk, b_ln_g, b_ln_b, c_w_in, c_w_out, c_conv,
    c_conv_b, c_wq, c_wk, c_wv, c_bi, c_bf, c_norm, c_skip, norm_w_2, w_in_2, qkv_conv_w_2,
    a_log_2, dt_bias_2, dn_norm_w_2, w_dn_out_2, cf_conv_w_2, cf_conv_b_2, cf_ln_w_2, cf_ln_b_2,
    w_cf_out_2, gate_b_2, w_out_2, final_norm_w_2,
):
    x = first_block(
        x, c, ctx, c_ctx, ada_w, ada_b, norm_mix_pre, norm_mix_post, norm_ffn_pre,
        norm_ffn_post, ffn_up, ffn_conv, ffn_conv_b, ffn_down, ab_w_in, ab_w_out, a_ws, a_bs,
        a_gv, b_shift, b_w0, b_w_up, b_a0, b_a_up, b_g_up, b_kk, b_ka, b_rk, b_ln_g, b_ln_b,
        c_w_in, c_w_out, c_conv, c_conv_b, c_wq, c_wk, c_wv, c_bi, c_bf, c_norm, c_skip,
    )
    return second_block(
        x, norm_w_2, w_in_2, qkv_conv_w_2, a_log_2, dt_bias_2, dn_norm_w_2, w_dn_out_2,
        cf_conv_w_2, cf_conv_b_2, cf_ln_w_2, cf_ln_b_2, w_cf_out_2, gate_b_2, w_out_2,
        final_norm_w_2,
    )


_drawn_inputs = setup_inputs


def setup_inputs(seed=0):
    import zlib

    import numpy as np

    out = dict(_drawn_inputs(seed))
    spreads = {}
    factors = {'dn_norm_w_2': 3.445,
     'cf_conv_b_2': 8.0,
     'cf_ln_w_2': 5.789,
     'cf_ln_b_2': 8.0,
     'gate_b_2': 8.0}
    for name, (base, spread) in spreads.items():
        noise = np.random.default_rng([zlib.crc32(name.encode()), seed]).standard_normal(out[name].shape)
        drawn = base * np.exp(spread * noise) if base else spread * noise
        out[name] = __import__('jax').numpy.asarray(drawn.astype(out[name].dtype))
    for name, factor in factors.items():
        out[name] = (out[name] * factor).astype(out[name].dtype)
    return out
```

```python
from contextlib import ExitStack, contextmanager
import math

import concourse.bass as bass
from concourse import mybir

F32 = mybir.dt.float32
ALU = mybir.AluOpType
ACT = mybir.ActivationFunctionType
AX = mybir.AxisListType.X

P = 128
D = 1024
KD = D // P
CTX, LAT = 256, 512
T = CTX + LAT
DFF = 2816
KF = DFF // P
EPS = 1e-6
LN_EPS = 64e-5
RC = 64
RDECAY = math.exp(-0.5)
MC = 128
NEG = -1e30
SLOTS = 4
ROWS, COLS = 8, 64

VECTORS = [("c", 16), ("ada_b", 96), ("mix_pre", 16), ("mix_post", 16), ("ffn_pre", 16), ("ffn_post", 16),
           ("ffn_conv", 2 * 9 * KF), ("ffn_conv_b", 2 * KF), ("a_gv", 4), ("b_shift", 36), ("b_w0", 8), ("b_a0", 8),
           ("b_kk", 4), ("b_ka", 4), ("b_rk", 4), ("b_ln_g", 4), ("b_ln_b", 4), ("c_conv", 24), ("c_conv_b", 8),
           ("c_norm", 8), ("c_skip", 8), ("norm_w", 16), ("qkv_conv", 120), ("dn_norm", 2), ("cf_conv", 248),
           ("cf_conv_b", 8), ("cf_ln_w", 8), ("cf_ln_b", 8), ("gate_b", 32), ("final_w", 8)]
COL, _n = {}, 0
for _name, _rows in VECTORS:
    COL[_name] = _n
    _n += _rows
NVEC = _n


def rwkv_constants():
    import numpy as np
    s = np.arange(P)[:, None] % RC
    t = np.arange(RC)[None, :]
    parts = []
    for d in range(2):
        strict = (s < t) if d == 0 else (s > t)
        incl = (s <= t) if d == 0 else (s >= t)
        parts += [strict, incl]
    for d in range(2):
        strict = (s < t) if d == 0 else (s > t)
        for lv in range(6):
            w = 1 << lv
            parts.append(strict & (s // (2 * w) == t // (2 * w)) & (s // w != t // w))
    pos = np.arange(T)[None, :] % RC
    parts.append(np.broadcast_to(pos != 0, (P, T)))
    return np.concatenate([np.asarray(x, np.float32) for x in parts], 1)


def delta_constants():
    import numpy as np
    s = np.arange(P)[:, None]
    t = np.arange(P)[None, :]
    parts = []
    for d in range(2):
        incl = (s <= t) if d == 0 else (s >= t)
        parts.append(incl)
    for d in range(2):
        incl = (s <= t) if d == 0 else (s >= t)
        parts.append(np.where(incl, 0.0, NEG))
    for d in range(2):
        strict = (s < t) if d == 0 else (s > t)
        for lv in range(7):
            w = 1 << lv
            parts.append(strict & (s // (2 * w) == t // (2 * w)) & (s // w != t // w))
    parts.append(s // 4 == t // 4)
    return np.concatenate([np.asarray(x, np.float32) for x in parts], 1)


def general_constants():
    import numpy as np
    i = np.arange(P)
    return np.concatenate([np.ones((P, P)), np.eye(P), (i[:, None] // 64 == i[None, :] // 64),
                           (i[:, None] % 64 == np.arange(64)[None, :])], 1).astype(np.float32)


NRC = 4 * RC + 12 * RC + 2 * T
NDC = 19 * P
NGC = 3 * P + 64


class Signal:

    def __init__(self, sem):
        self.sem = sem
        self.seen = {}

    def due(self, who, n=1):
        self.seen[who.name] = k = self.seen.get(who.name, 0) + n
        if who.turn is None or self not in who.per:
            return k
        return who.turn * who.per[self] + k

    def skip(self, who, n):
        self.seen[who.name] = self.seen.get(who.name, 0) + n


class Engine:

    def __init__(self, name, e):
        self.name, self.e, self.turn, self.per = name, e, None, {}
        self.items = 0
        self.also = {}
        self.tiles = 0

    def wait_ge(self, sig, n=1):
        self.e.wait_ge(sig.sem, sig.due(self, n))

    @contextmanager
    def repeat(self, n, per):
        if n == 1:
            yield 0
            return
        with self.e.Fori(0, n) as i:
            before = {s: s.seen.get(self.name, 0) for s in SIGNALS}
            self.turn, self.per = i, per
            yield i
            self.turn = None
        for s in SIGNALS:
            got = s.seen.get(self.name, 0) - before[s]
            assert got == per.get(s, 0), (self.name, s.label, got, per.get(s, 0))
            s.seen[self.name] = before[s] + got * n


SIGNALS = []


def program(nc, A, out):
    with ExitStack() as ctx:
        build(nc, A, out, ctx)


def build(nc, A, out, ctx):
    SIGNALS.clear()
    V, S, G, M = nc.vector, nc.scalar, nc.gpsimd, nc.tensor

    def signal(name):
        q = Signal(ctx.enter_context(nc.semaphore(name)))
        q.label = name
        SIGNALS.append(q)
        return q

    def sb(name, n):
        return ctx.enter_context(nc.sbuf_tensor(name, [P, n], F32))

    x_all = sb("x_all", KD * T)
    h_all = sb("h_all", KD * T)
    ring = [sb(f"ring{i}", 8 * P) for i in range(SLOTS)]
    vec = sb("vec", NVEC)
    gen = sb("gen", NGC)
    mods = sb("mods", 2 * 96)
    modv = sb("modv", 6 * KD * 2)
    small = sb("small", 256)
    xT = x_all[:, :].rearrange("p (k t) -> p k t", k=KD)
    hT = h_all[:, :].rearrange("p (k t) -> p k t", k=KD)
    ones, ident, halves, ident64 = gen[:, 0:P], gen[:, P:2 * P], gen[:, 2 * P:3 * P], gen[:, 3 * P:3 * P + 64]
    ARENA = (nc.sbuf_bytes_remaining - 512) // 4
    arena = sb("arena", ARENA)
    psum = [ctx.enter_context(nc.psum_tensor(f"bank{i}", [P, 512], F32)) for i in range(8)]

    class Room:

        def __init__(self, at=0, end=ARENA, where=arena):
            self.at, self.end, self.where = at, end, where

        def take(self, n):
            self.at += n
            assert self.at <= self.end, (self.at, self.end)
            return self.where[:, self.at - n:self.at]

    def cols(name, at=0, n=1):
        return vec[:, COL[name] + at:COL[name] + at + n]

    BOTH = [(0, CTX), (CTX, LAT)]
    LATENT = [(CTX, LAT)]

    def bank_of(pair, seg):
        return psum[2 * pair + (seg[0] == 0)][:, 0:seg[1]]

    landed = [signal(f"block_landed{i}") for i in range(SLOTS)]
    item_done = signal("block_used")
    tile_read = signal("tile_read")
    inputs_in = signal("inputs_in")
    extra_in = signal("extra_in")
    phase_done = signal("phase_done")
    sq_ready = signal("squares_ready")
    sum_ready = signal("sums_ready")
    ms_ready = signal("mean_squares_ready")
    root_ready = signal("roots_ready")
    scaled = signal("scaled_ready")
    moved = signal("inputs_moved")
    dve_step = signal("dve_step")
    act_step = signal("act_step")
    stored = signal("stored")
    made = signal("dve_made")
    made_act = signal("act_made")
    prod = signal("product_ready")
    prod_act = signal("product_ready_act")
    to_act = signal("dve_to_act")
    to_dve = signal("act_to_dve")
    room_dve = signal("room_from_dve")
    room_pe = signal("banks_free")

    group_read = signal("group_read")
    bonus_read = signal("bonus_read")
    step_through = signal("step_through")

    def link(e, step, ins):
        ins.then_inc(step.sem, 1)
        e.wait_ge(step)

    def loaded(e, n):
        e.e.wait_ge(extra_in.sem, 16 * n)

    def phase(e):
        if e.name != "sp":
            e.e.drain().then_inc(phase_done.sem, 1)
        e.wait_ge(phase_done, 4)

    def weights_sp(sp, w, n, width):
        def one(src, slot):
            sp.wait_ge(item_done)
            sp.e.dma_start(ring[slot][:, 0:width], src).then_inc(landed[slot].sem, 16)

        turns = n // SLOTS if n >= 2 * SLOTS else 0
        if turns:
            with sp.repeat(turns, {item_done: SLOTS}) as i:
                for j in range(SLOTS):
                    one(w[bass.ds(i * SLOTS + j, 1)].rearrange("a p n -> (a p) n"), (sp.items + j) % SLOTS)
        for j in range(turns * SLOTS, n):
            one(w[j], (sp.items + j) % SLOTS)
        sp.items += n

    def product_pe(pe, n, rhs, segs, parts=(8,), loop=True):
        def one(tile, item):
            pe.wait_ge(tile_read)
            done = 0
            for b, nk in enumerate(parts):
                slot = (item + b) % SLOTS
                pe.wait_ge(landed[slot], 16)
                for k in range(nk):
                    for seg in segs:
                        ins = M.matmul(bank_of(tile % 2, seg), ring[slot][:, k * P:(k + 1) * P], rhs(done + k, seg),
                                       start=(done + k == 0), stop=(done + k == sum(parts) - 1))
                done += nk
                ins.then_inc(item_done.sem, 1)

        per = len(parts)
        turns = n // 4 if loop and n >= 8 else 0
        if turns:
            counts = {landed[i]: 16 * per for i in range(SLOTS)}
            counts[tile_read] = 4
            with pe.repeat(turns, counts):
                for j in range(4):
                    one(pe.tiles + j, pe.items + j * per)
        for j in range(4 * turns, n):
            one(pe.tiles + j, pe.items + j * per)
        pe.items += n * per
        pe.tiles += n

    def tiles_act(act, n, evict, per=1, loop=True):
        def one(i, j):
            act.wait_ge(item_done, per)
            evict(i, (act.tiles + j) % 2).then_inc(tile_read.sem, 1)

        turns = n // 4 if loop and n >= 8 else 0
        if turns:
            with act.repeat(turns, {item_done: 4 * per, **act.also}) as t:
                for j in range(4):
                    one(t * 4 + j, j)
        for j in range(4 * turns, n):
            one(j, j)
        act.tiles += n

    rtN = arena[:, 0:T]

    def rms_act(act, src, scratch, n, segs, rt):
        lo, hi = segs[0][0], segs[-1][0] + segs[-1][1]
        for k in range(n):
            S.activation(scratch(k)[:, lo:hi], src(k)[:, lo:hi], ACT.Square).then_inc(sq_ready.sem, 1)
        act.wait_ge(ms_ready)
        S.activation(rt[:, lo:hi], rt[:, lo:hi], ACT.Sqrt).then_inc(root_ready.sem, 1)

    def rms_pe(pe, scratch, n, segs, matrix=ones):
        for k in range(n):
            pe.wait_ge(sq_ready)
            for seg in segs:
                ins = M.matmul(psum[4 + (seg[0] == 0)][:, 0:seg[1]], matrix, scratch(k)[:, seg[0]:seg[0] + seg[1]],
                               start=(k == 0), stop=(k == n - 1))
        ins.then_inc(sum_ready.sem, 1)

    def rms_dve(dve, segs, rt, scale, eps=EPS):
        dve.wait_ge(sum_ready)
        for seg in segs:
            ins = V.tensor_scalar(rt[:, seg[0]:seg[0] + seg[1]], psum[4 + (seg[0] == 0)][:, 0:seg[1]], scale, eps,
                                  ALU.mult, ALU.add)
        ins.then_inc(ms_ready.sem, 1)
        dve.wait_ge(root_ready)
        lo, hi = segs[0][0], segs[-1][0] + segs[-1][1]
        link(dve, dve_step, V.reciprocal(rt[:, lo:hi], rt[:, lo:hi]))

    def mod_col(i, k, seg):
        at = (i * KD + k) * 2 + (seg[0] == 0)
        return modv[:, at:at + 1]

    def prenorm_dve(dve, segs, rt, weight=None):
        rms_dve(dve, segs, rt, 1.0 / D)
        lo, hi = segs[0][0], segs[-1][0] + segs[-1][1]
        for k in range(KD):
            if weight is None:
                V.tensor_tensor(hT[:, k, lo:hi], xT[:, k, lo:hi], rt[:, lo:hi], ALU.mult).then_inc(scaled.sem, 1)
            else:
                V.scalar_tensor_tensor(hT[:, k, lo:hi], xT[:, k, lo:hi], weight[:, k:k + 1], rt[:, lo:hi],
                                       ALU.mult, ALU.mult)

    def prenorm_act(act, segs, which):
        for k in range(KD):
            act.wait_ge(scaled)
            for seg in segs:
                t = hT[:, k, seg[0]:seg[0] + seg[1]]
                S.activation(t, t, ACT.Identity, bias=mod_col(which + 1, k, seg), scale=mod_col(which, k, seg))

    def residual_dve(dve, segs, y, rt, which):
        rms_dve(dve, segs, rt, 1.0 / D)
        for k in range(KD):
            for seg in segs:
                a, b = seg[0], seg[0] + seg[1]
                ins = V.scalar_tensor_tensor(y(k)[:, a:b], y(k)[:, a:b], mod_col(which, k, seg), rt[:, a:b],
                                             ALU.mult, ALU.mult)
        link(dve, dve_step, ins)
        lo, hi = segs[0][0], segs[-1][0] + segs[-1][1]
        for k in range(KD):
            V.tensor_tensor(xT[:, k, lo:hi], xT[:, k, lo:hi], y(k)[:, lo:hi], ALU.add)

    def ada_pe(pe, layer):
        bank = psum[7 - layer]
        counts = {landed[i]: 16 for i in range(SLOTS)}
        cs = small[:, 0:16].rearrange("p (s k) -> p k s", s=2)
        with pe.repeat(12, counts) as i:
            for j in range(4):
                slot = (pe.items + j) % SLOTS
                pe.wait_ge(landed[slot], 16)
                for k in range(KD):
                    ins = M.matmul(bank[:, bass.ds(i * 8 + 2 * j, 2)], ring[slot][:, k * P:(k + 1) * P], cs[:, k, :],
                                   start=(k == 0), stop=(k == KD - 1))
                ins.then_inc(item_done.sem, 1)
        pe.items += 48
        M.drain().then_inc(prod.sem, 1)

    def ada_dve(dve, layer):
        dve.wait_ge(prod)
        mod = mods[:, 96 * layer:96 * layer + 96].rearrange("p (n s) -> p n s", s=2)
        V.tensor_tensor(mod, psum[7 - layer][:, 0:96].rearrange("p (n s) -> p n s", s=2),
                        cols("ada_b", 48 * layer, 48).unsqueeze(2).to_broadcast([P, 48, 2]), ALU.add)

    def modv_dve(dve, layer):
        mod = mods[:, 96 * layer:96 * layer + 96].rearrange("p (i k s) -> p i k s", i=6, s=2)
        mv = modv[:, :].rearrange("p (i k s) -> p i k s", i=6, s=2)
        for a, pre, post in ((0, "mix_pre", "mix_post"), (3, "ffn_pre", "ffn_post")):
            wpre = cols(pre, 8 * layer, 8).unsqueeze(2).to_broadcast([P, 8, 2])
            wpost = cols(post, 8 * layer, 8).unsqueeze(2).to_broadcast([P, 8, 2])
            V.scalar_tensor_tensor(mv[:, a], mod[:, a + 1], 1.0, wpre, ALU.add, ALU.mult)
            V.tensor_copy(mv[:, a + 1], mod[:, a])
            V.tensor_tensor(mv[:, a + 2], mod[:, a + 2], wpost, ALU.mult)

    room = Room()
    take4 = lambda r: r.take(4 * T).rearrange("p (j t) -> p j t", j=4)
    uT, rT, vT, kkT, kT = (take4(room) for _ in range(5))
    kd0T = take4(room)
    kdT = [kd0T, kT]
    GT = [take4(room), take4(room)]
    bT = [take4(room), take4(room)]
    rest_at = room.at
    gT = h_all[:, 0:4 * T].rearrange("p (j t) -> p j t", j=4)
    yacc = h_all[:, 4 * T:8 * T].rearrange("p (n j v) -> p n j v", n=T // RC, v=RC)

    stage = Room(0, KD * T, x_all)
    tail = Room(rest_at)
    raw = [stage.take(T + 3), stage.take(T + 3)]
    lora = stage.take(3 * T).rearrange("p (j t) -> p j t", j=3)
    rtA = stage.take(T)
    vstat = stage.take(32)
    flat = lambda t: t.rearrange("p j t -> p (j t)")
    vtok = flat(kd0T).rearrange("p (n c) -> p n c", n=6)
    vsq = flat(GT[0]).rearrange("p (n c) -> p n c", n=6)
    wsT, bs_rep = flat(bT[1])[:, 0:512], flat(bT[1])[:, 512:1024]
    rcons = tail.take(16 * RC)
    order_mask = [rcons[:, 2 * RC * d:2 * RC * d + 2 * RC].rearrange("p (a t) -> p a t", a=2) for d in range(2)]
    level_mask = [[rcons[:, RC * (4 + 6 * d + lv):RC * (5 + 6 * d + lv)] for lv in range(6)] for d in range(2)]
    resets = tail.take(T)
    loraw = tail.take(1536)

    def raw_seg(p, seg, tap):
        at = (0 if seg[0] == 0 else CTX + 1) + tap
        return raw[p][:, at:at + seg[1]]

    def mixer_ab_in_pe(pe):
        for j in range(4):
            pe.wait_ge(landed[(pe.items + j) % SLOTS], 16)
        for t in range(6):
            if t >= 2:
                pe.wait_ge(room_pe)
            for k in range(KD):
                slot = (pe.items + k // 2) % SLOTS
                ins = M.matmul(psum[4 + t % 2][:, :], hT[:, k, t * P:(t + 1) * P],
                               ring[slot][:, (k % 2) * 512:(k % 2) * 512 + 512], start=(k == 0), stop=(k == KD - 1))
                if t == 5 and k % 2:
                    ins.then_inc(item_done.sem, 1)
            if t < 5:
                ins.then_inc(prod_act.sem, 1)
        pe.items += 4
        product_pe(pe, 19, lambda k, seg: hT[:, k, seg[0]:seg[0] + seg[1]], BOTH)

    def mixer_ab_in_act(act):
        for t in range(6):
            if t < 5:
                act.wait_ge(prod_act)
            else:
                act.wait_ge(item_done, 4)
            ins = S.activation(vtok[:, t, :], psum[4 + t % 2][:, :], ACT.Gelu_apprx_tanh)
            if t < 4:
                ins.then_inc(room_pe.sem, 1)

        def plain(dst, func):
            def evict(i, p):
                for seg in BOTH:
                    ins = S.activation(dst(i)[:, seg[0]:seg[0] + seg[1]], bank_of(p, seg), func)
                return ins
            return evict

        tiles_act(act, 4, plain(lambda i: uT[:, i, :], ACT.Gelu_apprx_tanh))
        tiles_act(act, 1, plain(lambda i: lora[:, 0, :], ACT.Tanh))
        tiles_act(act, 1, plain(lambda i: lora[:, 1, :], ACT.Identity))
        tiles_act(act, 1, plain(lambda i: lora[:, 2, :], ACT.Sigmoid))
        for i in range(12):
            act.wait_ge(item_done)
            if i >= 2:
                act.wait_ge(room_dve)
            for seg in BOTH:
                ins = S.activation(raw_seg(i % 2, seg, 1), bank_of(act.tiles % 2, seg), ACT.Identity)
            ins.then_inc(tile_read.sem, 1)
            act.tiles += 1

    def mixer_ab_in_dve(dve):
        for p in range(2):
            for at in (0, CTX + 1, T + 2):
                ins = V.memset(raw[p][:, at:at + 1], 0.0)
        link(dve, dve_step, ins)
        tile_read.skip(dve, 7)
        for i in range(12):
            dve.wait_ge(tile_read)
            dst = (rT, kT, vT)[i // 4][:, i % 4, :]
            for seg in BOTH:
                ins = V.tensor_scalar(dst[:, seg[0]:seg[0] + seg[1]], raw_seg(i % 2, seg, 0), cols("b_shift", i), None,
                                ALU.mult)
            for tap in (1, 2):
                link(dve, dve_step, ins)
                for seg in BOTH:
                    y = dst[:, seg[0]:seg[0] + seg[1]]
                    ins = V.scalar_tensor_tensor(y, raw_seg(i % 2, seg, tap), cols("b_shift", 12 * tap + i), y,
                                                 ALU.mult, ALU.add)
            ins.then_inc(room_dve.sem, 1)

    def mixer_ab_load_sp(sp):
        sp.e.dma_start(rcons, A["rwkv_masks"][:, 0:16 * RC]).then_inc(extra_in.sem, 16)
        sp.e.dma_start(resets, A["rwkv_masks"][:, 16 * RC:16 * RC + T]).then_inc(extra_in.sem, 16)
        sp.e.dma_start(loraw, A["lora_w"]).then_inc(extra_in.sem, 16)
        sp.e.dma_start(wsT, A["a_wsT"]).then_inc(extra_in.sem, 16)
        sp.e.dma_start(bs_rep, A["a_bs"].partition_broadcast(P)).then_inc(extra_in.sem, 16)

    def spatial_pe(pe):
        loaded(pe, 5)
        pe.wait_ge(made)
        for g in range(4):
            if g >= 2:
                pe.wait_ge(group_read)
            for n in range(6):
                lat, ctxb = psum[2 * (g % 2)], psum[2 * (g % 2) + 1]
                dst = ctxb[:, P * n:P * n + P] if n < 2 else lat[:, P * (n - 2):P * (n - 2) + P]
                ins = M.matmul(dst, vtok[:, n, P * g:P * g + P], wsT[:, P * g:P * g + P], start=True, stop=True)
            ins.then_inc(prod.sem, 1)
        for j in range(4):
            pe.wait_ge(made)
            for seg in BOTH:
                ins = M.matmul(psum[4 + (seg[0] == 0)][:, 0:seg[1]], halves, raw[j % 2][:, seg[0]:seg[0] + seg[1]],
                               start=True, stop=True)
            ins.then_inc(sum_ready.sem, 1)

    def spatial_act(act):
        act.wait_ge(ms_ready)
        S.activation(vstat[:, 0:24], vstat[:, 0:24], ACT.Sqrt).then_inc(root_ready.sem, 1)
        for j in range(4):
            act.wait_ge(ms_ready)
            S.activation(rtA, rtA, ACT.Sqrt).then_inc(root_ready.sem, 1)

    def spatial_dve(dve):
        loaded(dve, 5)
        link(dve, dve_step, V.tensor_tensor(vsq, vtok, vtok, ALU.mult))
        groups = lambda t: t.rearrange("p n (g c) -> p (n g) c", g=4)
        link(dve, dve_step, V.tensor_reduce(vstat[:, 0:24], groups(vsq), AX, ALU.add))
        V.tensor_scalar(vstat[:, 0:24], vstat[:, 0:24], 1.0 / P, EPS, ALU.mult, ALU.add).then_inc(ms_ready.sem, 1)
        dve.wait_ge(root_ready)
        link(dve, dve_step, V.reciprocal(vstat[:, 0:24], vstat[:, 0:24]))
        V.tensor_tensor(groups(vtok), groups(vtok), vstat[:, 0:24].unsqueeze(2).to_broadcast([P, 24, P]),
                        ALU.mult).then_inc(made.sem, 1)
        for g in range(4):
            dve.wait_ge(prod)
            for seg in BOTH:
                n = seg[1] // P
                z = vsq_flat[:, seg[0]:seg[0] + seg[1]]
                ins = V.scalar_tensor_tensor(z.rearrange("p (n t) -> p n t", n=n),
                                             bank_of(g % 2, seg).rearrange("p (n t) -> p n t", n=n), cols("a_gv", g),
                                             bs_rep[:, P * g:P * g + P].unsqueeze(1).to_broadcast([P, n, P]),
                                             ALU.mult, ALU.add)
            link(dve, group_read, ins)
            link(dve, dve_step, V.tensor_tensor(uT[:, g, :], uT[:, g, :], vsq_flat[:, 0:T], ALU.mult))
        for j in range(4):
            link(dve, dve_step, V.tensor_scalar(kkT[:, j, :], kT[:, j, :], cols("b_kk", j), None, ALU.mult))
            V.tensor_tensor(raw[j % 2][:, 0:T], kkT[:, j, :], kkT[:, j, :], ALU.mult).then_inc(made.sem, 1)
            dve.wait_ge(sum_ready)
            for seg in BOTH:
                ins = V.tensor_scalar(rtA[:, seg[0]:seg[0] + seg[1]], psum[4 + (seg[0] == 0)][:, 0:seg[1]], 1e-12,
                                      None, ALU.max)
            ins.then_inc(ms_ready.sem, 1)
            dve.wait_ge(root_ready)
            link(dve, dve_step, V.reciprocal(rtA, rtA))
            link(dve, dve_step, V.tensor_tensor(kkT[:, j, :], kkT[:, j, :], rtA, ALU.mult))

    vsq_flat = flat(GT[0])

    LORA = [(0, 0, j) for j in range(4)] + [(0, 1, j) for j in range(4)] + \
           [(1, 0, j) for j in range(4)] + [(1, 1, j) for j in range(4)] + [(2, 0, j) for j in range(4)]

    def lora_pe(pe):
        for kind, d, j in LORA:
            rows = slice(64 * d, 64 * d + 64) if kind < 2 else slice(0, P)
            pe.wait_ge(tile_read)
            for seg in BOTH:
                ins = M.matmul(bank_of(pe.tiles % 2, seg), loraw[rows, 512 * kind + P * j:512 * kind + P * j + P],
                               lora[rows, kind, seg[0]:seg[0] + seg[1]], start=True, stop=True)
            ins.then_inc(prod_act.sem, 1)
            pe.tiles += 1

    def lora_act(act):
        for kind, d, j in LORA:
            act.wait_ge(prod_act)
            for seg in BOTH:
                src, a, b = bank_of(act.tiles % 2, seg), seg[0], seg[0] + seg[1]
                if kind == 2:
                    ins = S.activation(gT[:, j, a:b], src, ACT.Identity)
                elif kind == 0:
                    ins = S.activation(GT[d][:, j, a:b], src, ACT.Sigmoid, bias=cols("b_w0", 4 * d + j))
                else:
                    ins = S.activation(bT[d][:, j, a:b], src, ACT.Sigmoid, bias=cols("b_a0", 4 * d + j))
            ins.then_inc(tile_read.sem, 1)
            act.tiles += 1

    def lora_dve(dve):
        link(dve, dve_step, V.tensor_scalar(small[:, 48:52], cols("b_ka", 0, 4), -1.0, 1.0, ALU.mult, ALU.add))
        for i, (kind, d, j) in enumerate(LORA[:8]):
            dve.wait_ge(tile_read)
            s = GT[d][:, j, :]
            if d == 0:
                V.tensor_tensor_scan(s, resets, s, 0.0, ALU.mult, ALU.add)
            else:
                V.tensor_tensor_scan(s[:, ::-1], resets, s[:, ::-1], 0.0, ALU.mult, ALU.add)
        for kind, d, j in LORA[8:16]:
            dve.wait_ge(tile_read)
            a, k = bT[d][:, j, :], kT[:, j, :]
            link(dve, dve_step, V.tensor_scalar(raw[d][:, 0:T], a, cols("b_ka", j), small[:, 48 + j:49 + j],
                                                ALU.mult, ALU.add))
            V.tensor_tensor(a, a, kkT[:, j, :], ALU.mult)
            link(dve, dve_step, V.tensor_tensor(kdT[d][:, j, :], k, raw[d][:, 0:T], ALU.mult))
        tile_read.skip(dve, 4)

    NCH = T // RC
    scan_a, scan_b = Room(0, KD * T, x_all), Room(rest_at + 16 * RC)
    def scan_take(n):
        return (scan_a if scan_a.at + n <= scan_a.end else scan_b).take(n)
    q4 = lambda n: scan_take(n)
    KR = [q4(512).rearrange("p (j a t) -> p j a t", j=4, a=2) for _ in range(2)]
    SC = [[q4(512).rearrange("p (j a t) -> p j a t", j=4, a=2) for _ in range(2)] for _ in range(2)]
    XX = [q4(512).rearrange("p (a j t) -> p a j t", a=2, j=4) for _ in range(2)]
    TOK = [q4(768).rearrange("p (a j t) -> p a j t", a=3, j=4) for _ in range(2)]
    PM, RH, ST = ([q4(256).rearrange("p (j t) -> p j t", j=4) for _ in range(2)] for _ in range(3))
    NSA = RH
    LM = [[q4(256).rearrange("p (j t) -> p j t", j=4) for _ in range(2)] for _ in range(2)]
    EM = [q4(260).rearrange("p (j t) -> p j t", j=4) for _ in range(2)]
    PCOL = [q4(4) for _ in range(2)]
    HALF = (slice(0, 64), slice(64, 128))

    def chunk_of(d, i):
        return i if d == 0 else (3 - i if i < 4 else 15 - i)

    def four(bank, at=0):
        return bank[:, at:at + 256].rearrange("p (j t) -> p j t", j=4)

    def each_head(out4, lhs4, rhs4, start=True, stop=True):
        for j in range(4):
            for h in HALF:
                ins = M.matmul(out4(j)[h], lhs4(j)[h], rhs4(j)[h], start=start, stop=stop)
        return ins

    def rwkv_pe(pe):
        B = [[psum[4 * d + i] for i in range(4)] for d in range(2)]
        for i in range(NCH):
            for d in range(2):
                n = chunk_of(d, i)
                pe.wait_ge(made)
                for a, src in enumerate((lambda j: vT[:, j, n * RC:(n + 1) * RC], lambda j: XX[d][:, 1, j, :],
                                         lambda j: XX[d][:, 0, j, :])):
                    dst = four(B[d][2 + a // 2], 256 * (a % 2))
                    ins = each_head(lambda j: dst[:, j, :], src, lambda j: ident64)
                ins.then_inc(prod_act.sem, 1)
                for a in range(2):
                    dst = B[d][a][:, :].rearrange("p (j a t) -> p j a t", j=4, a=2)
                    ins = each_head(lambda j: dst[:, j], lambda j: XX[d][:, a, j, :], lambda j: KR[d][:, j])
                ins.then_inc(prod.sem, 1)
            for d in range(2):
                pe.wait_ge(made)
                pe.wait_ge(made_act)
                p = four(B[d][0])
                each_head(lambda j: p[:, j, :], lambda j: LM[d][0][:, j, :], lambda j: ident64).then_inc(prod.sem, 1)
            for lv in range(1, 6):
                for d in range(2):
                    pe.wait_ge(made)
                    p = four(B[d][0])
                    each_head(lambda j: p[:, j, :], lambda j: LM[d][lv % 2][:, j, :],
                              lambda j: XX[d][:, 0, j, :]).then_inc(prod_act.sem, 1)
                for d in range(2):
                    pe.wait_ge(made_act)
                    dx, dt = four(B[d][1]), four(B[d][1], 256)
                    if lv < 5:
                        each_head(lambda j: dx[:, j, :], lambda j: XX[d][:, 1, j, :], lambda j: PM[d][:, j, :])
                    each_head(lambda j: dt[:, j, :], lambda j: PM[d][:, j, :],
                              lambda j: XX[d][:, 1, j, :]).then_inc(prod.sem, 1)
            for d in range(2):
                p = four(B[d][2])
                for j in range(4):
                    for h in HALF:
                        M.matmul(p[h, j, :], KR[d][h, j, 0, :], ST[d][h, j, :], start=True, stop=False)
                        ins = M.matmul(p[h, j, :], SC[d][1][h, j, 0, :], TOK[d][h, 0, j, :], start=False, stop=True)
                ins.then_inc(prod_act.sem, 1)
            for d in range(2):
                pe.wait_ge(made)
                pe.wait_ge(made_act)
                p = four(B[d][2], 256)
                each_head(lambda j: p[:, j, :], lambda j: XX[d][:, 1, j, :], lambda j: RH[d][:, j, :])\
                    .then_inc(prod_act.sem, 1)
            for d in range(2):
                pe.wait_ge(made_act)
                s, y = four(B[d][3]), four(B[d][3], 256)
                for j in range(4):
                    for h in HALF:
                        M.matmul(y[h, j, :], KR[d][h, j, 1, :], ST[d][h, j, :], start=True, stop=False)
                        M.matmul(y[h, j, :], SC[d][1][h, j, 1, :], TOK[d][h, 0, j, :], start=False, stop=False)
                        M.matmul(y[h, j, :], SC[d][0][h, j, 1, :], NSA[d][h, j, :], start=False, stop=True)
                        M.matmul(s[h, j, :], TOK[d][h, 1, j, :], TOK[d][h, 0, j, :], start=True, stop=False)
                        ins = M.matmul(s[h, j, :], TOK[d][h, 2, j, :], NSA[d][h, j, :], start=False, stop=True)
                ins.then_inc(prod.sem, 1)

    def rwkv_act(act):
        B = [[psum[4 * d + i] for i in range(4)] for d in range(2)]
        for i in range(NCH):
            for d in range(2):
                n = chunk_of(d, i)
                if i:
                    act.wait_ge(step_through)
                g = GT[d][:, :, n * RC:(n + 1) * RC]
                S.activation(EM[d][:, :, 1 - d:65 - d], g, ACT.Exp, scale=-RDECAY)
                S.activation(PM[d][:, :, :], g, ACT.Exp, scale=RDECAY).then_inc(to_dve.sem, 1)
            for d in range(2):
                act.wait_ge(prod_act)
                S.activation(TOK[d][:, 0:2], B[d][2][:, :].rearrange("p (a j t) -> p a j t", a=2, j=4), ACT.Identity)
                S.activation(TOK[d][:, 2], four(B[d][3]), ACT.Identity).then_inc(made_act.sem, 1)
            for lv in range(1, 6):
                for d in range(2):
                    act.wait_ge(prod_act)
                    S.activation(PM[d][:, :, :], four(B[d][0]), ACT.Identity).then_inc(made_act.sem, 1)
            for d in range(2):
                act.wait_ge(prod_act)
                S.activation(RH[d][:, :, :], four(B[d][2]), ACT.Identity).then_inc(made_act.sem, 1)
            for d in range(2):
                act.wait_ge(prod_act)
                S.activation(NSA[d][:, :, :], four(B[d][2], 256), ACT.Identity, scale=-1.0).then_inc(made_act.sem, 1)

    def rwkv_dve(dve):
        B = [[psum[4 * d + i] for i in range(4)] for d in range(2)]
        eye = ident64.unsqueeze(1).to_broadcast([P, 4, RC])
        for d in range(2):
            V.memset(EM[d][:, :, 64 * d:64 * d + 1], 1.0)
            link(dve, dve_step, V.memset(ST[d], 0.0))
        for i in range(NCH):
            for d in range(2):
                n = chunk_of(d, i)
                at = slice(n * RC, (n + 1) * RC)
                dve.wait_ge(to_dve)
                V.tensor_tensor(KR[d][:, :, 1, :], rT[:, :, at], EM[d][:, :, 1 - d:65 - d], ALU.mult)
                V.tensor_tensor(KR[d][:, :, 0, :], kkT[:, :, at], EM[d][:, :, d:64 + d], ALU.mult)
                V.tensor_tensor(XX[d][:, 0], bT[d][:, :, at], PM[d][:, :, :], ALU.mult)
                V.tensor_copy(PCOL[d], EM[d][:, :, 64 - 64 * d])
                V.tensor_tensor(XX[d][:, 1], kdT[d][:, :, at], PM[d][:, :, :], ALU.mult).then_inc(made.sem, 1)
            for d in range(2):
                dve.wait_ge(prod)
                level = lambda lv: level_mask[d][lv].unsqueeze(1).to_broadcast([P, 4, RC])
                mask = order_mask[d].unsqueeze(1).to_broadcast([P, 4, 2, RC])
                banks = [B[d][a][:, :].rearrange("p (j a t) -> p j a t", j=4, a=2) for a in range(2)]
                link(dve, dve_step, V.tensor_tensor(SC[d][0], banks[0], mask, ALU.mult))
                link(dve, dve_step, V.tensor_tensor(LM[d][0], SC[d][0][:, :, 0, :], level(0), ALU.mult))
                V.tensor_tensor(SC[d][1], banks[1], mask, ALU.mult)
                V.scalar_tensor_tensor(XX[d][:, 1], LM[d][0], -1.0, eye, ALU.mult, ALU.add).then_inc(made.sem, 1)
            for d in range(2):
                level = lambda lv: level_mask[d][lv].unsqueeze(1).to_broadcast([P, 4, RC])
                V.tensor_tensor(LM[d][1], SC[d][0][:, :, 0, :], level(1), ALU.mult)
                dve.wait_ge(prod)
                V.scalar_tensor_tensor(XX[d][:, 0], four(B[d][0]), -1.0, eye, ALU.mult, ALU.add).then_inc(made.sem, 1)
            for lv in range(1, 6):
                for d in range(2):
                    level = lambda lv: level_mask[d][lv].unsqueeze(1).to_broadcast([P, 4, RC])
                    if lv < 5:
                        V.tensor_tensor(LM[d][(lv + 1) % 2], SC[d][0][:, :, 0, :], level(lv + 1), ALU.mult)
                    dve.wait_ge(prod)
                    p = B[d][1][:, :].rearrange("p (a j t) -> p a j t", a=2, j=4)
                    if lv < 5:
                        V.tensor_tensor(XX[d], XX[d], p, ALU.subtract).then_inc(made.sem, 1)
                    else:
                        V.tensor_tensor(XX[d][:, 1], XX[d][:, 1], p[:, 1], ALU.subtract).then_inc(made.sem, 1)
            for d in range(2):
                n = chunk_of(d, i)
                dve.wait_ge(prod)
                link(dve, dve_step, V.tensor_tensor(ST[d], ST[d], four(B[d][3]), ALU.add))
                V.tensor_tensor(ST[d], ST[d], PCOL[d].unsqueeze(2).to_broadcast([P, 4, RC]), ALU.mult)
                y = four(B[d][3], 256)
                if n not in visited:
                    visited.add(n)
                    ins = V.tensor_copy(yacc[:, n], y)
                else:
                    ins = V.tensor_tensor(yacc[:, n], yacc[:, n], y, ALU.add)
                link(dve, step_through, ins)

    visited = set()

    def rwkv_out_pe(pe):
        pe.wait_ge(made)
        for j in range(4):
            pe.wait_ge(tile_read)
            for n in range(NCH):
                bank, at = (psum[2 * (j % 2) + 1], n * RC) if n < 4 else (psum[2 * (j % 2)], (n - 4) * RC)
                for h in HALF:
                    ins = M.matmul(bank[h, at:at + RC], yacc[h, n, j, :], ident64[h], start=True, stop=True)
            ins.then_inc(prod_act.sem, 1)
            if j:
                pe.wait_ge(bonus_read)
            for seg in BOTH:
                ins = M.matmul(psum[4 + (seg[0] == 0)][:, 0:seg[1]], halves, bT[0][:, j, seg[0]:seg[0] + seg[1]],
                               start=True, stop=True)
            ins.then_inc(prod.sem, 1)
        bonus_read.skip(pe, 1)

    def rwkv_out_act(act):
        act.wait_ge(ms_ready)
        S.activation(ystat[:, 48:96], ystat[:, 48:96], ACT.Sqrt).then_inc(root_ready.sem, 1)
        for j in range(4):
            act.wait_ge(prod_act)
            for seg in BOTH:
                ins = S.activation(GT[1][:, j, seg[0]:seg[0] + seg[1]], bank_of(j % 2, seg), ACT.Identity,
                                   bias=cols("b_ln_b", j), scale=cols("b_ln_g", j))
            ins.then_inc(tile_read.sem, 1)

    def rwkv_out_dve(dve):
        y = yacc.rearrange("p n j v -> p (n j) v")
        sq = flat(GT[0]).rearrange("p (m v) -> p m v", v=RC)
        for j in range(4):
            ins = V.tensor_tensor(bT[0][:, j, :], kdT[0][:, j, :], kdT[1][:, j, :], ALU.add)
        link(dve, dve_step, ins)
        for j in range(4):
            V.scalar_tensor_tensor(bT[0][:, j, :], bT[0][:, j, :], cols("b_rk", j), rT[:, j, :], ALU.mult, ALU.mult)
        link(dve, dve_step, V.tensor_reduce(ystat[:, 0:48], y, AX, ALU.add))
        link(dve, dve_step, V.tensor_scalar(ystat[:, 0:48], ystat[:, 0:48], 1.0 / RC, None, ALU.mult))
        spread = lambda a: ystat[:, a:a + 48].unsqueeze(2).to_broadcast([P, 48, RC])
        link(dve, dve_step, V.tensor_tensor(y, y, spread(0), ALU.subtract))
        link(dve, dve_step, V.tensor_tensor(sq, y, y, ALU.mult))
        link(dve, dve_step, V.tensor_reduce(ystat[:, 48:96], sq, AX, ALU.add))
        V.tensor_scalar(ystat[:, 48:96], ystat[:, 48:96], 1.0 / RC, LN_EPS, ALU.mult, ALU.add).then_inc(ms_ready.sem, 1)
        dve.wait_ge(root_ready)
        link(dve, dve_step, V.reciprocal(ystat[:, 48:96], ystat[:, 48:96]))
        V.tensor_tensor(y, y, spread(48), ALU.mult).then_inc(made.sem, 1)
        for j in range(4):
            dve.wait_ge(prod)
            dst = bT[1][:, j, :]
            for seg in BOTH:
                a, b = seg[0], seg[0] + seg[1]
                ins = V.tensor_tensor(dst[:, a:b], psum[4 + (seg[0] == 0)][:, 0:seg[1]], vT[:, j, a:b], ALU.mult)
            link(dve, bonus_read, ins)
            dve.wait_ge(tile_read)
            link(dve, dve_step, V.tensor_tensor(dst, dst, GT[1][:, j, :], ALU.add))
            V.tensor_tensor(dst, dst, gT[:, j, :], ALU.mult)

    out_tail = Room(rest_at + 16 * RC)
    ystat = out_tail.take(96)
    rtB = out_tail.take(T)
    yT_l0 = lambda k: (rT, vT)[k // 4][:, k % 4, :]
    sq_l0 = lambda k: GT[k // 4][:, k % 4, :]
    mix_in = lambda k, seg: (uT, bT[1])[k // 4][:, k % 4, seg[0]:seg[0] + seg[1]]

    def keep(dst, segs, func=ACT.Identity):
        def evict(i, p):
            for seg in segs:
                ins = S.activation(dst(i)[:, seg[0]:seg[0] + seg[1]], bank_of(p, seg), func)
            return ins
        return evict

    froom = Room()
    hf = froom.take(KF * T).rearrange("p (k t) -> p k t", k=KF)
    grid = [froom.take((ROWS + 2) * (COLS + 2)).rearrange("p (r c) -> p r c", c=COLS + 2) for _ in range(2)]
    line = [froom.take(CTX + 2) for _ in range(2)]
    bside = [froom.take(T) for _ in range(2)]
    conv = [froom.take(T) for _ in range(2)]
    fsq = froom.take(KD * T).rearrange("p (k t) -> p k t", k=KD)
    frt = froom.take(T)
    conv_ready, gelu_ready, pair_free = signal("conv_ready"), signal("gelu_ready"), signal("pair_free")

    def ffn_pe(pe, segs):
        product_pe(pe, 2 * KF, lambda k, seg: hT[:, k, seg[0]:seg[0] + seg[1]], segs)

    def ffn_down_pe(pe, segs):
        product_pe(pe, KD, lambda k, seg: hf[:, k, seg[0]:seg[0] + seg[1]], segs, parts=(8, 8, 6))

    def grid_at(q, dy, dx):
        return grid[q][:, dy:dy + ROWS, dx:dx + COLS]

    def ffn_act(act, layer, segs):
        lo, hi = segs[0][0], segs[-1][0] + segs[-1][1]
        with act.repeat(KF // 2, {item_done: 4, conv_ready: 2, pair_free: 2}) as t:
            for q in range(2):
                act.wait_ge(item_done)
                act.wait_ge(pair_free)
                par = (act.tiles + 2 * q) % 2
                for seg in segs:
                    if seg[0]:
                        ins = S.activation(grid_at(q, 1, 1), bank_of(par, seg).rearrange("p (r c) -> p r c", c=COLS),
                                           ACT.Identity)
                    else:
                        ins = S.activation(line[q][:, 1:1 + CTX], bank_of(par, seg), ACT.Identity)
                ins.then_inc(tile_read.sem, 1)
                act.wait_ge(item_done)
                for seg in segs:
                    ins = S.activation(bside[q][:, seg[0]:seg[0] + seg[1]], bank_of(1 - par, seg), ACT.Identity)
                ins.then_inc(tile_read.sem, 1)
                act.wait_ge(conv_ready)
                S.activation(conv[q][:, lo:hi], conv[q][:, lo:hi], ACT.Gelu_apprx_tanh,
                             bias=vec[:, bass.ds(t * 2 + (COL["ffn_conv_b"] + KF * layer + q), 1)])\
                    .then_inc(gelu_ready.sem, 1)
        act.tiles += 2 * KF
        act.wait_ge(pair_free, 2)

    def ffn_dve(dve, layer, segs):
        for q in range(2):
            V.memset(grid[q], 0.0)
            link(dve, dve_step, V.memset(line[q], 0.0))
        dve.e.sem_inc(pair_free.sem, 2)
        lo, hi = segs[0][0], segs[-1][0] + segs[-1][1]
        taps = [(dy, dx) for dy in (1, 0, 2) for dx in (0, 1, 2)]
        with dve.repeat(KF // 2, {tile_read: 4, dve_step: 18, gelu_ready: 2}) as t:
            for q in range(2):
                w = lambda dy, dx: vec[:, bass.ds(t * 2 + (COL["ffn_conv"] + KF * (9 * layer + 3 * dy + dx) + q), 1)]
                dve.wait_ge(tile_read, 2)
                for n, (dy, dx) in enumerate(taps):
                    for seg in segs:
                        y = conv[q][:, seg[0]:seg[0] + seg[1]]
                        if seg[0]:
                            y, a = y.rearrange("p (r c) -> p r c", c=COLS), grid_at(q, dy, dx)
                        elif dy == 1:
                            a = line[q][:, dx:dx + CTX]
                        else:
                            continue
                        if n == 0:
                            ins = V.tensor_scalar(y, a, w(dy, dx), None, ALU.mult)
                        else:
                            ins = V.scalar_tensor_tensor(y, a, w(dy, dx), y, ALU.mult, ALU.add)
                    if n < 8:
                        link(dve, dve_step, ins)
                    else:
                        ins.then_inc(conv_ready.sem, 1)
                dve.wait_ge(gelu_ready)
                k = hf[:, bass.ds(t * 2 + q, 1), lo:hi].rearrange("p a t -> p (a t)")
                link(dve, dve_step, V.tensor_tensor(k, conv[q][:, lo:hi], bside[q][:, lo:hi], ALU.mult))
                dve.e.sem_inc(pair_free.sem, 1)

    NC6 = T // MC
    NL = LAT // MC
    mroom = Room()
    tall = lambda r, w: r.take(KD * w).rearrange("p (k t) -> p k t", k=KD)
    xmT, xcT, zT, kqT = tall(mroom, T), tall(mroom, T), tall(mroom, LAT), tall(mroom, LAT)
    vtk = mroom.take(NC6 * D).rearrange("p (c f) -> p c f", c=NC6)
    hacc = mroom.take(NL * D).rearrange("p (c f) -> p c f", c=NL)
    ktk = h_all[:, :].rearrange("p (c f) -> p c f", c=NC6)
    mmask = mroom.take(5 * P)
    incl128 = [mmask[:, 0:P], mmask[:, P:2 * P]]
    neg128 = [mmask[:, 2 * P:3 * P], mmask[:, 3 * P:4 * P]]
    diag4 = mmask[:, 4 * P:5 * P]
    gcols = mroom.take(1)
    bdw = mroom.take(96).rearrange("p (a n o) -> p a n o", a=3, n=KD)
    ctk = mroom.take(4 * 6 * 8).rearrange("p (c q d h) -> p c q d h", c=6, q=4, d=2)
    csb = mroom.take(48).rearrange("p (u c) -> p u c", c=6)
    nvec = mroom.take(16)
    mrow = mroom.take(24)
    dens = [mroom.take(4), mroom.take(4)]
    mstat = mroom.take(16)
    mrt = mroom.take(T)
    bdm = [mroom.take(3 * P) for _ in range(2)]
    rows = Room(0, NL * D, flat(hacc))
    RA, RB, RX, RW, RK = (rows.take(T) for _ in range(5))
    RM = mrt
    eb, tb, stb = ([xmT[:, i, P * j:P * j + P] for j in range(2)] for i in range(3))
    t1b = [xmT[:, 3 + j, 0:256] for j in range(2)]
    kwb = [bdm[0][:, 0:256], bdm[1][:, 0:256]]

    def state(d, h):
        return (xT if d == 0 else xcT)[:, 2 * h:2 * h + 2, 0:256]

    def mlstm_load_sp(sp):
        for dst, src in ((mmask[:, 0:4 * P], A["delta_masks"][:, 0:4 * P]), (diag4, A["delta_masks"][:, 18 * P:19 * P]),
                         (gcols, A["gate_cols"]), (bdw.rearrange("p a n o -> p (a n o)"), A["qkv_blocks"])):
            sp.e.dma_start(dst, src).then_inc(extra_in.sem, 16)

    def mlstm_in_pe(pe):
        rhs = lambda k, seg: hT[:, k, seg[0]:seg[0] + seg[1]]
        product_pe(pe, 8, rhs, BOTH)
        product_pe(pe, 8, rhs, LATENT)
        product_pe(pe, 1, rhs, BOTH)

    def mlstm_in_act(act):
        def evict(i, p):
            for seg in BOTH:
                ins = S.activation(xmT[:, i, seg[0]:seg[0] + seg[1]], bank_of(p, seg), ACT.Identity)
            return ins
        tiles_act(act, 8, evict, loop=False)
        for k in range(KD):
            act.wait_ge(to_act)
            S.activation(xcT[:, k, :], xcT[:, k, :], ACT.Silu, bias=cols("c_conv_b", k))
        tiles_act(act, 8, lambda i, p: S.activation(zT[:, i, :], bank_of(p, LATENT[0]), ACT.Sigmoid), loop=False)
        loaded(act, 9)
        def gates(i, p):
            for seg in BOTH:
                a, b = seg[0], seg[0] + seg[1]
                S.activation(RA[0:64, a:b], bank_of(p, seg)[0:64], ACT.Identity, bias=gcols[0:64, 0:1])
                ins = S.activation(RX[64:128, a:b], bank_of(p, seg)[64:128], ACT.Identity, bias=gcols[64:128, 0:1])
            return ins
        tiles_act(act, 1, gates)

    def shift3_dve(dve, src, dst, w, segs, step):
        for seg in segs:
            a, b = seg[0], seg[0] + seg[1]
            ins = V.tensor_scalar(dst[:, a:b], src[:, a:b], w(1), None, ALU.mult)
        link(dve, step, ins)
        for seg in segs:
            a, b = seg[0], seg[0] + seg[1]
            ins = V.scalar_tensor_tensor(dst[:, a + 1:b], src[:, a:b - 1], w(0), dst[:, a + 1:b], ALU.mult, ALU.add)
        link(dve, step, ins)
        for seg in segs:
            a, b = seg[0], seg[0] + seg[1]
            ins = V.scalar_tensor_tensor(dst[:, a:b - 1], src[:, a + 1:b], w(2), dst[:, a:b - 1], ALU.mult, ALU.add)
        return ins

    def mlstm_in_dve(dve):
        for k in range(KD):
            dve.wait_ge(tile_read)
            shift3_dve(dve, xmT[:, k, :], xcT[:, k, :], lambda tap: cols("c_conv", 8 * tap + k), BOTH, dve_step)\
                .then_inc(to_act.sem, 1)
        tile_read.skip(dve, 9)

    def mlstm_mid_pe(pe):
        for n in range(KD):
            pe.wait_ge(made)
            w = bdm[n % 2]
            for src, m in ((xmT, 2), (xcT, 1)):
                pe.wait_ge(tile_read)
                for c in range(NC6):
                    p = pe.tiles % 2
                    dst = psum[2 * p + 1][:, P * c:P * c + P] if c < 2 else psum[2 * p][:, P * (c - 2):P * (c - 1)]
                    ins = M.matmul(dst, src[:, n, P * c:P * c + P], w[:, P * m:P * m + P], start=True, stop=True)
                ins.then_inc(prod_act.sem, 1)
                pe.tiles += 1
            pe.wait_ge(tile_read)
            p = pe.tiles % 2
            for m in range(2):
                ins = M.matmul(psum[2 * p + m][:, :], w[:, P * m:P * m + P], xcT[:, n, CTX:T], start=True, stop=True)
            ins.then_inc(prod_act.sem, 1)
            pe.tiles += 1
        pe.wait_ge(made)
        pe.wait_ge(made_act)
        for c in range(NC6):
            for i, r in enumerate((RA, RW, RX, RK)):
                dst = psum[6][:, 32 * c + 8 * i:32 * c + 8 * i + 8].rearrange("p (d h) -> p d h", d=2)
                M.matmul(dst, r[0:64, P * c:P * c + P], ident[0:64, 0:64].rearrange("p (d r) -> p d r", d=2)[:, :, 0:4],
                         start=True, stop=True)
        for u in range(8):
            row = 32 * (u // 4) + u % 4
            ins = M.matmul(psum[7][:, 6 * u:6 * u + 6], ident[0:64, row:row + 1].to_broadcast([64, P]),
                           mrow[0:64, 12:18], start=True, stop=True)
        ins.then_inc(prod.sem, 1)

    def mlstm_mid_act(act):
        r = slice(0, 64)
        act.wait_ge(to_act)
        link(act, act_step, S.activation(RW[r, :], RX[r, :], ACT.Abs))
        S.activation(RW[r, :], RW[r, :], ACT.Exp, scale=-1.0).then_inc(to_dve.sem, 1)
        act.wait_ge(to_act)
        S.activation(RW[r, :], RW[r, :], ACT.Ln).then_inc(to_dve.sem, 1)
        for n in range(KD):
            for what, scale in (("v", 1.0), ("k", C_SCALE)):
                act.wait_ge(prod_act)
                p, dst = act.tiles % 2, vtk if what == "v" else ktk
                S.activation(dst[:, 0:2, P * n:P * n + P], psum[2 * p + 1][:, 0:256].rearrange("p (c f) -> p c f", c=2),
                             ACT.Identity, scale=scale)
                S.activation(dst[:, 2:6, P * n:P * n + P], psum[2 * p][:, :].rearrange("p (c f) -> p c f", c=4),
                             ACT.Identity, scale=scale).then_inc(tile_read.sem, 1)
                act.tiles += 1
            act.wait_ge(prod_act)
            p = act.tiles % 2
            S.activation(qstage(n), psum[2 * p][:, :], ACT.Identity)
            S.activation(kqT[:, n, :], psum[2 * p + 1][:, :], ACT.Identity, scale=C_SCALE).then_inc(tile_read.sem, 1)
            act.tiles += 1
        act.wait_ge(to_act)
        S.activation(RW[r, :], RW[r, :], ACT.Exp, scale=-1.0)
        S.activation(RX[r, :], RX[r, :], ACT.Exp, scale=-1.0)
        S.activation(mrow[r, 12:18], mrow[r, 12:18], ACT.Exp, scale=-1.0)
        S.activation(RK[r, :], RK[r, :], ACT.Exp).then_inc(made_act.sem, 1)

    C_SCALE = 1.0 / 16.0
    def qstage(n):
        return xmT[:, n, CTX:T]

    def mlstm_mid_dve(dve):
        r = slice(0, 64)
        loaded(dve, 9)
        V.tensor_copy(RX[r, :], RX[64:128, :]).then_inc(to_act.sem, 1)
        V.memset(mrow[r, 0:24], 0.0)
        V.memset(RM[r, :], 1.0)
        for h in range(4):
            V.memset(state(0, h), 0.0)
        link(dve, dve_step, V.memset(nvec, 0.0))
        def weights(n):
            for a in range(3):
                ins = V.tensor_tensor(bdm[n % 2][:, P * a:P * a + P].rearrange("p (g o) -> p g o", o=4),
                                      bdw[:, a, n, :].unsqueeze(1).to_broadcast([P, 32, 4]),
                                      diag4.rearrange("p (g o) -> p g o", o=4), ALU.mult)
            ins.then_inc(made.sem, 1)
        weights(0)
        weights(1)
        dve.wait_ge(to_dve)
        V.tensor_scalar(RW[r, :], RW[r, :], 1.0, None, ALU.add).then_inc(to_act.sem, 1)
        dve.wait_ge(to_dve)
        link(dve, dve_step, V.scalar_tensor_tensor(RB[r, :], RX[r, :], 0.0, RW[r, :], ALU.min, ALU.subtract))
        for c in range(NC6):
            for d, q in enumerate((slice(0, 32), slice(32, 64))):
                s = RB[q, P * c:P * c + P]
                o = RM[q, 0:P]
                if d:
                    s = s[:, ::-1]
                ins = V.tensor_tensor_scan(s, o, s, 0.0, ALU.mult, ALU.add)
        link(dve, dve_step, ins)
        link(dve, dve_step, V.tensor_tensor(RA[r, :], RA[r, :], RB[r, :], ALU.subtract))
        for i in range(NC6):
            for d, q in enumerate((slice(0, 32), slice(32, 64))):
                c = mchunk(d, i)
                src, dst = RA[q, P * c:P * c + P], RK[q, P * c:P * c + P]
                if d:
                    src, dst = src[:, ::-1], dst[:, ::-1]
                end = P * c + (0 if d else P - 1)
                link(dve, dve_step, V.tensor_tensor_scan(dst, RM[q, 0:P], src, mrow[q, c:c + 1], ALU.mult, ALU.max))
                link(dve, dve_step, V.tensor_copy(mrow[q, 6 + c:7 + c], RK[q, end:end + 1]))
                if i < NC6 - 1:
                    nx = mchunk(d, i + 1)
                    link(dve, dve_step, V.tensor_tensor(mrow[q, nx:nx + 1], RB[q, end:end + 1], RK[q, end:end + 1],
                                                        ALU.add))
        for n in range(2, KD):
            dve.wait_ge(tile_read, 3)
            weights(n)
        dve.wait_ge(tile_read, 6)
        for h in range(4):
            V.memset(state(1, h), 0.0)
        chunks = lambda t: t[r, :].rearrange("p (c t) -> p c t", c=NC6)
        per = lambda at: mrow[r, at:at + 6].unsqueeze(2).to_broadcast([64, NC6, P])
        link(dve, dve_step, V.tensor_tensor(chunks(RW), chunks(RK), per(0), ALU.subtract))
        link(dve, dve_step, V.tensor_tensor(RX[r, :], RB[r, :], RK[r, :], ALU.add))
        link(dve, dve_step, V.tensor_tensor(mrow[r, 12:18], mrow[r, 6:12], mrow[r, 0:6], ALU.subtract))
        link(dve, dve_step, V.tensor_copy(RM[r, :], RK[r, :]))
        V.tensor_tensor(chunks(RK), chunks(RA), per(6), ALU.subtract).then_inc(to_act.sem, 1)
        V.engine_nop().then_inc(made.sem, 1)
        dve.wait_ge(prod)
        V.tensor_copy(ctk.rearrange("p c q d h -> p (c q d h)"), psum[6][:, 0:192])
        V.tensor_copy(csb.rearrange("p u c -> p (u c)"), psum[7][:, 0:48])

    def mchunk(d, i):
        return i if d == 0 else (1 - i if i < 2 else 7 - i)

    UNITS = [(i, d, h) for i in range(NC6) for d in range(2) for h in range(4)]

    def mlstm_scan_pe(pe):
        def first(u):
            i, d, h = UNITS[u]
            c, b = mchunk(d, i), psum[4 * (u % 2)]
            if c < 2:
                return
            row = 32 * d + h
            M.matmul(b[:, P:2 * P], ident[0:64, row:row + 1].to_broadcast([64, P]), RM[0:64, P * c:P * c + P],
                     start=True, stop=True)
            for a in range(2):
                ins = M.matmul(b[:, 0:P], kqT[:, 2 * h + a, P * (c - 2):P * (c - 1)], q_at(2 * h + a, c),
                               start=(a == 0), stop=(a == 1))
            ins.then_inc(prod.sem, 1)

        def second(u):
            i, d, h = UNITS[u]
            c, b = mchunk(d, i), psum[4 * (u % 2):4 * (u % 2) + 4]
            pe.wait_ge(made_act)
            v, st = vtk[:, c, 256 * h:256 * h + 256], state(d, h)
            if c >= 2:
                pe.wait_ge(made)
                M.matmul(b[1][:, 0:256], stb[u % 2], v, start=True, stop=True)
                M.matmul(b[3][:, 0:1], stb[u % 2], ones[:, 0:1], start=True, stop=True)
                for a in range(2):
                    M.matmul(b[1][:, 256:512], q_at(2 * h + a, c), st[:, a, :], start=(a == 0), stop=(a == 1))
                for a in range(2):
                    M.matmul(b[3][:, 1:2], q_at(2 * h + a, c), nvec[:, 2 * (4 * d + h) + a:2 * (4 * d + h) + a + 1],
                             start=(a == 0), stop=(a == 1))
            for a in range(2):
                M.matmul(b[2][:, 256 * a:256 * a + 256], kwb[u % 2][:, P * a:P * a + P], v, start=True, stop=True)
            for a in range(2):
                ins = M.matmul(b[3][:, 2 + a:3 + a], kwb[u % 2][:, P * a:P * a + P], ones[:, 0:1], start=True, stop=True)
            ins.then_inc(prod.sem, 1)

        for u in range(len(UNITS) + 1):
            if u < len(UNITS):
                if u >= 2:
                    pe.wait_ge(unit_read)
                first(u)
            if u:
                second(u - 1)

    def q_at(n, c):
        return xmT[:, n, P * c:P * c + P]

    def mlstm_scan_act(act):
        def first(u):
            i, d, h = UNITS[u]
            c = mchunk(d, i)
            if u >= 2:
                act.wait_ge(unit_read)
            S.activation(kwb[u % 2], ktk[:, c, 256 * h:256 * h + 256], ACT.Identity, scale=ctk[:, c, 3, d, h:h + 1])\
                .then_inc(made_act.sem, 1)
            if c >= 2:
                act.wait_ge(to_act)
                S.activation(eb[u % 2], tb[u % 2], ACT.Exp, bias=ctk[:, c, 0, d, h:h + 1], scale=-1.0)\
                    .then_inc(to_dve.sem, 1)

        def second(u):
            i, d, h = UNITS[u]
            c = mchunk(d, i)
            if c >= 2:
                act.wait_ge(prod_read)
                S.activation(t1b[u % 2], psum[4 * (u % 2) + 1][:, 256:512], ACT.Identity,
                             scale=ctk[:, c, 1, d, h:h + 1]).then_inc(to_dve.sem, 1)

        for u in range(len(UNITS) + 1):
            if u < len(UNITS):
                first(u)
            if u:
                second(u - 1)

    unit_read, prod_read = signal("unit_through"), signal("unit_products_seen")

    def mlstm_scan_dve(dve):
        seen = set()

        def first(u):
            i, d, h = UNITS[u]
            c, b = mchunk(d, i), psum[4 * (u % 2)]
            if c < 2:
                return
            dve.wait_ge(prod)
            V.tensor_tensor(tb[u % 2], b[:, P:2 * P], neg128[d], ALU.subtract).then_inc(to_act.sem, 1)
            dve.wait_ge(to_dve)
            V.tensor_tensor(stb[u % 2], b[:, 0:P], eb[u % 2], ALU.mult).then_inc(made.sem, 1)

        def second(u):
            i, d, h = UNITS[u]
            c, b, m = mchunk(d, i), psum[4 * (u % 2):4 * (u % 2) + 4], 4 * d + h
            dve.wait_ge(prod)
            den = dens[u % 2]
            if c >= 2:
                dve.e.sem_inc(prod_read.sem, 1)
                link(dve, dve_step, V.tensor_copy(den[:, 2:4], b[3][:, 0:2]))
                link(dve, dve_step, V.scalar_tensor_tensor(den[:, 0:1], den[:, 3:4], ctk[:, c, 1, d, h:h + 1], den[:, 2:3],
                                                           ALU.mult, ALU.add))
                link(dve, dve_step, V.tensor_scalar(den[:, 1:2], den[:, 0:1], -1.0, ctk[:, c, 2, d, h:h + 1],
                                                    ALU.mult, ALU.max))
                link(dve, dve_step, V.tensor_tensor(den[:, 0:1], den[:, 0:1], den[:, 1:2], ALU.max))
                link(dve, dve_step, V.reciprocal(den[:, 1:2], den[:, 0:1]))
            V.scalar_tensor_tensor(nvec[:, 2 * m:2 * m + 2], nvec[:, 2 * m:2 * m + 2], csb[:, m, c:c + 1], b[3][:, 2:4],
                                   ALU.mult, ALU.add)
            ins = V.scalar_tensor_tensor(state(d, h), state(d, h), csb[:, m, c:c + 1],
                                         b[2][:, :].rearrange("p (a v) -> p a v", a=2), ALU.mult, ALU.add)
            if c >= 2:
                dve.wait_ge(to_dve)
                link(dve, dve_step, V.tensor_tensor(t1b[u % 2], t1b[u % 2], b[1][:, 0:256], ALU.add))
                dst = hacc[:, c - 2, 256 * h:256 * h + 256]
                if (c, h) in seen:
                    ins = V.scalar_tensor_tensor(dst, t1b[u % 2], den[:, 1:2], dst, ALU.mult, ALU.add)
                else:
                    seen.add((c, h))
                    ins = V.tensor_scalar(dst, t1b[u % 2], den[:, 1:2], None, ALU.mult)
            link(dve, unit_read, ins)

        for u in range(len(UNITS) + 1):
            if u < len(UNITS):
                first(u)
            if u:
                second(u - 1)

    def mlstm_out_pe(pe):
        pe.wait_ge(made)
        for n in range(KD):
            if n >= 2:
                pe.wait_ge(bonus_read)
            for c in range(NL):
                ins = M.matmul(psum[n % 2][:, P * c:P * c + P], hacc[:, c, P * n:P * n + P], ident, start=True, stop=True)
            ins.then_inc(prod.sem, 1)
        bonus_read.skip(pe, 2)

    def mlstm_out_act(act):
        for n in range(KD):
            S.activation(xcT[:, n, CTX:T], xcT[:, n, CTX:T], ACT.Identity, scale=cols("c_skip", n))\
                .then_inc(to_dve.sem, 1)
        act.wait_ge(ms_ready)
        S.activation(mstat, mstat, ACT.Sqrt).then_inc(root_ready.sem, 1)

    def mlstm_out_dve(dve):
        h4 = hacc.rearrange("p c (h v) -> p (c h) v", h=4)
        sq = flat(vtk)[:, 0:NL * D].rearrange("p (m v) -> p m v", v=256)
        link(dve, dve_step, V.tensor_tensor(sq, h4, h4, ALU.mult))
        link(dve, dve_step, V.tensor_reduce(mstat, sq, AX, ALU.add))
        V.tensor_scalar(mstat, mstat, 1.0 / 256, EPS, ALU.mult, ALU.add).then_inc(ms_ready.sem, 1)
        dve.wait_ge(root_ready)
        link(dve, dve_step, V.reciprocal(mstat, mstat))
        V.tensor_tensor(h4, h4, mstat.unsqueeze(2).to_broadcast([P, 16, 256]), ALU.mult).then_inc(made.sem, 1)
        for n in range(KD):
            dve.wait_ge(prod)
            dve.wait_ge(to_dve)
            t = xcT[:, n, CTX:T]
            link(dve, bonus_read, V.scalar_tensor_tensor(t, psum[n % 2][:, :], cols("c_norm", n), t, ALU.mult, ALU.add))
            V.tensor_tensor(zT[:, n, :], t, zT[:, n, :], ALU.mult)

    ysq1 = vtk.rearrange("p c f -> p (c f)").rearrange("p (k t) -> p k t", k=KD)

    droom = Room()
    half = lambda n: droom.take(n * LAT).rearrange("p (k t) -> p k t", k=n)
    qkvT = half(12)
    zaT = half(4)
    ktok, vtok2, oacc = (droom.take(NL * 512).rearrange("p (c h v) -> p c h v", c=NL, h=4) for _ in range(3))
    dmask = droom.take(18 * P)
    incl_d = [dmask[:, 0:P], dmask[:, P:2 * P]]
    neg_d = [dmask[:, 2 * P:3 * P], dmask[:, 3 * P:4 * P]]
    lev_d = [[dmask[:, P * (4 + 7 * d + lv):P * (5 + 7 * d + lv)] for lv in range(7)] for d in range(2)]
    wab = droom.take(KD * 16).rearrange("p (k n) -> p k n", k=KD)
    alog = droom.take(16)
    cols4 = lambda: droom.take(32).rearrange("p (c m) -> p c m", c=NL)
    gl, beta, gx, Gc, Gt, eG, kdc, dl = (cols4() for _ in range(8))
    dstat = droom.take(16)
    drt = droom.take(T)
    d_at = droom.at
    aroom = Room(d_at)
    fraw = [aroom.take(LAT + 4) for _ in range(2)]
    sqb = aroom.take(4 * LAT)
    msb = aroom.take(4 * LAT)
    sroomd = Room(d_at)
    f4 = lambda: sroomd.take(4 * P).rearrange("p (h t) -> p h t", h=4)
    AT, LT, PMd, RHd, STd, KDC, QD, DM, LMd0, LMd1, XD, XTd = ([f4() for _ in range(2)] for _ in range(12))
    LMd = [[LMd0[d], LMd1[d]] for d in range(2)]
    broom = Room(d_at)
    bh = lambda n: broom.take(n * LAT).rearrange("p (k t) -> p k t", k=n)
    gatesT = bh(16)
    zbT = bh(4)
    ccT = qkvT[:, 0:4, :]
    cfsq = qkvT[:, 4:8, :]
    cpad = [broom.take(LAT + 30) for _ in range(4)]
    sgb = [broom.take(LAT) for _ in range(2)]
    vbb = [broom.take(LAT) for _ in range(2)]
    delta_through, val_used = signal("delta_delta_through"), signal("values_used")

    def delta_load_sp(sp, l):
        if l == 0:
            sp.e.dma_start(dmask, A["delta_masks"][:, 0:18 * P]).then_inc(extra_in.sem, 16)
        for dst, src in ((wab, A[f"ab_cols{l}"]), (alog, A[f"decay_rows{l}"].partition_broadcast(P))):
            sp.e.dma_start(dst, src).then_inc(extra_in.sem, 16)

    def delta_in_pe(pe, l):
        rhs = lambda k, seg: hT[:, k, seg[0]:seg[0] + seg[1]]
        loaded(pe, 12 + 2 * l)
        for c in range(NL):
            for k in range(KD):
                ins = M.matmul(psum[6][:, 16 * c:16 * c + 16], hT[:, k, CTX + P * c:CTX + P * c + P], wab[:, k, :],
                               start=(k == 0), stop=(k == KD - 1))
        ins.then_inc(prod.sem, 1)
        product_pe(pe, 16, rhs, LATENT)

    def delta_in_act(act, l):
        act.wait_ge(to_act)
        link(act, act_step, S.activation(gl, gx, ACT.Abs))
        link(act, act_step, S.activation(gl, gl, ACT.Exp, scale=-1.0))
        S.activation(gl, gl, ACT.Ln, bias=ones[:, 0:1]).then_inc(to_dve.sem, 1)
        link(act, act_step, S.activation(alog[:, 0:8], alog[:, 0:8], ACT.Exp))
        S.activation(beta, psum[6][:, 0:64].rearrange("p (c a m) -> p c a m", c=NL, a=2)[:, :, 1, :], ACT.Sigmoid)\
            .then_inc(to_dve.sem, 1)
        for i in range(13):
            if i < 12:
                act.wait_ge(item_done)
                S.activation(fraw[i % 2][:, 2:2 + LAT], bank_of(act.tiles % 2, LATENT[0]), ACT.Identity)\
                    .then_inc(tile_read.sem, 1)
                act.tiles += 1
            if i:
                act.wait_ge(to_act)
                S.activation(qkvT[:, i - 1, :], qkvT[:, i - 1, :], ACT.Silu)
        tiles_act(act, 4, lambda i, p: S.activation(zaT[:, i, :], bank_of(p, LATENT[0]), ACT.Silu), loop=False)

    def delta_in_dve(dve, l):
        for q in range(2):
            V.memset(fraw[q][:, 0:2], 0.0)
            link(dve, dve_step, V.memset(fraw[q][:, LAT + 2:LAT + 4], 0.0))
        loaded(dve, 12 + 2 * l)
        dve.wait_ge(prod)
        V.tensor_tensor(gx, psum[6][:, 0:64].rearrange("p (c a m) -> p c a m", c=NL, a=2)[:, :, 0, :],
                        alog[:, 8:16].unsqueeze(1).to_broadcast([P, NL, 8]), ALU.add).then_inc(to_act.sem, 1)
        dve.wait_ge(to_dve, 2)
        link(dve, dve_step, V.scalar_tensor_tensor(gl, gx, 0.0, gl, ALU.max, ALU.add))
        link(dve, dve_step, V.scalar_tensor_tensor(gl, gl, -1.0, alog[:, 0:8].unsqueeze(1).to_broadcast([P, NL, 8]),
                                                   ALU.mult, ALU.mult))
        for i in range(12):
            dve.wait_ge(tile_read)
            w = lambda tap: cols("qkv_conv", 12 * (5 * l + tap) + i)
            y = qkvT[:, i, :]
            link(dve, dve_step, V.tensor_scalar(y, fraw[i % 2][:, 0:LAT], w(0), None, ALU.mult))
            for tap in range(1, 5):
                ins = V.scalar_tensor_tensor(y, fraw[i % 2][:, tap:tap + LAT], w(tap), y, ALU.mult, ALU.add)
                if tap < 4:
                    link(dve, dve_step, ins)
                else:
                    ins.then_inc(to_act.sem, 1)
        tile_read.skip(dve, 4)

    def delta_norm_pe(pe):
        for r in range(2):
            pe.wait_ge(sq_ready)
            for j in range(4):
                ins = M.matmul(psum[4 * r + j][:, :], ones, sqb[:, LAT * j:LAT * j + LAT], start=True, stop=True)
            ins.then_inc(sum_ready.sem, 1)

    def delta_norm_act(act):
        for r in range(2):
            if r:
                act.wait_ge(to_act)
            S.activation(sqb, flat(qkvT)[:, 2048 * r:2048 * r + 2048], ACT.Square).then_inc(sq_ready.sem, 1)
            act.wait_ge(ms_ready)
            S.activation(msb, msb, ACT.Sqrt).then_inc(root_ready.sem, 1)

    def delta_norm_dve(dve):
        for r in range(2):
            dve.wait_ge(sum_ready)
            if r == 0:
                V.engine_nop().then_inc(to_act.sem, 1)
            scale = (float(P), P * EPS) if r == 0 else (1.0, EPS)
            for j in range(4):
                ins = V.tensor_scalar(msb[:, LAT * j:LAT * j + LAT], psum[4 * r + j][:, :], scale[0], scale[1],
                                      ALU.mult, ALU.add)
            ins.then_inc(ms_ready.sem, 1)
            dve.wait_ge(root_ready)
            link(dve, dve_step, V.reciprocal(msb, msb))
            t = flat(qkvT)[:, 2048 * r:2048 * r + 2048]
            link(dve, dve_step, V.tensor_tensor(t, t, msb, ALU.mult))

    def delta_turn_pe(pe):
        for c in range(NL):
            for a in range(2):
                for h in range(4):
                    ins = M.matmul(psum[2 * c + a][:, P * h:P * h + P], qkvT[:, 4 + 4 * a + h, P * c:P * c + P], ident,
                                   start=True, stop=True)
            ins.then_inc(prod_act.sem, 1)
        pe.wait_ge(made_act)
        for c in range(NL):
            for d in range(2):
                at = 8 * c + 4 * d
                M.matmul(psum[0][:, at:at + 4], incl_d[d], gl[:, c, 4 * d:4 * d + 4], start=True, stop=True)
                ins = M.matmul(psum[0][:, 64 + at:64 + at + 4], ones, gl[:, c, 4 * d:4 * d + 4], start=True, stop=True)
        ins.then_inc(prod.sem, 1)

    def delta_turn_act(act):
        for c in range(NL):
            act.wait_ge(prod_act)
            b = 2 * c
            ins = S.activation(ktok[:, c], psum[b][:, :].rearrange("p (h v) -> p h v", h=4), ACT.Identity)
            if c == 0:
                ins.then_inc(made_act.sem, 1)
            S.activation(vtok2[:, c], psum[b + 1][:, :].rearrange("p (h v) -> p h v", h=4), ACT.Identity)
        act.wait_ge(to_act)
        link(act, act_step, S.activation(eG, Gc, ACT.Exp))
        link(act, act_step, S.activation(kdc, kdc, ACT.Exp))
        link(act, act_step, S.activation(dl, Gt, ACT.Exp))

    def delta_turn_dve(dve):
        dve.wait_ge(prod)
        link(dve, dve_step, V.tensor_copy(Gc, psum[0][:, 0:32].rearrange("p (c m) -> p c m", c=NL)))
        link(dve, dve_step, V.tensor_copy(Gt, psum[0][:, 64:96].rearrange("p (c m) -> p c m", c=NL)))
        V.tensor_tensor(kdc, Gt, Gc, ALU.subtract).then_inc(to_act.sem, 1)
        link(dve, dve_step, V.tensor_scalar(gx, Gc, -1.0, None, ALU.mult))
        for d in range(2):
            V.memset(STd[d], 0.0)

    def head_mm(dst, lhs, rhs, start=True, stop=True):
        for h in range(4):
            ins = M.matmul(dst[:, P * h:P * h + P], lhs(h), rhs(h), start=start, stop=stop)
        return ins

    def delta_scan_pe(pe):
        B = [[psum[4 * d + i] for i in range(4)] for d in range(2)]
        for i in range(NL):
            for d in range(2):
                c = i if d == 0 else NL - 1 - i
                at = slice(P * c, P * c + P)
                kc, qc = (lambda h: qkvT[:, 4 + h, at]), (lambda h: qkvT[:, h, at])
                if i:
                    pe.wait_ge(delta_through)
                head_mm(B[d][0], lambda h: gl[:, c, 4 * d + h:4 * d + h + 1].to_broadcast([P, P]), lambda h: incl_d[d])\
                    .then_inc(prod_act.sem, 1)
                head_mm(B[d][1], kc, kc)
                head_mm(B[d][2], kc, qc).then_inc(prod.sem, 1)
                head_mm(B[d][3], kc, lambda h: STd[d][:, h, :]).then_inc(prod.sem, 1)
            for lv in range(7):
                for d in range(2):
                    pe.wait_ge(made)
                    ins = head_mm(B[d][0], lambda h: LMd[d][lv % 2][:, h, :],
                                  (lambda h: ident) if lv == 0 else (lambda h: XD[d][:, h, :]))
                    ins.then_inc((prod if lv == 0 else prod_act).sem, 1)
                if lv == 0:
                    continue
                for d in range(2):
                    pe.wait_ge(made_act)
                    if lv < 6:
                        head_mm(B[d][1], lambda h: XTd[d][:, h, :], lambda h: PMd[d][:, h, :])
                    head_mm(B[d][2], lambda h: PMd[d][:, h, :], lambda h: XTd[d][:, h, :]).then_inc(prod.sem, 1)
            for d in range(2):
                pe.wait_ge(made)
                head_mm(B[d][3], lambda h: XTd[d][:, h, :], lambda h: RHd[d][:, h, :]).then_inc(prod.sem, 1)
            for d in range(2):
                pe.wait_ge(made)
                for h in range(4):
                    hs = slice(P * h, P * h + P)
                    M.matmul(B[d][0][:, hs], QD[d][:, h, :], STd[d][:, h, :], start=True, stop=False)
                    ins = M.matmul(B[d][0][:, hs], AT[d][:, h, :], RHd[d][:, h, :], start=False, stop=True)
                head_mm(B[d][1], lambda h: KDC[d][:, h, :], lambda h: RHd[d][:, h, :]).then_inc(prod.sem, 1)
        delta_through.skip(pe, 2)

    def delta_scan_act(act):
        B = [[psum[4 * d + i] for i in range(4)] for d in range(2)]
        for i in range(NL):
            for d in range(2):
                c = i if d == 0 else NL - 1 - i
                act.wait_ge(prod_act)
                S.activation(QD[d], B[d][0][:, :].rearrange("p (h t) -> p h t", h=4), ACT.Exp)
                S.activation(DM[d], B[d][0][:, :].rearrange("p (h t) -> p h t", h=4), ACT.Identity)\
                    .then_inc(to_dve.sem, 1)
                act.wait_ge(to_act)
                for h in range(4):
                    ins = S.activation(DM[d][:, h, :], DM[d][:, h, :], ACT.Exp, bias=gx[:, c, 4 * d + h:4 * d + h + 1])
                ins.then_inc(to_dve.sem, 1)
            for lv in range(1, 7):
                for d in range(2):
                    act.wait_ge(prod_act)
                    S.activation(PMd[d], B[d][0][:, :].rearrange("p (h t) -> p h t", h=4), ACT.Identity)\
                        .then_inc(made_act.sem, 1)

    def delta_scan_dve(dve):
        B = [[psum[4 * d + i][:, :].rearrange("p (h t) -> p h t", h=4) for i in range(4)] for d in range(2)]
        eye = ident.unsqueeze(1).to_broadcast([P, 4, P])
        every = lambda t, c, d: t[:, c, 4 * d:4 * d + 4].unsqueeze(2).to_broadcast([P, 4, P])
        came = set()
        for i in range(NL):
            for d in range(2):
                c = i if d == 0 else NL - 1 - i
                at = slice(P * c, P * c + P)
                level = lambda lv: lev_d[d][lv].unsqueeze(1).to_broadcast([P, 4, P])
                dve.wait_ge(to_dve)
                V.tensor_tensor(DM[d], DM[d], neg_d[d].unsqueeze(1).to_broadcast([P, 4, P]), ALU.add)\
                    .then_inc(to_act.sem, 1)
                V.tensor_tensor(QD[d], QD[d], qkvT[:, 0:4, at], ALU.mult)
                V.tensor_tensor(KDC[d], ktok[:, c], every(kdc, c, d), ALU.mult)
                dve.wait_ge(prod, 2)
                link(dve, dve_step, V.tensor_tensor(RHd[d], B[d][3], every(eG, c, d), ALU.mult))
                link(dve, dve_step, V.tensor_tensor(RHd[d], vtok2[:, c], RHd[d], ALU.subtract))
                dve.wait_ge(to_dve)
                link(dve, dve_step, V.tensor_tensor(LT[d], B[d][1], DM[d], ALU.mult))
                link(dve, dve_step, V.tensor_tensor(LT[d], LT[d], every(beta, c, d), ALU.mult))
                V.tensor_tensor(AT[d], B[d][2], DM[d], ALU.mult)
                link(dve, dve_step, V.tensor_tensor(LMd[d][0], LT[d], level(0), ALU.mult))
                V.scalar_tensor_tensor(XTd[d], LMd[d][0], -1.0, eye, ALU.mult, ALU.add).then_inc(made.sem, 1)
            for lv in range(7):
                for d in range(2):
                    level = lambda lv: lev_d[d][lv].unsqueeze(1).to_broadcast([P, 4, P])
                    if lv < 6:
                        V.tensor_tensor(LMd[d][(lv + 1) % 2], LT[d], level(lv + 1), ALU.mult)
                    dve.wait_ge(prod)
                    if lv == 0:
                        V.scalar_tensor_tensor(XD[d], B[d][0], -1.0, eye, ALU.mult, ALU.add).then_inc(made.sem, 1)
                        continue
                    if lv < 6:
                        V.tensor_tensor(XD[d], XD[d], B[d][1], ALU.subtract)
                    V.tensor_tensor(XTd[d], XTd[d], B[d][2], ALU.subtract).then_inc(made.sem, 1)
            for d in range(2):
                c = i if d == 0 else NL - 1 - i
                dve.wait_ge(prod)
                V.tensor_tensor(RHd[d], B[d][3], every(beta, c, d), ALU.mult).then_inc(made.sem, 1)
            for d in range(2):
                c = i if d == 0 else NL - 1 - i
                dve.wait_ge(prod)
                link(dve, dve_step, V.tensor_tensor(STd[d], STd[d], every(dl, c, d), ALU.mult))
                V.tensor_tensor(STd[d], STd[d], B[d][1], ALU.add)
                if c in came:
                    ins = V.tensor_tensor(oacc[:, c], oacc[:, c], B[d][0], ALU.add)
                else:
                    came.add(c)
                    ins = V.tensor_copy(oacc[:, c], B[d][0])
                link(dve, delta_through, ins)

    def branch_pe(pe):
        product_pe(pe, 28, lambda k, seg: hT[:, k, seg[0]:seg[0] + seg[1]], LATENT)

    def branch_act(act, l):
        for i in range(4):
            act.wait_ge(item_done)
            if i >= 2:
                act.wait_ge(val_used)
            S.activation(sgb[i % 2], bank_of(act.tiles % 2, LATENT[0]), ACT.Sigmoid).then_inc(tile_read.sem, 1)
            act.wait_ge(item_done)
            S.activation(vbb[i % 2], bank_of((act.tiles + 1) % 2, LATENT[0]), ACT.Identity).then_inc(tile_read.sem, 1)
            act.tiles += 2
        val_used.skip(act, 2)
        tiles_act(act, 4, lambda i, p: S.activation(zbT[:, i, :], bank_of(p, LATENT[0]), ACT.Silu), loop=False)
        tiles_act(act, 16, lambda i, p: S.activation(gatesT[:, i, :], bank_of(p, LATENT[0]), ACT.Sigmoid,
                                                     bias=cols("gate_b", 16 * l + i)), loop=False)

    def branch_dve(dve, l):
        for q in range(4):
            V.memset(cpad[q][:, 0:15], 0.0)
            link(dve, dve_step, V.memset(cpad[q][:, LAT + 15:LAT + 30], 0.0))
        for i in range(4):
            dve.wait_ge(tile_read, 2)
            ins = V.tensor_tensor(cpad[i][:, 15:15 + LAT], sgb[i % 2], vbb[i % 2], ALU.mult)
            link(dve, val_used, ins)
            y = ccT[:, i, :]
            w = lambda tap: cols("cf_conv", 4 * (31 * l + tap) + i)
            link(dve, dve_step, V.tensor_scalar(y, cpad[i][:, 0:LAT], w(0), cols("cf_conv_b", 4 * l + i),
                                                ALU.mult, ALU.add))
            for tap in range(1, 31):
                link(dve, dve_step, V.scalar_tensor_tensor(y, cpad[i][:, tap:tap + LAT], w(tap), y, ALU.mult, ALU.add))
        tile_read.skip(dve, 20)

    blocks_before = []
    joined = signal("joined")
    ymixT = qkvT[:, 4:12, :]
    osq = broom.take(4 * LAT)
    t2b = [sgb[0], sgb[1]]

    def join_pe(pe):
        for j in range(4):
            ins = M.matmul(psum[4][:, :], ones, ccT[:, j, :], start=(j == 0), stop=(j == 3))
        ins.then_inc(prod.sem, 1)
        pe.wait_ge(sq_ready)
        for j in range(4):
            ins = M.matmul(psum[5][:, :], ones, cfsq[:, j, :], start=(j == 0), stop=(j == 3))
        ins.then_inc(sum_ready.sem, 1)
        pe.wait_ge(made)
        for h in range(4):
            for c in range(NL):
                ins = M.matmul(psum[h][:, P * c:P * c + P], oacc[:, c, h, :], ident, start=True, stop=True)
            ins.then_inc(prod.sem, 1)
        pe.wait_ge(made)
        blocks_before.append(pe.items)
        for n in range(KD):
            slot = pe.items % SLOTS
            if n >= 2:
                pe.wait_ge(joined)
            pe.wait_ge(landed[slot], 16)
            for b, src in enumerate((zaT, ccT)):
                for k in range(4):
                    ins = M.matmul(psum[2 * (n % 2) + b][:, :], ring[slot][:, P * (4 * b + k):P * (4 * b + k) + P],
                                   src[:, k, :], start=(k == 0), stop=(k == 3))
            ins.then_inc(item_done.sem, 1)
            pe.items += 1
        joined.skip(pe, 2)
        pe.wait_ge(made)
        for n in range(KD):
            slot = pe.items % SLOTS
            if n >= 2:
                pe.wait_ge(joined)
            pe.wait_ge(landed[slot], 16)
            for k in range(KD):
                ins = M.matmul(psum[n % 2][:, :], ring[slot][:, P * k:P * k + P], ymixT[:, k, :],
                               start=(k == 0), stop=(k == KD - 1))
            ins.then_inc(item_done.sem, 1)
            pe.items += 1
        joined.skip(pe, 2)

    def join_act(act, l):
        act.wait_ge(to_act)
        S.activation(cfsq, ccT, ACT.Square).then_inc(sq_ready.sem, 1)
        act.wait_ge(ms_ready)
        S.activation(dstat, dstat, ACT.Sqrt).then_inc(root_ready.sem, 1)
        act.wait_ge(ms_ready)
        S.activation(drt[:, 0:LAT], drt[:, 0:LAT], ACT.Sqrt).then_inc(root_ready.sem, 1)
        act.wait_ge(to_act)
        for j in range(4):
            S.activation(ccT[:, j, :], ccT[:, j, :], ACT.Silu, bias=cols("cf_ln_b", 4 * l + j),
                         scale=cols("cf_ln_w", 4 * l + j)).then_inc(to_dve.sem, 1)
        item_done.skip(act, 16)

    def join_dve(dve, l):
        item_done.seen[dve.name] = SLOTS + blocks_before[l]
        mean = drt[:, 0:LAT]
        dve.wait_ge(prod)
        link(dve, dve_step, V.tensor_scalar(mean, psum[4][:, :], 1.0 / 512, None, ALU.mult))
        spread = mean.unsqueeze(1).to_broadcast([P, 4, LAT])
        ins = V.tensor_tensor(ccT, ccT, spread, ALU.subtract)
        link(dve, dve_step, ins)
        V.engine_nop().then_inc(to_act.sem, 1)
        o = oacc.rearrange("p c h v -> p (c h) v")
        sq = osq.rearrange("p (m v) -> p m v", v=P)
        link(dve, dve_step, V.tensor_tensor(sq, o, o, ALU.mult))
        link(dve, dve_step, V.tensor_reduce(dstat, sq, AX, ALU.add))
        V.tensor_scalar(dstat, dstat, 1.0 / P, EPS, ALU.mult, ALU.add).then_inc(ms_ready.sem, 1)
        dve.wait_ge(root_ready)
        link(dve, dve_step, V.reciprocal(dstat, dstat))
        V.tensor_tensor(o, o, dstat.unsqueeze(2).to_broadcast([P, 16, P]), ALU.mult).then_inc(made.sem, 1)
        dve.wait_ge(sum_ready)
        V.tensor_scalar(mean, psum[5][:, :], 1.0 / 512, EPS, ALU.mult, ALU.add).then_inc(ms_ready.sem, 1)
        dve.wait_ge(root_ready)
        link(dve, dve_step, V.reciprocal(mean, mean))
        V.tensor_tensor(ccT, ccT, spread, ALU.mult).then_inc(to_act.sem, 1)
        for h in range(4):
            dve.wait_ge(prod)
            V.scalar_tensor_tensor(zaT[:, h, :], psum[h][:, :], cols("dn_norm", l), zaT[:, h, :], ALU.mult, ALU.mult)
        for j in range(4):
            dve.wait_ge(to_dve)
            ins = V.tensor_tensor(ccT[:, j, :], ccT[:, j, :], zbT[:, j, :], ALU.mult)
        ins.then_inc(made.sem, 1)
        for n in range(KD):
            tile_ready(dve)
            V.tensor_tensor(ymixT[:, n, :], psum[2 * (n % 2)][:, :], gatesT[:, n, :], ALU.mult)
            link(dve, joined, V.tensor_tensor(t2b[n % 2], psum[2 * (n % 2) + 1][:, :], gatesT[:, KD + n, :], ALU.mult))
            ins = V.tensor_tensor(ymixT[:, n, :], ymixT[:, n, :], t2b[n % 2], ALU.add)
        ins.then_inc(made.sem, 1)
        for n in range(KD):
            tile_ready(dve)
            link(dve, joined, V.tensor_tensor(xT[:, n, CTX:T], xT[:, n, CTX:T], psum[n % 2][:, :], ALU.add))

    def tile_ready(dve):
        dve.wait_ge(item_done)

    def final_dve(dve):
        rms_dve(dve, LATENT, drt, 1.0 / D)
        for k in range(KD):
            V.scalar_tensor_tensor(hT[:, k, CTX:T], xT[:, k, CTX:T], cols("final_w", k), drt[:, CTX:T],
                                   ALU.mult, ALU.mult)

    block = ctx.enter_context(nc.Block())

    @block.sync
    def _(e):
        sp = Engine("sp", e)
        e.dma_start(vec[:, :], A["vectors"]).then_inc(inputs_in.sem, 16)
        e.dma_start(gen[:, :], A["gen_consts"]).then_inc(inputs_in.sem, 16)
        e.dma_start(xT, A["x_in"]).then_inc(inputs_in.sem, 16)
        weights_sp(sp, A["ada_w0"], 48, 8 * P)
        weights_sp(sp, A["ada_w1"], 48, 8 * P)
        mixer_ab_load_sp(sp)
        weights_sp(sp, A["ab_v"], 4, 8 * P)
        weights_sp(sp, A["ab_in"], 19, 8 * P)
        for _ in range(3 + 3):
            phase(sp)
        e.dma_start(xT, A["x_in"]).then_inc(moved.sem, 16)
        weights_sp(sp, A["ab_out"], 8, 8 * P)
        weights_sp(sp, A["ffn_up0"], 2 * KF, 8 * P)
        weights_sp(sp, A["ffn_down0"], 24, 8 * P)
        phase(sp)
        phase(sp)
        phase(sp)
        mlstm_load_sp(sp)
        weights_sp(sp, A["c_in"], 17, 8 * P)
        weights_sp(sp, A["c_out"], 8, 8 * P)
        weights_sp(sp, A["ffn_up1"], 2 * KF, 8 * P)
        weights_sp(sp, A["ffn_down1"], 24, 8 * P)
        for _ in range(8):
            phase(sp)
        for l in range(2):
            delta_load_sp(sp, l)
            weights_sp(sp, A[f"d_in{l}"], 16, 8 * P)
            weights_sp(sp, A[f"d_branch{l}"], 28, 8 * P)
            weights_sp(sp, A[f"d_join{l}"], 8, 8 * P)
            weights_sp(sp, A[f"d_out{l}"], 8, 8 * P)
            for _ in range(7):
                phase(sp)
        phase(sp)
        e.dma_start(out, hT[:, :, CTX:T]).then_inc(stored.sem, 16)
        sp.wait_ge(stored, 16)

    @block.tensor
    def _(e):
        pe = Engine("pe", e)
        e.sem_inc(item_done.sem, SLOTS)
        pe.wait_ge(inputs_in, 48)
        pe.wait_ge(made_act)
        ada_pe(pe, 0)
        ada_pe(pe, 1)
        rms_pe(pe, lambda k: hT[:, k, :], KD, BOTH)
        phase(pe)
        mixer_ab_in_pe(pe)
        phase(pe)
        spatial_pe(pe)
        phase(pe)
        lora_pe(pe)
        phase(pe)
        rwkv_pe(pe)
        phase(pe)
        rwkv_out_pe(pe)
        phase(pe)
        product_pe(pe, 8, mix_in, BOTH)
        rms_pe(pe, sq_l0, KD, BOTH)
        phase(pe)
        rms_pe(pe, lambda k: hT[:, k, :], KD, BOTH)
        phase(pe)
        ffn_pe(pe, BOTH)
        pe.wait_ge(made)
        ffn_down_pe(pe, BOTH)
        rms_pe(pe, lambda k: fsq[:, k, :], KD, BOTH)
        phase(pe)
        rms_pe(pe, lambda k: hT[:, k, :], KD, BOTH)
        phase(pe)
        mlstm_in_pe(pe)
        phase(pe)
        mlstm_mid_pe(pe)
        phase(pe)
        mlstm_scan_pe(pe)
        phase(pe)
        mlstm_out_pe(pe)
        phase(pe)
        product_pe(pe, 8, lambda k, seg: zT[:, k, :], LATENT)
        rms_pe(pe, lambda k: ysq1[:, k, :], KD, LATENT)
        phase(pe)
        rms_pe(pe, lambda k: hT[:, k, :], KD, LATENT)
        phase(pe)
        ffn_pe(pe, LATENT)
        pe.wait_ge(made)
        ffn_down_pe(pe, LATENT)
        rms_pe(pe, lambda k: fsq[:, k, :], KD, LATENT)
        phase(pe)
        for l in range(2):
            rms_pe(pe, lambda k: hT[:, k, :], KD, LATENT)
            phase(pe)
            delta_in_pe(pe, l)
            phase(pe)
            delta_norm_pe(pe)
            phase(pe)
            delta_turn_pe(pe)
            phase(pe)
            delta_scan_pe(pe)
            phase(pe)
            branch_pe(pe)
            phase(pe)
            join_pe(pe)
            phase(pe)
        rms_pe(pe, lambda k: hT[:, k, :], KD, LATENT)
        phase(pe)

    @block.scalar
    def _(e):
        act = Engine("act", e)
        e.sem_inc(tile_read.sem, 2)
        item_done.skip(act, SLOTS)
        act.wait_ge(inputs_in, 48)
        S.activation(small[:, 0:16], cols("c", 0, 16), ACT.Silu).then_inc(made_act.sem, 1)
        item_done.skip(act, 96)
        rms_act(act, lambda k: xT[:, k, :], lambda k: hT[:, k, :], KD, BOTH, rtN)
        prenorm_act(act, BOTH, 0)
        phase(act)
        mixer_ab_in_act(act)
        phase(act)
        spatial_act(act)
        phase(act)
        lora_act(act)
        phase(act)
        rwkv_act(act)
        phase(act)
        rwkv_out_act(act)
        phase(act)
        tiles_act(act, 8, keep(yT_l0, BOTH), loop=False)
        act.e.drain()
        rms_act(act, yT_l0, sq_l0, KD, BOTH, rtB)
        phase(act)
        rms_act(act, lambda k: xT[:, k, :], lambda k: hT[:, k, :], KD, BOTH, frt)
        prenorm_act(act, BOTH, 3)
        phase(act)
        ffn_act(act, 0, BOTH)
        tiles_act(act, KD, keep(lambda k: hT[:, k, :], BOTH), per=3, loop=False)
        act.e.drain()
        rms_act(act, lambda k: hT[:, k, :], lambda k: fsq[:, k, :], KD, BOTH, frt)
        phase(act)
        rms_act(act, lambda k: xT[:, k, :], lambda k: hT[:, k, :], KD, BOTH, frt)
        prenorm_act(act, BOTH, 0)
        phase(act)
        mlstm_in_act(act)
        phase(act)
        mlstm_mid_act(act)
        phase(act)
        mlstm_scan_act(act)
        phase(act)
        mlstm_out_act(act)
        phase(act)
        tiles_act(act, 8, keep(lambda k: xmT[:, k, :], LATENT), loop=False)
        act.e.drain()
        rms_act(act, lambda k: xmT[:, k, :], lambda k: ysq1[:, k, :], KD, LATENT, mrt)
        phase(act)
        rms_act(act, lambda k: xT[:, k, :], lambda k: hT[:, k, :], KD, LATENT, frt)
        prenorm_act(act, LATENT, 3)
        phase(act)
        ffn_act(act, 1, LATENT)
        tiles_act(act, KD, keep(lambda k: hT[:, k, :], LATENT), per=3, loop=False)
        act.e.drain()
        rms_act(act, lambda k: hT[:, k, :], lambda k: fsq[:, k, :], KD, LATENT, frt)
        phase(act)
        for l in range(2):
            rms_act(act, lambda k: xT[:, k, :], lambda k: hT[:, k, :], KD, LATENT, drt)
            phase(act)
            delta_in_act(act, l)
            phase(act)
            delta_norm_act(act)
            phase(act)
            delta_turn_act(act)
            phase(act)
            delta_scan_act(act)
            phase(act)
            branch_act(act, l)
            phase(act)
            join_act(act, l)
            phase(act)
        rms_act(act, lambda k: xT[:, k, :], lambda k: hT[:, k, :], KD, LATENT, drt)
        phase(act)

    @block.vector
    def _(e):
        dve = Engine("dve", e)
        tile_read.skip(dve, 2)
        dve.wait_ge(inputs_in, 48)
        ada_dve(dve, 0)
        ada_dve(dve, 1)
        link(dve, dve_step, V.memset(small[:, 41:42], 0.0))
        modv_dve(dve, 0)
        prenorm_dve(dve, BOTH, rtN)
        phase(dve)
        mixer_ab_in_dve(dve)
        phase(dve)
        spatial_dve(dve)
        phase(dve)
        lora_dve(dve)
        phase(dve)
        rwkv_dve(dve)
        phase(dve)
        rwkv_out_dve(dve)
        phase(dve)
        tile_read.skip(dve, 8)
        dve.wait_ge(moved, 16)
        residual_dve(dve, BOTH, yT_l0, rtB, 2)
        phase(dve)
        prenorm_dve(dve, BOTH, frt)
        phase(dve)
        ffn_dve(dve, 0, BOTH)
        V.drain().then_inc(made.sem, 1)
        tile_read.skip(dve, 8)
        residual_dve(dve, BOTH, lambda k: hT[:, k, :], frt, 5)
        phase(dve)
        modv_dve(dve, 1)
        prenorm_dve(dve, BOTH, frt)
        phase(dve)
        mlstm_in_dve(dve)
        phase(dve)
        mlstm_mid_dve(dve)
        phase(dve)
        mlstm_scan_dve(dve)
        phase(dve)
        mlstm_out_dve(dve)
        phase(dve)
        tile_read.skip(dve, 8)
        residual_dve(dve, LATENT, lambda k: xmT[:, k, :], mrt, 2)
        phase(dve)
        prenorm_dve(dve, LATENT, frt)
        phase(dve)
        ffn_dve(dve, 1, LATENT)
        V.drain().then_inc(made.sem, 1)
        tile_read.skip(dve, 8)
        residual_dve(dve, LATENT, lambda k: hT[:, k, :], frt, 5)
        phase(dve)
        for l in range(2):
            prenorm_dve(dve, LATENT, drt, cols("norm_w", 8 * l, 8))
            phase(dve)
            delta_in_dve(dve, l)
            phase(dve)
            delta_norm_dve(dve)
            phase(dve)
            delta_turn_dve(dve)
            phase(dve)
            delta_scan_dve(dve)
            phase(dve)
            branch_dve(dve, l)
            phase(dve)
            join_dve(dve, l)
            phase(dve)
        final_dve(dve)
        phase(dve)

    @block.gpsimd
    def _(e):
        pool = Engine("pool", e)
        for _ in range(17 + 15):
            phase(pool)


def tiles_of(w, n=P):
    import numpy as np
    k, m = w.shape
    return np.ascontiguousarray(w.reshape(k // P, P, m // n, n).transpose(2, 1, 0, 3)).reshape(m // n, P, -1)


def lay_out(I):
    import numpy as np
    r = lambda a: np.asarray(a).reshape(-1, P)
    rows = {"c": np.concatenate([r(I["c"]), r(I["c_ctx"])]), "ada_b": r(I["ada_b"]), "mix_pre": r(I["norm_mix_pre"]),
            "mix_post": r(I["norm_mix_post"]), "ffn_pre": r(I["norm_ffn_pre"]), "ffn_post": r(I["norm_ffn_post"]),
            "ffn_conv": r(I["ffn_conv"]), "ffn_conv_b": r(I["ffn_conv_b"]), "norm_w": r(I["norm_w_2"]),
            "qkv_conv": r(I["qkv_conv_w_2"]), "dn_norm": r(I["dn_norm_w_2"]), "cf_conv": r(I["cf_conv_w_2"]),
            "cf_conv_b": r(I["cf_conv_b_2"]), "cf_ln_w": r(I["cf_ln_w_2"]), "cf_ln_b": r(I["cf_ln_b_2"]),
            "gate_b": r(I["gate_b_2"]), "final_w": r(I["final_norm_w_2"])}
    for name, _ in VECTORS:
        if name not in rows:
            rows[name] = r(I[name])
    L = {"vectors": np.ascontiguousarray(np.concatenate([rows[n] for n, _ in VECTORS]).T),
         "gen_consts": general_constants(), "rwkv_masks": rwkv_constants(), "delta_masks": delta_constants()}
    x = np.concatenate([I["ctx"][0], I["x"][0]]).T
    L["x_in"] = np.ascontiguousarray(x.reshape(KD, P, T).transpose(1, 0, 2))
    w = I["ab_w_in"][0]
    aw = 512
    L["ab_v"] = np.ascontiguousarray(w[:, aw:2 * aw].reshape(4, 2, P, aw).transpose(0, 2, 1, 3)).reshape(4, P, 2 * aw)
    o = 2 * aw + 3 * 512
    L["ab_in"] = tiles_of(np.concatenate([w[:, 0:aw], w[:, o:o + 384], w[:, 2 * aw:o]], 1))
    lora = np.concatenate([I["b_w_up"][0].reshape(P, 512), I["b_a_up"][0].reshape(P, 512), I["b_g_up"][0]], 1)
    L["lora_w"] = np.ascontiguousarray(lora)
    L["a_wsT"] = np.ascontiguousarray(I["a_ws"][0].transpose(2, 0, 1)).reshape(P, 512)
    L["a_bs"] = I["a_bs"][0].reshape(512)
    L["ab_out"] = tiles_of(I["ab_w_out"][0])
    w = I["c_w_in"][0]
    gates = np.zeros((D, 4, 32), w.dtype)
    gates[:, :, 0:4] = w[:, 2 * D:].reshape(D, 4, 4)
    L["c_in"] = tiles_of(np.concatenate([w[:, :2 * D], gates.reshape(D, P)], 1))
    gc = np.zeros((4, 32), w.dtype)
    gc[0:2, 0:4], gc[2:4, 0:4] = I["c_bi"][0], I["c_bf"][0]
    L["gate_cols"] = gc.reshape(P, 1)
    L["c_out"] = tiles_of(I["c_w_out"][0])
    q = np.stack([I["c_wq"][0], I["c_wk"][0], I["c_wv"][0]]).reshape(3, KD, P, 4)
    L["qkv_blocks"] = np.ascontiguousarray(q.transpose(2, 0, 1, 3)).reshape(P, 96)
    for l in range(2):
        w = I["w_in_2"][l]
        L[f"d_in{l}"] = tiles_of(w[:, 0:2048])
        L[f"ab_cols{l}"] = np.ascontiguousarray(w[:, 2048:2064].reshape(KD, P, 16).transpose(1, 0, 2))
        L[f"decay_rows{l}"] = np.concatenate([I["a_log_2"][l].reshape(8), I["dt_bias_2"][l].reshape(8)])
        val, glu, rest = w[:, 2064:2576].reshape(D, 4, P), w[:, 2576:3088].reshape(D, 4, P), w[:, 3088:]
        L[f"d_branch{l}"] = tiles_of(np.concatenate([np.stack([glu, val], 2).reshape(D, 1024), rest], 1))
        both = np.concatenate([I["w_dn_out_2"][l], I["w_cf_out_2"][l]])
        L[f"d_join{l}"] = tiles_of(both)
        L[f"d_out{l}"] = tiles_of(I["w_out_2"][l])
    for l in range(2):
        L[f"ada_w{l}"] = tiles_of(I["ada_w"][l])
        up = I["ffn_up"][l].reshape(D, 2, KF, P).transpose(0, 2, 1, 3).reshape(D, 2 * DFF)
        L[f"ffn_up{l}"] = tiles_of(up)
        L[f"ffn_down{l}"] = down_blocks(I["ffn_down"][l])
    return L


def down_blocks(w):
    import numpy as np
    full = np.concatenate([w, np.zeros((2 * P, D), w.dtype)])
    t = tiles_of(full)
    return np.ascontiguousarray(t.reshape(KD, P, 3, 8 * P).transpose(0, 2, 1, 3)).reshape(24, P, 8 * P)


def kernel(**inputs):
    import numpy as np
    import concourse.bacc as bacc
    from concourse.bass_utils import run_bass_kernel_spmd

    nc = bacc.Bacc("TRN2", target_bir_lowering=False, num_devices=1)
    arrays, A = {}, {}
    for name, a in lay_out({n: np.asarray(v) for n, v in inputs.items()}).items():
        a = np.ascontiguousarray(a)
        arrays[f"in_{name}_dram"] = a
        A[name] = nc.dram_tensor(f"in_{name}_dram", a.shape, mybir.dt.from_np(a.dtype), kind="ExternalInput").ap()
    out = nc.dram_tensor("out_0_dram", (P, KD, LAT), F32, kind="ExternalOutput").ap()
    program(nc, A, out)
    r = run_bass_kernel_spmd(nc, [arrays], core_ids=[0])
    got = r.results[0]["out_0_dram"]
    return np.ascontiguousarray(got.transpose(1, 0, 2).reshape(D, LAT).T).reshape(1, LAT, D)
```

```python
from contextlib import ExitStack, contextmanager
import math

import concourse.bass as bass
from concourse import mybir

F32 = mybir.dt.float32
F32R = mybir.dt.float32r
ALU = mybir.AluOpType
ACT = mybir.ActivationFunctionType
AX = mybir.AxisListType.X

P = 128
D = 1024
KD = D // P
CTX, LAT = 256, 512
T = CTX + LAT
DFF = 2816
KF = DFF // P
EPS = 1e-6
LN_EPS = 64e-5
RC = 64
RDECAY = math.exp(-0.5)
MC = 128
NEG = -1e30
SLOTS = 4
ROWS, COLS = 8, 64

VECTORS = [("c", 16), ("ada_b", 96), ("mix_pre", 16), ("mix_post", 16), ("ffn_pre", 16), ("ffn_post", 16),
           ("ffn_conv", 2 * 9 * KF), ("ffn_conv_b", 2 * KF), ("a_gv", 4), ("b_shift", 36), ("b_w0", 8), ("b_a0", 8),
           ("b_kk", 4), ("b_ka", 4), ("b_rk", 4), ("b_ln_g", 4), ("b_ln_b", 4), ("c_conv", 24), ("c_conv_b", 8),
           ("c_norm", 8), ("c_skip", 8), ("norm_w", 16), ("qkv_conv", 120), ("dn_norm", 2), ("cf_conv", 248),
           ("cf_conv_b", 8), ("cf_ln_w", 8), ("cf_ln_b", 8), ("gate_b", 32), ("final_w", 8)]
COL, _n = {}, 0
for _name, _rows in VECTORS:
    COL[_name] = _n
    _n += _rows
NVEC = _n


def rwkv_constants():
    import numpy as np
    s = np.arange(P)[:, None] % RC
    t = np.arange(RC)[None, :]
    parts = []
    for d in range(2):
        strict = (s < t) if d == 0 else (s > t)
        incl = (s <= t) if d == 0 else (s >= t)
        parts += [strict, incl]
    for d in range(2):
        strict = (s < t) if d == 0 else (s > t)
        for lv in range(6):
            w = 1 << lv
            parts.append(strict & (s // (2 * w) == t // (2 * w)) & (s // w != t // w))
    pos = np.arange(T)[None, :] % RC
    parts.append(np.broadcast_to(pos != 0, (P, T)))
    return np.concatenate([np.asarray(x, np.float32) for x in parts], 1)


def delta_constants():
    import numpy as np
    s = np.arange(P)[:, None]
    t = np.arange(P)[None, :]
    parts = []
    for d in range(2):
        incl = (s <= t) if d == 0 else (s >= t)
        parts.append(incl)
    for d in range(2):
        incl = (s <= t) if d == 0 else (s >= t)
        parts.append(np.where(incl, 0.0, NEG))
    for d in range(2):
        strict = (s < t) if d == 0 else (s > t)
        for lv in range(7):
            w = 1 << lv
            parts.append(strict & (s // (2 * w) == t // (2 * w)) & (s // w != t // w))
    parts.append(s // 4 == t // 4)
    return np.concatenate([np.asarray(x, np.float32) for x in parts], 1)


def general_constants():
    import numpy as np
    i = np.arange(P)
    return np.concatenate([np.ones((P, P)), np.eye(P), (i[:, None] // 64 == i[None, :] // 64),
                           (i[:, None] % 64 == np.arange(64)[None, :])], 1).astype(np.float32)


NRC = 4 * RC + 12 * RC + 2 * T
NDC = 19 * P
NGC = 3 * P + 64


class Signal:

    def __init__(self, sem):
        self.sem = sem
        self.seen = {}

    def due(self, who, n=1):
        self.seen[who.name] = k = self.seen.get(who.name, 0) + n
        if who.turn is None or self not in who.per:
            return k
        return who.turn * who.per[self] + k

    def skip(self, who, n):
        self.seen[who.name] = self.seen.get(who.name, 0) + n


class Engine:

    def __init__(self, name, e):
        self.name, self.e, self.turn, self.per = name, e, None, {}
        self.items = 0
        self.also = {}
        self.tiles = 0

    def wait_ge(self, sig, n=1):
        self.e.wait_ge(sig.sem, sig.due(self, n))

    @contextmanager
    def repeat(self, n, per):
        if n == 1:
            yield 0
            return
        with self.e.Fori(0, n) as i:
            before = {s: s.seen.get(self.name, 0) for s in SIGNALS}
            self.turn, self.per = i, per
            yield i
            self.turn = None
        for s in SIGNALS:
            got = s.seen.get(self.name, 0) - before[s]
            assert got == per.get(s, 0), (self.name, s.label, got, per.get(s, 0))
            s.seen[self.name] = before[s] + got * n


SIGNALS = []


def program(nc, A, out):
    with ExitStack() as ctx:
        build(nc, A, out, ctx)


def build(nc, A, out, ctx):
    SIGNALS.clear()
    V, S, G, M = nc.vector, nc.scalar, nc.gpsimd, nc.tensor

    def signal(name):
        q = Signal(ctx.enter_context(nc.semaphore(name)))
        q.label = name
        SIGNALS.append(q)
        return q

    def sb(name, n):
        return ctx.enter_context(nc.sbuf_tensor(name, [P, n], F32))

    def parts_at(name, n, before=0):
        with ExitStack() as place:
            if before:
                place.enter_context(nc.sbuf_tensor(f"{name}_before", [P, before], F32))
            return place.enter_context(nc.sbuf_tensor(name, [P, n], F32R))

    x_all = sb("x_all", KD * T)
    h_low = parts_at("h_low", KD * T)
    h_all = sb("h_all", KD * T)
    ring, ring_low = [], []
    for i in range(SLOTS):
        ring_low.append(parts_at(f"ring_low{i}", 8 * P))
        ring.append(sb(f"ring{i}", 8 * P))
    vec = sb("vec", NVEC)
    gen = sb("gen", NGC)
    mods = sb("mods", 2 * 96)
    modv = sb("modv", 6 * KD * 2)
    small = sb("small", 256)
    xT = x_all[:, :].rearrange("p (k t) -> p k t", k=KD)
    hT = h_all[:, :].rearrange("p (k t) -> p k t", k=KD)
    hlT = h_low[:, :].rearrange("p (k t) -> p k t", k=KD)
    ones, ident, halves, ident64 = gen[:, 0:P], gen[:, P:2 * P], gen[:, 2 * P:3 * P], gen[:, 3 * P:3 * P + 64]
    ARENA = (nc.sbuf_bytes_remaining - 512) // 4
    J4, A8, L8 = 4 * T, KD * T, KD * LAT
    tiles8 = lambda t: t[:, :].rearrange("p (k t) -> p k t", k=KD)
    hh_ab = tiles8(parts_at("h_high_ab", A8, 6 * J4))
    wh_ab = [parts_at(f"w_high_ab{i}", D, 8 * J4 + D * i if i < 3 else 3 * J4)[:, :] for i in range(SLOTS)]
    HH_FFN, WH_FFN = 21808, 28720
    hh_ffn = tiles8(parts_at("h_high_ffn", A8, HH_FFN))
    wh_ffn = [parts_at(f"w_high_ffn{i}", D, WH_FFN + D * i)[:, :] for i in range(SLOTS)]
    hh_m = tiles8(parts_at("h_high_m", A8, 2 * A8 + 2 * L8))
    wh_m = [parts_at(f"w_high_m{i}", D, 2 * A8 + L8 + D * i)[:, :] for i in range(SLOTS)]
    HH_D = 22952
    hh_d, hl_d = (tiles8(parts_at(f"h_{n}_d", L8, HH_D + L8 * i)) for i, n in enumerate(("high", "low")))
    wh_d = [parts_at(f"w_high_d{i}", D, 16 * LAT + D * i)[:, :] for i in range(SLOTS)]
    hh_b = tiles8(parts_at("h_high_b", L8, 4 * LAT))
    arena = sb("arena", ARENA)
    psum = [ctx.enter_context(nc.psum_tensor(f"bank{i}", [P, 512], F32)) for i in range(8)]

    class Room:

        def __init__(self, at=0, end=ARENA, where=arena):
            self.at, self.end, self.where = at, end, where

        def take(self, n):
            self.at += n
            assert self.at <= self.end, (self.at, self.end)
            return self.where[:, self.at - n:self.at]

    def cols(name, at=0, n=1):
        return vec[:, COL[name] + at:COL[name] + at + n]

    BOTH = [(0, CTX), (CTX, LAT)]
    LATENT = [(CTX, LAT)]

    def bank_of(pair, seg):
        return psum[2 * pair + (seg[0] == 0)][:, 0:seg[1]]

    landed = [signal(f"block_landed{i}") for i in range(SLOTS)]
    item_done = signal("block_used")
    tile_read = signal("tile_read")
    inputs_in = signal("inputs_in")
    extra_in = signal("extra_in")
    phase_done = signal("phase_done")
    sq_ready = signal("squares_ready")
    sum_ready = signal("sums_ready")
    ms_ready = signal("mean_squares_ready")
    root_ready = signal("roots_ready")
    scaled = signal("scaled_ready")
    moved = signal("inputs_moved")
    dve_step = signal("dve_step")
    act_step = signal("act_step")
    stored = signal("stored")
    pool_step = signal("pool_step")
    block_seen = signal("block_seen")
    split_ready = signal("split_ready")
    made = signal("dve_made")
    made_act = signal("act_made")
    prod = signal("product_ready")
    prod_act = signal("product_ready_act")
    to_act = signal("dve_to_act")
    to_dve = signal("act_to_dve")
    room_dve = signal("room_from_dve")
    room_pe = signal("banks_free")

    group_read = signal("group_read")
    bonus_read = signal("bonus_read")
    step_through = signal("step_through")

    def link(e, step, ins):
        ins.then_inc(step.sem, 1)
        e.wait_ge(step)

    def loaded(e, n):
        e.e.wait_ge(extra_in.sem, 16 * n)

    def phase(e):
        if e.name != "sp":
            e.e.drain().then_inc(phase_done.sem, 1)
        e.wait_ge(phase_done, 4)

    def weights_sp(sp, w, n, start=0):
        def one(src, slot):
            sp.wait_ge(item_done)
            sp.e.dma_start(ring[slot][:, :], src).then_inc(landed[slot].sem, 16)

        n -= start
        turns = n // SLOTS if n >= 2 * SLOTS else 0
        if turns:
            with sp.repeat(turns, {item_done: SLOTS}) as i:
                for j in range(SLOTS):
                    one(w[bass.ds(i * SLOTS + (j + start), 1)].rearrange("a p n -> (a p) n"), (sp.items + j) % SLOTS)
        for j in range(turns * SLOTS, n):
            one(w[start + j], (sp.items + j) % SLOTS)
        sp.items += n

    def split_pool(pool, n, high, start):
        pool.items = start
        for i in range(SLOTS):
            landed[i].seen["pool"] = 16 * ((start - i + SLOTS - 1) // SLOTS)

        def one(j):
            slot = (start + j) % SLOTS
            w, wh = ring[slot][:, :], high[slot]
            pool.wait_ge(landed[slot], 16)
            pool.e.sem_inc(block_seen.sem, 1)
            link(pool, pool_step, G.tensor_scalar(wh, w, 1.0, 0.0, ALU.mult, ALU.add))
            G.tensor_tensor(ring_low[slot][:, :], w, wh.bitcast(F32), ALU.subtract).then_inc(split_ready.sem, 1)

        turns = n // SLOTS
        with pool.repeat(turns, {pool_step: SLOTS, **{landed[i]: 16 for i in range(SLOTS)}}):
            for j in range(SLOTS):
                one(j)
        for j in range(turns * SLOTS, n):
            one(j)

    def split_product_pe(pe, n, high, xh, xl, segs):
        def one(tile, slot):
            pe.wait_ge(tile_read)
            pe.wait_ge(split_ready)
            landed[slot].skip(pe, 16)
            wl, wh = ring_low[slot], high[slot]
            for k in range(KD):
                at = slice(k * P, k * P + P)
                for w, x, first, last in ((wh, xh, k == 0, False), (wh, xl, False, False), (wl, xh, False, k == KD - 1)):
                    for seg in segs:
                        ins = M.matmul(bank_of(tile % 2, seg), w[:, at], x(k, seg), start=first, stop=last)
            ins.then_inc(item_done.sem, 1)

        turns = n // 4 if n >= 8 else 0
        if turns:
            with pe.repeat(turns, {tile_read: 4, split_ready: 4, **{landed[i]: 16 for i in range(SLOTS)}}):
                for j in range(4):
                    one(pe.tiles + j, (pe.items + j) % SLOTS)
        for j in range(4 * turns, n):
            one(pe.tiles + j, (pe.items + j) % SLOTS)
        pe.items += n
        pe.tiles += n

    def part(t, at=0):
        return lambda k, seg: t[:, k, seg[0] - at:seg[0] - at + seg[1]]

    block_starts = {}

    def product_pe(pe, n, rhs, segs, parts=(8,), loop=True, last_part=None):
        def one(tile, item):
            pe.wait_ge(tile_read)
            done = 0
            for b, nk in enumerate(parts):
                slot = (item + b) % SLOTS
                pe.wait_ge(landed[slot], 16)
                if last_part and b == len(parts) - 1:
                    pe.wait_ge(last_part)
                for k in range(nk):
                    for seg in segs:
                        ins = M.matmul(bank_of(tile % 2, seg), ring[slot][:, k * P:(k + 1) * P], rhs(done + k, seg),
                                       start=(done + k == 0), stop=(done + k == sum(parts) - 1))
                done += nk
                ins.then_inc(item_done.sem, 1)

        per = len(parts)
        turns = n // 4 if loop and n >= 8 else 0
        if turns:
            counts = {landed[i]: 16 * per for i in range(SLOTS)}
            counts[tile_read] = 4
            with pe.repeat(turns, counts):
                for j in range(4):
                    one(pe.tiles + j, pe.items + j * per)
        for j in range(4 * turns, n):
            one(pe.tiles + j, pe.items + j * per)
        pe.items += n * per
        pe.tiles += n

    def tiles_act(act, n, evict, per=1, loop=True):
        def one(i, j):
            act.wait_ge(item_done, per)
            evict(i, (act.tiles + j) % 2).then_inc(tile_read.sem, 1)

        turns = n // 4 if loop and n >= 8 else 0
        if turns:
            with act.repeat(turns, {item_done: 4 * per, **act.also}) as t:
                for j in range(4):
                    one(t * 4 + j, j)
        for j in range(4 * turns, n):
            one(j, j)
        act.tiles += n

    rtN = arena[:, 0:T]

    def rms_act(act, src, scratch, n, segs, rt, added=False):
        lo, hi = segs[0][0], segs[-1][0] + segs[-1][1]
        for k in range(n):
            if added:
                act.wait_ge(to_act)
            S.activation(scratch(k)[:, lo:hi], src(k)[:, lo:hi], ACT.Square).then_inc(sq_ready.sem, 1)
        act.wait_ge(ms_ready)
        S.activation(rt[:, lo:hi], rt[:, lo:hi], ACT.Sqrt).then_inc(root_ready.sem, 1)

    def rms_pe(pe, scratch, n, segs, matrix=ones):
        for k in range(n):
            pe.wait_ge(sq_ready)
            for seg in segs:
                ins = M.matmul(psum[4 + (seg[0] == 0)][:, 0:seg[1]], matrix, scratch(k)[:, seg[0]:seg[0] + seg[1]],
                               start=(k == 0), stop=(k == n - 1))
        ins.then_inc(sum_ready.sem, 1)

    def rms_dve(dve, segs, rt, scale, eps=EPS):
        dve.wait_ge(sum_ready)
        for seg in segs:
            ins = V.tensor_scalar(rt[:, seg[0]:seg[0] + seg[1]], psum[4 + (seg[0] == 0)][:, 0:seg[1]], scale, eps,
                                  ALU.mult, ALU.add)
        ins.then_inc(ms_ready.sem, 1)
        dve.wait_ge(root_ready)
        lo, hi = segs[0][0], segs[-1][0] + segs[-1][1]
        link(dve, dve_step, V.reciprocal(rt[:, lo:hi], rt[:, lo:hi]))

    def mod_col(i, k, seg):
        at = (i * KD + k) * 2 + (seg[0] == 0)
        return modv[:, at:at + 1]

    def split_dve(dve, segs, high, ready):
        lo, hi = segs[0][0], segs[-1][0] + segs[-1][1]
        for k in range(KD):
            dve.wait_ge(ready)
            h, hh = hT[:, k, lo:hi], high[:, k, lo:hi]
            link(dve, dve_step, V.tensor_copy(hh, h))
            V.tensor_tensor(hlT[:, k, lo:hi], h, hh.bitcast(F32), ALU.subtract)

    def prenorm_dve(dve, segs, rt, weight=None):
        rms_dve(dve, segs, rt, 1.0 / D)
        lo, hi = segs[0][0], segs[-1][0] + segs[-1][1]
        for k in range(KD):
            if weight is None:
                V.tensor_tensor(hT[:, k, lo:hi], xT[:, k, lo:hi], rt[:, lo:hi], ALU.mult).then_inc(scaled.sem, 1)
            else:
                V.scalar_tensor_tensor(hT[:, k, lo:hi], xT[:, k, lo:hi], weight[:, k:k + 1], rt[:, lo:hi],
                                       ALU.mult, ALU.mult).then_inc(to_act.sem, 1)

    def prenorm_act(act, segs, which):
        for k in range(KD):
            act.wait_ge(scaled)
            for seg in segs:
                t = hT[:, k, seg[0]:seg[0] + seg[1]]
                ins = S.activation(t, t, ACT.Identity, bias=mod_col(which + 1, k, seg), scale=mod_col(which, k, seg))
            ins.then_inc(to_dve.sem, 1)

    def residual_dve(dve, segs, y, rt, which):
        rms_dve(dve, segs, rt, 1.0 / D)
        for k in range(KD):
            for seg in segs:
                a, b = seg[0], seg[0] + seg[1]
                ins = V.scalar_tensor_tensor(y(k)[:, a:b], y(k)[:, a:b], mod_col(which, k, seg), rt[:, a:b],
                                             ALU.mult, ALU.mult)
        link(dve, dve_step, ins)
        lo, hi = segs[0][0], segs[-1][0] + segs[-1][1]
        for k in range(KD):
            V.tensor_tensor(xT[:, k, lo:hi], xT[:, k, lo:hi], y(k)[:, lo:hi], ALU.add).then_inc(to_act.sem, 1)

    ADA_GROUPS, ADA_FIRST = 2 * 6 * D // 512, 2 * D // 512
    ada_rows = [arena[:, T + 512 * q:T + 512 * q + 512] for q in range(2)]
    cs = small[:, 0:16].rearrange("p (s k) -> p k s", s=2)

    def ada_pe(pe):
        def products(g, q):
            for k in range(KD):
                slot = (pe.items + k // 2) % SLOTS
                if k % 2 == 0:
                    pe.wait_ge(landed[slot], 16)
                ins = M.matmul(psum[2 + q][0:2, :], cs[:, k, :], ring[slot][:, (k % 2) * 512:(k % 2) * 512 + 512],
                               start=(k == 0), stop=(k == KD - 1))
                if k % 2:
                    ins.then_inc(item_done.sem, 1)
            pe.items += 4

        def turn(g, q):
            pe.wait_ge(made_act)
            for i in range(4):
                at = g * 8 + 2 * i
                if isinstance(g, int):
                    out2 = psum[6 if g < ADA_FIRST else 7][:, at:at + 2]
                else:
                    out2 = psum[7][:, bass.ds(at, 2)]
                ins = M.matmul(out2, ada_rows[q][0:2, P * i:P * i + P], ident[0:2, 0:2], start=True, stop=True)
            return ins

        products(0, 0)
        for g in range(ADA_FIRST):
            products(g + 1, (g + 1) % 2)
            ins = turn(g, g % 2)
        ins.then_inc(prod.sem, 1)
        items, turns = pe.items, (ADA_GROUPS - 2 - ADA_FIRST) // 2
        with pe.repeat(turns, {landed[0]: 32, landed[1]: 32, landed[2]: 32, landed[3]: 32, made_act: 2}) as t:
            for q in range(2):
                products(None, 1 - q)
                turn(t * 2 + (q + ADA_FIRST), q)
        pe.items = items + 8 * turns
        products(ADA_GROUPS - 1, 1)
        turn(ADA_GROUPS - 2, 0)
        turn(ADA_GROUPS - 1, 1).then_inc(prod.sem, 1)

    def ada_act(act, groups):
        with act.repeat(groups // 2, {item_done: 8}):
            for q in range(2):
                act.wait_ge(item_done, 4)
                S.activation(ada_rows[q][0:2, :], psum[2 + q][0:2, :], ACT.Identity).then_inc(made_act.sem, 1)

    def ada_dve(dve, bank, lo, hi):
        dve.wait_ge(prod)
        link(dve, dve_step, V.tensor_tensor(mods[:, 2 * lo:2 * hi].rearrange("p (n s) -> p n s", s=2),
                                            bank[:, 2 * lo:2 * hi].rearrange("p (n s) -> p n s", s=2),
                                            cols("ada_b", lo, hi - lo).unsqueeze(2).to_broadcast([P, hi - lo, 2]),
                                            ALU.add))

    def modv_first_dve():
        mod = mods[:, 0:96].rearrange("p (i k s) -> p i k s", i=6, s=2)
        mv = modv[:, :].rearrange("p (i k s) -> p i k s", i=6, s=2)
        V.scalar_tensor_tensor(mv[:, 0], mod[:, 1], 1.0, cols("mix_pre", 0, 8).unsqueeze(2).to_broadcast([P, 8, 2]),
                               ALU.add, ALU.mult)
        return V.tensor_copy(mv[:, 1], mod[:, 0])

    def modv_dve(dve, layer):
        mod = mods[:, 96 * layer:96 * layer + 96].rearrange("p (i k s) -> p i k s", i=6, s=2)
        mv = modv[:, :].rearrange("p (i k s) -> p i k s", i=6, s=2)
        for a, pre, post in ((0, "mix_pre", "mix_post"), (3, "ffn_pre", "ffn_post")):
            wpre = cols(pre, 8 * layer, 8).unsqueeze(2).to_broadcast([P, 8, 2])
            wpost = cols(post, 8 * layer, 8).unsqueeze(2).to_broadcast([P, 8, 2])
            V.scalar_tensor_tensor(mv[:, a], mod[:, a + 1], 1.0, wpre, ALU.add, ALU.mult)
            V.tensor_copy(mv[:, a + 1], mod[:, a])
            ins = V.tensor_tensor(mv[:, a + 2], mod[:, a + 2], wpost, ALU.mult)
        return ins

    room = Room()
    take4 = lambda r: r.take(4 * T).rearrange("p (j t) -> p j t", j=4)
    uT, rT, vT, kkT, kT = (take4(room) for _ in range(5))
    kd0T = take4(room)
    kdT = [kd0T, kT]
    GT = [take4(room), take4(room)]
    bT = [take4(room), take4(room)]
    rest_at = room.at
    gT = h_all[:, 0:4 * T].rearrange("p (j t) -> p j t", j=4)
    yacc = h_all[:, 4 * T:8 * T].rearrange("p (n j v) -> p n j v", n=T // RC, v=RC)

    stage = Room(0, KD * T, x_all)
    tail = Room(rest_at)
    raw = [stage.take(T + 3), stage.take(T + 3)]
    lora = stage.take(3 * T).rearrange("p (j t) -> p j t", j=3)
    rtA = stage.take(T)
    vstat = stage.take(32)
    flat = lambda t: t.rearrange("p j t -> p (j t)")
    vtok = flat(kd0T).rearrange("p (n c) -> p n c", n=6)
    vsq = flat(GT[0]).rearrange("p (n c) -> p n c", n=6)
    wsT, bs_rep = flat(bT[1])[:, 0:512], flat(bT[1])[:, 512:1024]
    rcons = tail.take(16 * RC)
    order_mask = [rcons[:, 2 * RC * d:2 * RC * d + 2 * RC].rearrange("p (a t) -> p a t", a=2) for d in range(2)]
    level_mask = [[rcons[:, RC * (4 + 6 * d + lv):RC * (5 + 6 * d + lv)] for lv in range(6)] for d in range(2)]
    resets = tail.take(T)
    loraw = tail.take(1536)

    def raw_seg(p, seg, tap):
        at = (0 if seg[0] == 0 else CTX + 1) + tap
        return raw[p][:, at:at + seg[1]]

    def mixer_ab_in_pe(pe):
        block_starts["ab"] = pe.items
        pe.wait_ge(split_ready, 4)
        for j in range(4):
            landed[(pe.items + j) % SLOTS].skip(pe, 16)
        for t in range(6):
            if t >= 2:
                pe.wait_ge(room_pe)
            for k in range(KD):
                slot = (pe.items + k // 2) % SLOTS
                at = slice((k % 2) * 512, (k % 2) * 512 + 512)
                wh, wl = wh_ab[slot][:, at], ring_low[slot][:, at]
                xh, xl = part(hh_ab)(k, (t * P, P)), part(hlT)(k, (t * P, P))
                for x, w, first, last in ((xh, wh, k == 0, False), (xh, wl, False, False), (xl, wh, False, k == KD - 1)):
                    ins = M.matmul(psum[4 + t % 2][:, :], x, w, start=first, stop=last)
                if t == 5 and k % 2:
                    ins.then_inc(item_done.sem, 1)
            if t < 5:
                ins.then_inc(prod_act.sem, 1)
        pe.items += 4
        split_product_pe(pe, 19, wh_ab, part(hh_ab), part(hlT), BOTH)

    def mixer_ab_in_act(act):
        for t in range(6):
            if t < 5:
                act.wait_ge(prod_act)
            else:
                act.wait_ge(item_done, 4)
            ins = S.activation(vtok[:, t, :], psum[4 + t % 2][:, :], ACT.Gelu_apprx_tanh)
            if t < 4:
                ins.then_inc(room_pe.sem, 1)

        def plain(dst, func):
            def evict(i, p):
                for seg in BOTH:
                    ins = S.activation(dst(i)[:, seg[0]:seg[0] + seg[1]], bank_of(p, seg), func)
                return ins
            return evict

        tiles_act(act, 4, plain(lambda i: uT[:, i, :], ACT.Gelu_apprx_tanh))
        tiles_act(act, 1, plain(lambda i: lora[:, 0, :], ACT.Tanh))
        tiles_act(act, 1, plain(lambda i: lora[:, 1, :], ACT.Identity))
        tiles_act(act, 1, plain(lambda i: lora[:, 2, :], ACT.Sigmoid))
        for i in range(12):
            act.wait_ge(item_done)
            if i >= 2:
                act.wait_ge(room_dve)
            for seg in BOTH:
                ins = S.activation(raw_seg(i % 2, seg, 1), bank_of(act.tiles % 2, seg), ACT.Identity)
            ins.then_inc(tile_read.sem, 1)
            act.tiles += 1

    def mixer_ab_in_dve(dve):
        for p in range(2):
            for at in (0, CTX + 1, T + 2):
                ins = V.memset(raw[p][:, at:at + 1], 0.0)
        link(dve, dve_step, ins)
        tile_read.skip(dve, 7)
        for i in range(12):
            dve.wait_ge(tile_read)
            dst = (rT, kT, vT)[i // 4][:, i % 4, :]
            for seg in BOTH:
                ins = V.tensor_scalar(dst[:, seg[0]:seg[0] + seg[1]], raw_seg(i % 2, seg, 0), cols("b_shift", i), None,
                                ALU.mult)
            for tap in (1, 2):
                link(dve, dve_step, ins)
                for seg in BOTH:
                    y = dst[:, seg[0]:seg[0] + seg[1]]
                    ins = V.scalar_tensor_tensor(y, raw_seg(i % 2, seg, tap), cols("b_shift", 12 * tap + i), y,
                                                 ALU.mult, ALU.add)
            ins.then_inc(room_dve.sem, 1)

    def mixer_ab_load_sp(sp):
        sp.e.dma_start(rcons, A["rwkv_masks"][:, 0:16 * RC]).then_inc(extra_in.sem, 16)
        sp.e.dma_start(resets, A["rwkv_masks"][:, 16 * RC:16 * RC + T]).then_inc(extra_in.sem, 16)
        sp.e.dma_start(loraw, A["lora_w"]).then_inc(extra_in.sem, 16)
        sp.e.dma_start(wsT, A["a_wsT"]).then_inc(extra_in.sem, 16)
        sp.e.dma_start(bs_rep, A["a_bs"].partition_broadcast(P)).then_inc(extra_in.sem, 16)

    def spatial_pe(pe):
        loaded(pe, 5)
        pe.wait_ge(made)
        for g in range(4):
            if g >= 2:
                pe.wait_ge(group_read)
            for n in range(6):
                lat, ctxb = psum[2 * (g % 2)], psum[2 * (g % 2) + 1]
                dst = ctxb[:, P * n:P * n + P] if n < 2 else lat[:, P * (n - 2):P * (n - 2) + P]
                ins = M.matmul(dst, vtok[:, n, P * g:P * g + P], wsT[:, P * g:P * g + P], start=True, stop=True)
            ins.then_inc(prod.sem, 1)
        for j in range(4):
            pe.wait_ge(made)
            for seg in BOTH:
                ins = M.matmul(psum[4 + (seg[0] == 0)][:, 0:seg[1]], halves, raw[j % 2][:, seg[0]:seg[0] + seg[1]],
                               start=True, stop=True)
            ins.then_inc(sum_ready.sem, 1)

    def spatial_act(act):
        act.wait_ge(ms_ready)
        S.activation(vstat[:, 0:24], vstat[:, 0:24], ACT.Sqrt).then_inc(root_ready.sem, 1)
        for j in range(4):
            act.wait_ge(ms_ready)
            S.activation(rtA, rtA, ACT.Sqrt).then_inc(root_ready.sem, 1)

    def spatial_dve(dve):
        loaded(dve, 5)
        link(dve, dve_step, V.tensor_tensor(vsq, vtok, vtok, ALU.mult))
        groups = lambda t: t.rearrange("p n (g c) -> p (n g) c", g=4)
        link(dve, dve_step, V.tensor_reduce(vstat[:, 0:24], groups(vsq), AX, ALU.add))
        V.tensor_scalar(vstat[:, 0:24], vstat[:, 0:24], 1.0 / P, EPS, ALU.mult, ALU.add).then_inc(ms_ready.sem, 1)
        dve.wait_ge(root_ready)
        link(dve, dve_step, V.reciprocal(vstat[:, 0:24], vstat[:, 0:24]))
        V.tensor_tensor(groups(vtok), groups(vtok), vstat[:, 0:24].unsqueeze(2).to_broadcast([P, 24, P]),
                        ALU.mult).then_inc(made.sem, 1)
        for g in range(4):
            dve.wait_ge(prod)
            for seg in BOTH:
                n = seg[1] // P
                z = vsq_flat[:, seg[0]:seg[0] + seg[1]]
                ins = V.scalar_tensor_tensor(z.rearrange("p (n t) -> p n t", n=n),
                                             bank_of(g % 2, seg).rearrange("p (n t) -> p n t", n=n), cols("a_gv", g),
                                             bs_rep[:, P * g:P * g + P].unsqueeze(1).to_broadcast([P, n, P]),
                                             ALU.mult, ALU.add)
            link(dve, group_read, ins)
            link(dve, dve_step, V.tensor_tensor(uT[:, g, :], uT[:, g, :], vsq_flat[:, 0:T], ALU.mult))
        for j in range(4):
            link(dve, dve_step, V.tensor_scalar(kkT[:, j, :], kT[:, j, :], cols("b_kk", j), None, ALU.mult))
            V.tensor_tensor(raw[j % 2][:, 0:T], kkT[:, j, :], kkT[:, j, :], ALU.mult).then_inc(made.sem, 1)
            dve.wait_ge(sum_ready)
            for seg in BOTH:
                ins = V.tensor_scalar(rtA[:, seg[0]:seg[0] + seg[1]], psum[4 + (seg[0] == 0)][:, 0:seg[1]], 1e-12,
                                      None, ALU.max)
            ins.then_inc(ms_ready.sem, 1)
            dve.wait_ge(root_ready)
            link(dve, dve_step, V.reciprocal(rtA, rtA))
            link(dve, dve_step, V.tensor_tensor(kkT[:, j, :], kkT[:, j, :], rtA, ALU.mult))

    vsq_flat = flat(GT[0])

    LORA = [(0, 0, j) for j in range(4)] + [(0, 1, j) for j in range(4)] + \
           [(1, 0, j) for j in range(4)] + [(1, 1, j) for j in range(4)] + [(2, 0, j) for j in range(4)]

    def lora_pe(pe):
        for kind, d, j in LORA:
            rows = slice(64 * d, 64 * d + 64) if kind < 2 else slice(0, P)
            pe.wait_ge(tile_read)
            for seg in BOTH:
                ins = M.matmul(bank_of(pe.tiles % 2, seg), loraw[rows, 512 * kind + P * j:512 * kind + P * j + P],
                               lora[rows, kind, seg[0]:seg[0] + seg[1]], start=True, stop=True)
            ins.then_inc(prod_act.sem, 1)
            pe.tiles += 1

    def lora_act(act):
        for kind, d, j in LORA:
            act.wait_ge(prod_act)
            for seg in BOTH:
                src, a, b = bank_of(act.tiles % 2, seg), seg[0], seg[0] + seg[1]
                if kind == 2:
                    ins = S.activation(gT[:, j, a:b], src, ACT.Identity)
                elif kind == 0:
                    ins = S.activation(GT[d][:, j, a:b], src, ACT.Sigmoid, bias=cols("b_w0", 4 * d + j))
                else:
                    ins = S.activation(bT[d][:, j, a:b], src, ACT.Sigmoid, bias=cols("b_a0", 4 * d + j))
            ins.then_inc(tile_read.sem, 1)
            act.tiles += 1

    def lora_dve(dve):
        link(dve, dve_step, V.tensor_scalar(small[:, 48:52], cols("b_ka", 0, 4), -1.0, 1.0, ALU.mult, ALU.add))
        for i, (kind, d, j) in enumerate(LORA[:8]):
            dve.wait_ge(tile_read)
            s = GT[d][:, j, :]
            if d == 0:
                V.tensor_tensor_scan(s, resets, s, 0.0, ALU.mult, ALU.add)
            else:
                V.tensor_tensor_scan(s[:, ::-1], resets, s[:, ::-1], 0.0, ALU.mult, ALU.add)
        for kind, d, j in LORA[8:16]:
            dve.wait_ge(tile_read)
            a, k = bT[d][:, j, :], kT[:, j, :]
            link(dve, dve_step, V.tensor_scalar(raw[d][:, 0:T], a, cols("b_ka", j), small[:, 48 + j:49 + j],
                                                ALU.mult, ALU.add))
            V.tensor_tensor(a, a, kkT[:, j, :], ALU.mult)
            link(dve, dve_step, V.tensor_tensor(kdT[d][:, j, :], k, raw[d][:, 0:T], ALU.mult))
        tile_read.skip(dve, 4)

    NCH = T // RC
    scan_a, scan_b = Room(0, KD * T, x_all), Room(rest_at + 16 * RC)
    def scan_take(n):
        return (scan_a if scan_a.at + n <= scan_a.end else scan_b).take(n)
    q4 = lambda n: scan_take(n)
    KR = [q4(512).rearrange("p (j a t) -> p j a t", j=4, a=2) for _ in range(2)]
    SC = [[q4(512).rearrange("p (j a t) -> p j a t", j=4, a=2) for _ in range(2)] for _ in range(2)]
    XX = [q4(512).rearrange("p (a j t) -> p a j t", a=2, j=4) for _ in range(2)]
    TOK = [q4(768).rearrange("p (a j t) -> p a j t", a=3, j=4) for _ in range(2)]
    PM, RH, ST = ([q4(256).rearrange("p (j t) -> p j t", j=4) for _ in range(2)] for _ in range(3))
    NSA = RH
    LM = [[q4(256).rearrange("p (j t) -> p j t", j=4) for _ in range(2)] for _ in range(2)]
    EM = [q4(260).rearrange("p (j t) -> p j t", j=4) for _ in range(2)]
    PCOL = [q4(4) for _ in range(2)]
    HALF = (slice(0, 64), slice(64, 128))

    def chunk_of(d, i):
        return i if d == 0 else (3 - i if i < 4 else 15 - i)

    def four(bank, at=0):
        return bank[:, at:at + 256].rearrange("p (j t) -> p j t", j=4)

    def each_head(out4, lhs4, rhs4, start=True, stop=True):
        for j in range(4):
            for h in HALF:
                ins = M.matmul(out4(j)[h], lhs4(j)[h], rhs4(j)[h], start=start, stop=stop)
        return ins

    def rwkv_pe(pe):
        B = [[psum[4 * d + i] for i in range(4)] for d in range(2)]
        for i in range(NCH):
            for d in range(2):
                n = chunk_of(d, i)
                pe.wait_ge(made)
                for a in range(2):
                    dst = B[d][a][:, :].rearrange("p (j a t) -> p j a t", j=4, a=2)
                    ins = each_head(lambda j: dst[:, j], lambda j: XX[d][:, a, j, :], lambda j: KR[d][:, j])
                ins.then_inc(prod.sem, 1)
            for lv in range(1, 6):
                for d in range(2):
                    pe.wait_ge(made)
                    p = four(B[d][0])
                    each_head(lambda j: p[:, j, :], lambda j: LM[d][lv % 2][:, j, :],
                              lambda j: XX[d][:, 0, j, :]).then_inc(prod_act.sem, 1)
                for d in range(2):
                    pe.wait_ge(made_act)
                    dx, dt = four(B[d][2]), four(B[d][1], 256)
                    if lv < 5:
                        ins = each_head(lambda j: dx[:, j, :], lambda j: XX[d][:, 1, j, :], lambda j: PM[d][:, j, :])
                    else:
                        ins = each_head(lambda j: dt[:, j, :], lambda j: PM[d][:, j, :], lambda j: XX[d][:, 1, j, :])
                    ins.then_inc(prod.sem, 1)
            for d in range(2):
                p = four(B[d][2])
                for j in range(4):
                    for h in HALF:
                        M.matmul(p[h, j, :], KR[d][h, j, 0, :], ST[d][h, j, :], start=True, stop=False)
                    for h in HALF:
                        ins = M.matmul(p[h, j, :], SC[d][1][h, j, 0, :], TOK[d][h, 0, j, :], start=False, stop=True)
                ins.then_inc(prod_act.sem, 1)
            for d in range(2):
                pe.wait_ge(made)
                pe.wait_ge(made_act)
                p = four(B[d][2], 256)
                each_head(lambda j: p[:, j, :], lambda j: XX[d][:, 1, j, :], lambda j: RH[d][:, j, :])\
                    .then_inc(prod_act.sem, 1)
            for d in range(2):
                pe.wait_ge(made_act)
                s, y = four(B[d][3]), four(B[d][3], 256)
                for j in range(4):
                    for out, lhs, rhs, first, last in (
                            (y, KR[d][:, j, 1, :], ST[d][:, j, :], True, False),
                            (y, SC[d][1][:, j, 1, :], TOK[d][:, 0, j, :], False, False),
                            (y, SC[d][0][:, j, 1, :], NSA[d][:, j, :], False, True),
                            (s, TOK[d][:, 1, j, :], TOK[d][:, 0, j, :], True, False),
                            (s, TOK[d][:, 2, j, :], NSA[d][:, j, :], False, True)):
                        for h in HALF:
                            ins = M.matmul(out[h, j, :], lhs[h], rhs[h], start=first, stop=last)
                ins.then_inc(prod.sem, 1)

    def rwkv_act(act):
        B = [[psum[4 * d + i] for i in range(4)] for d in range(2)]
        for i in range(NCH):
            for d in range(2):
                n = chunk_of(d, i)
                if i:
                    act.wait_ge(step_through)
                g = GT[d][:, :, n * RC:(n + 1) * RC]
                S.activation(EM[d][:, :, 1 - d:65 - d], g, ACT.Exp, scale=-RDECAY)
                S.activation(PM[d][:, :, :], g, ACT.Exp, scale=RDECAY).then_inc(to_dve.sem, 1)
            for lv in range(1, 6):
                for d in range(2):
                    act.wait_ge(prod_act)
                    S.activation(PM[d][:, :, :], four(B[d][0]), ACT.Identity).then_inc(made_act.sem, 1)
            for d in range(2):
                act.wait_ge(prod_act)
                S.activation(RH[d][:, :, :], four(B[d][2]), ACT.Identity).then_inc(made_act.sem, 1)
            for d in range(2):
                act.wait_ge(prod_act)
                S.activation(NSA[d][:, :, :], four(B[d][2], 256), ACT.Identity, scale=-1.0).then_inc(made_act.sem, 1)

    def turn_diagonal(dst, src):
        for q in range(4):
            rows, at = slice(32 * q, 32 * q + 32), slice(32 * (q % 2), 32 * (q % 2) + 32)
            ins = V.transpose(dst[rows, :, at], src[rows, :, at])
        return ins

    def turn_heads(dst, src):
        for h in range(2):
            for a in range(2):
                for b in range(2):
                    ra, rb = slice(64 * h + 32 * a, 64 * h + 32 * a + 32), slice(64 * h + 32 * b, 64 * h + 32 * b + 32)
                    ins = V.transpose(dst[rb, :, 32 * a:32 * a + 32], src[ra, :, 32 * b:32 * b + 32])
        return ins

    def rwkv_dve(dve):
        B = [[psum[4 * d + i] for i in range(4)] for d in range(2)]
        eye = ident64.unsqueeze(1).to_broadcast([P, 4, RC])
        for d in range(2):
            V.memset(EM[d][:, :, 64 * d:64 * d + 1], 1.0)
            link(dve, dve_step, V.memset(ST[d], 0.0))

        def start(i, d):
            n = chunk_of(d, i)
            at = slice(n * RC, (n + 1) * RC)
            dve.wait_ge(to_dve)
            V.tensor_tensor(KR[d][:, :, 1, :], rT[:, :, at], EM[d][:, :, 1 - d:65 - d], ALU.mult)
            V.tensor_tensor(KR[d][:, :, 0, :], kkT[:, :, at], EM[d][:, :, d:64 + d], ALU.mult)
            V.tensor_tensor(XX[d][:, 0], bT[d][:, :, at], PM[d][:, :, :], ALU.mult)
            V.tensor_copy(PCOL[d], EM[d][:, :, 64 - 64 * d])
            link(dve, dve_step, V.tensor_tensor(XX[d][:, 1], kdT[d][:, :, at], PM[d][:, :, :], ALU.mult))
            dve.e.sem_inc(made.sem, 1)
            turn_heads(TOK[d][:, 1], XX[d][:, 1])
            turn_heads(TOK[d][:, 2], XX[d][:, 0])

        start(0, 0)
        start(0, 1)
        for i in range(NCH):
            for d in range(2):
                dve.wait_ge(prod)
                level = lambda lv: level_mask[d][lv].unsqueeze(1).to_broadcast([P, 4, RC])
                mask = order_mask[d].unsqueeze(1).to_broadcast([P, 4, 2, RC])
                banks = [B[d][a][:, :].rearrange("p (j a t) -> p j a t", j=4, a=2) for a in range(2)]
                link(dve, dve_step, V.tensor_tensor(SC[d][0], banks[0], mask, ALU.mult))
                link(dve, dve_step, V.tensor_tensor(LM[d][0], SC[d][0][:, :, 0, :], level(0), ALU.mult))
                V.memset(XX[d][:, 0], 0.0)
                V.tensor_tensor(LM[d][1], SC[d][0][:, :, 0, :], level(1), ALU.mult)
                link(dve, dve_step, V.scalar_tensor_tensor(XX[d][:, 1], LM[d][0], -1.0, eye, ALU.mult, ALU.add))
                turn_diagonal(XX[d][:, 0], XX[d][:, 1]).then_inc(made.sem, 1)
                V.tensor_tensor(SC[d][1], banks[1], mask, ALU.mult)
            for lv in range(1, 6):
                for d in range(2):
                    level = lambda lv: level_mask[d][lv].unsqueeze(1).to_broadcast([P, 4, RC])
                    if lv < 5:
                        V.tensor_tensor(LM[d][(lv + 1) % 2], SC[d][0][:, :, 0, :], level(lv + 1), ALU.mult)
                    dve.wait_ge(prod)
                    dx, dt = four(B[d][2]), four(B[d][1], 256)
                    if lv < 5:
                        link(dve, dve_step, V.tensor_tensor(XX[d][:, 0], XX[d][:, 0], dx, ALU.subtract))
                        turn_diagonal(XX[d][:, 1], XX[d][:, 0]).then_inc(made.sem, 1)
                        if lv == 2:
                            n = chunk_of(d, i)
                            turn_heads(TOK[d][:, 0], vT[:, :, n * RC:(n + 1) * RC])
                    else:
                        V.tensor_tensor(XX[d][:, 1], XX[d][:, 1], dt, ALU.subtract).then_inc(made.sem, 1)
            for d in range(2):
                n = chunk_of(d, i)
                dve.wait_ge(prod)
                link(dve, dve_step, V.tensor_tensor(ST[d], ST[d], four(B[d][3]), ALU.add))
                V.tensor_tensor(ST[d], ST[d], PCOL[d].unsqueeze(2).to_broadcast([P, 4, RC]), ALU.mult)
                y = four(B[d][3], 256)
                if n not in visited:
                    visited.add(n)
                    ins = V.tensor_copy(yacc[:, n], y)
                else:
                    ins = V.tensor_tensor(yacc[:, n], yacc[:, n], y, ALU.add)
                link(dve, step_through, ins)
                if i + 1 < NCH:
                    start(i + 1, d)

    visited = set()

    def rwkv_out_pe(pe):
        pe.wait_ge(made)
        for j in range(4):
            pe.wait_ge(tile_read)
            for n in range(NCH):
                bank, at = (psum[2 * (j % 2) + 1], n * RC) if n < 4 else (psum[2 * (j % 2)], (n - 4) * RC)
                for h in HALF:
                    ins = M.matmul(bank[h, at:at + RC], yacc[h, n, j, :], ident64[h], start=True, stop=True)
            ins.then_inc(prod_act.sem, 1)
            if j:
                pe.wait_ge(bonus_read)
            for seg in BOTH:
                ins = M.matmul(psum[4 + (seg[0] == 0)][:, 0:seg[1]], halves, bT[0][:, j, seg[0]:seg[0] + seg[1]],
                               start=True, stop=True)
            ins.then_inc(prod.sem, 1)
        bonus_read.skip(pe, 1)

    def rwkv_out_act(act):
        act.wait_ge(ms_ready)
        S.activation(ystat[:, 48:96], ystat[:, 48:96], ACT.Sqrt).then_inc(root_ready.sem, 1)
        for j in range(4):
            act.wait_ge(prod_act)
            for seg in BOTH:
                ins = S.activation(GT[1][:, j, seg[0]:seg[0] + seg[1]], bank_of(j % 2, seg), ACT.Identity,
                                   bias=cols("b_ln_b", j), scale=cols("b_ln_g", j))
            ins.then_inc(tile_read.sem, 1)

    def rwkv_out_dve(dve):
        y = yacc.rearrange("p n j v -> p (n j) v")
        sq = flat(GT[0]).rearrange("p (m v) -> p m v", v=RC)
        for j in range(4):
            ins = V.tensor_tensor(bT[0][:, j, :], kdT[0][:, j, :], kdT[1][:, j, :], ALU.add)
        link(dve, dve_step, ins)
        for j in range(4):
            V.scalar_tensor_tensor(bT[0][:, j, :], bT[0][:, j, :], cols("b_rk", j), rT[:, j, :], ALU.mult, ALU.mult)
        link(dve, dve_step, V.tensor_reduce(ystat[:, 0:48], y, AX, ALU.add))
        link(dve, dve_step, V.tensor_scalar(ystat[:, 0:48], ystat[:, 0:48], 1.0 / RC, None, ALU.mult))
        spread = lambda a: ystat[:, a:a + 48].unsqueeze(2).to_broadcast([P, 48, RC])
        link(dve, dve_step, V.tensor_tensor(y, y, spread(0), ALU.subtract))
        link(dve, dve_step, V.tensor_tensor(sq, y, y, ALU.mult))
        link(dve, dve_step, V.tensor_reduce(ystat[:, 48:96], sq, AX, ALU.add))
        V.tensor_scalar(ystat[:, 48:96], ystat[:, 48:96], 1.0 / RC, LN_EPS, ALU.mult, ALU.add).then_inc(ms_ready.sem, 1)
        dve.wait_ge(root_ready)
        link(dve, dve_step, V.reciprocal(ystat[:, 48:96], ystat[:, 48:96]))
        V.tensor_tensor(y, y, spread(48), ALU.mult).then_inc(made.sem, 1)
        for j in range(4):
            dve.wait_ge(prod)
            dst = bT[1][:, j, :]
            for seg in BOTH:
                a, b = seg[0], seg[0] + seg[1]
                ins = V.tensor_tensor(dst[:, a:b], psum[4 + (seg[0] == 0)][:, 0:seg[1]], vT[:, j, a:b], ALU.mult)
            link(dve, bonus_read, ins)
            dve.wait_ge(tile_read)
            link(dve, dve_step, V.tensor_tensor(dst, dst, GT[1][:, j, :], ALU.add))
            V.tensor_tensor(dst, dst, gT[:, j, :], ALU.mult)

    out_tail = Room(rest_at + 16 * RC)
    ystat = out_tail.take(96)
    rtB = out_tail.take(T)
    yT_l0 = lambda k: (rT, vT)[k // 4][:, k % 4, :]
    sq_l0 = lambda k: GT[k // 4][:, k % 4, :]
    mix_in = lambda k, seg: (uT, bT[1])[k // 4][:, k % 4, seg[0]:seg[0] + seg[1]]

    def keep(dst, segs, func=ACT.Identity):
        def evict(i, p):
            for seg in segs:
                ins = S.activation(dst(i)[:, seg[0]:seg[0] + seg[1]], bank_of(p, seg), func)
            return ins
        return evict

    def keep_squared(dst, sq, segs):
        def evict(i, p):
            for seg in segs:
                ins = S.activation(sq(i)[:, seg[0]:seg[0] + seg[1]], bank_of(p, seg), ACT.Square)
            ins.then_inc(sq_ready.sem, 1)
            return keep(dst, segs)(i, p)
        return evict

    def root_act(act, segs, rt):
        lo, hi = segs[0][0], segs[-1][0] + segs[-1][1]
        act.wait_ge(ms_ready)
        S.activation(rt[:, lo:hi], rt[:, lo:hi], ACT.Sqrt).then_inc(root_ready.sem, 1)

    froom = Room()
    hf = froom.take(KF * T).rearrange("p (k t) -> p k t", k=KF)
    grid = [froom.take((ROWS + 2) * (COLS + 2)).rearrange("p (r c) -> p r c", c=COLS + 2) for _ in range(2)]
    line = [froom.take(CTX + 2) for _ in range(2)]
    bside = [froom.take(T) for _ in range(2)]
    conv = [froom.take(T) for _ in range(2)]
    froom.at = HH_FFN
    fsq = froom.take(KD * T).rearrange("p (k t) -> p k t", k=KD)
    frt = froom.take(T)
    conv_ready, gelu_ready, pair_free = signal("conv_ready"), signal("gelu_ready"), signal("pair_free")

    assert froom.at <= WH_FFN

    def ffn_pe(pe, layer, segs):
        block_starts["ffn", layer] = pe.items
        split_product_pe(pe, 2 * KF, wh_ffn, part(hh_ffn), part(hlT), segs)

    def ffn_down_pe(pe, layer, segs):
        rhs = lambda k, seg: hf[:, k, seg[0]:seg[0] + seg[1]]
        pe.e.wait_ge(pair_free.sem, layer * (KF + 2) + 2 + 16)
        product_pe(pe, 1, rhs, segs, parts=(8, 8, 6), last_part=made)
        product_pe(pe, KD - 1, rhs, segs, parts=(8, 8, 6))

    def grid_at(q, dy, dx):
        return grid[q][:, dy:dy + ROWS, dx:dx + COLS]

    def ffn_act(act, layer, segs):
        lo, hi = segs[0][0], segs[-1][0] + segs[-1][1]
        with act.repeat(KF // 2, {item_done: 4, conv_ready: 2, pair_free: 2}) as t:
            for q in range(2):
                act.wait_ge(item_done)
                act.wait_ge(pair_free)
                par = (act.tiles + 2 * q) % 2
                for seg in segs:
                    if seg[0]:
                        ins = S.activation(grid_at(q, 1, 1), bank_of(par, seg).rearrange("p (r c) -> p r c", c=COLS),
                                           ACT.Identity)
                    else:
                        ins = S.activation(line[q][:, 1:1 + CTX], bank_of(par, seg), ACT.Identity)
                ins.then_inc(tile_read.sem, 1)
                act.wait_ge(item_done)
                for seg in segs:
                    ins = S.activation(bside[q][:, seg[0]:seg[0] + seg[1]], bank_of(1 - par, seg), ACT.Identity)
                ins.then_inc(tile_read.sem, 1)
                act.wait_ge(conv_ready)
                S.activation(conv[q][:, lo:hi], conv[q][:, lo:hi], ACT.Gelu_apprx_tanh,
                             bias=vec[:, bass.ds(t * 2 + (COL["ffn_conv_b"] + KF * layer + q), 1)])\
                    .then_inc(gelu_ready.sem, 1)
        act.tiles += 2 * KF
        act.wait_ge(pair_free, 2)

    def ffn_dve(dve, layer, segs):
        for q in range(2):
            V.memset(grid[q], 0.0)
            link(dve, dve_step, V.memset(line[q], 0.0))
        dve.e.sem_inc(pair_free.sem, 2)
        lo, hi = segs[0][0], segs[-1][0] + segs[-1][1]
        taps = [(dy, dx) for dy in (1, 0, 2) for dx in (0, 1, 2)]
        with dve.repeat(KF // 2, {tile_read: 4, dve_step: 18, gelu_ready: 2}) as t:
            for q in range(2):
                w = lambda dy, dx: vec[:, bass.ds(t * 2 + (COL["ffn_conv"] + KF * (9 * layer + 3 * dy + dx) + q), 1)]
                dve.wait_ge(tile_read, 2)
                for n, (dy, dx) in enumerate(taps):
                    for seg in segs:
                        y = conv[q][:, seg[0]:seg[0] + seg[1]]
                        if seg[0]:
                            y, a = y.rearrange("p (r c) -> p r c", c=COLS), grid_at(q, dy, dx)
                        elif dy == 1:
                            a = line[q][:, dx:dx + CTX]
                        else:
                            continue
                        if n == 0:
                            ins = V.tensor_scalar(y, a, w(dy, dx), None, ALU.mult)
                        else:
                            ins = V.scalar_tensor_tensor(y, a, w(dy, dx), y, ALU.mult, ALU.add)
                    if n < 8:
                        link(dve, dve_step, ins)
                    else:
                        ins.then_inc(conv_ready.sem, 1)
                dve.wait_ge(gelu_ready)
                k = hf[:, bass.ds(t * 2 + q, 1), lo:hi].rearrange("p a t -> p (a t)")
                link(dve, dve_step, V.tensor_tensor(k, conv[q][:, lo:hi], bside[q][:, lo:hi], ALU.mult))
                dve.e.sem_inc(pair_free.sem, 1)

    NC6 = T // MC
    NL = LAT // MC
    mroom = Room()
    tall = lambda r, w: r.take(KD * w).rearrange("p (k t) -> p k t", k=KD)
    xmT, xcT, zT, kqT = tall(mroom, T), tall(mroom, T), tall(mroom, LAT), tall(mroom, LAT)
    vtk = mroom.take(NC6 * D).rearrange("p (c f) -> p c f", c=NC6)
    hacc = mroom.take(NL * D).rearrange("p (c f) -> p c f", c=NL)
    ktk = h_all[:, :].rearrange("p (c f) -> p c f", c=NC6)
    mmask = mroom.take(5 * P)
    incl128 = [mmask[:, 0:P], mmask[:, P:2 * P]]
    neg128 = [mmask[:, 2 * P:3 * P], mmask[:, 3 * P:4 * P]]
    diag4 = mmask[:, 4 * P:5 * P]
    gcols = mroom.take(1)
    bdw = mroom.take(96).rearrange("p (a n o) -> p a n o", a=3, n=KD)
    ctk = mroom.take(4 * 6 * 8).rearrange("p (c q d h) -> p c q d h", c=6, q=4, d=2)
    csb = mroom.take(48).rearrange("p (u c) -> p u c", c=6)
    nvec = mroom.take(16)
    mrow = mroom.take(24)
    dens = [mroom.take(4), mroom.take(4)]
    mstat = mroom.take(16)
    mrt = mroom.take(T)
    bdm = [mroom.take(3 * P) for _ in range(2)]
    rows = Room(0, NL * D, flat(hacc))
    RA, RB, RX, RW, RK = (rows.take(T) for _ in range(5))
    RM = mrt
    eb, tb, stb = ([xmT[:, i, P * j:P * j + P] for j in range(2)] for i in range(3))
    t1b = [xmT[:, 3 + j, 0:256] for j in range(2)]
    kwb = [bdm[0][:, 0:256], bdm[1][:, 0:256]]

    def state(d, h):
        return (xT if d == 0 else xcT)[:, 2 * h:2 * h + 2, 0:256]

    def mlstm_load_sp(sp):
        for dst, src in ((mmask[:, 0:4 * P], A["delta_masks"][:, 0:4 * P]), (diag4, A["delta_masks"][:, 18 * P:19 * P]),
                         (gcols, A["gate_cols"]), (bdw.rearrange("p a n o -> p (a n o)"), A["qkv_blocks"])):
            sp.e.dma_start(dst, src).then_inc(extra_in.sem, 16)

    def mlstm_in_pe(pe):
        block_starts["mlstm"] = pe.items
        for n, segs in ((8, BOTH), (8, LATENT), (1, BOTH)):
            split_product_pe(pe, n, wh_m, part(hh_m), part(hlT), segs)

    def mlstm_in_act(act):
        def evict(i, p):
            for seg in BOTH:
                ins = S.activation(xmT[:, i, seg[0]:seg[0] + seg[1]], bank_of(p, seg), ACT.Identity)
            return ins
        tiles_act(act, 8, evict, loop=False)
        for k in range(KD):
            act.wait_ge(to_act)
            S.activation(xcT[:, k, :], xcT[:, k, :], ACT.Silu, bias=cols("c_conv_b", k))
        tiles_act(act, 8, lambda i, p: S.activation(zT[:, i, :], bank_of(p, LATENT[0]), ACT.Sigmoid), loop=False)
        loaded(act, 9)
        def gates(i, p):
            for seg in BOTH:
                a, b = seg[0], seg[0] + seg[1]
                S.activation(RA[0:64, a:b], bank_of(p, seg)[0:64], ACT.Identity, bias=gcols[0:64, 0:1])
                ins = S.activation(RX[64:128, a:b], bank_of(p, seg)[64:128], ACT.Identity, bias=gcols[64:128, 0:1])
            return ins
        tiles_act(act, 1, gates)

    def shift3_dve(dve, src, dst, w, segs, step):
        for seg in segs:
            a, b = seg[0], seg[0] + seg[1]
            ins = V.tensor_scalar(dst[:, a:b], src[:, a:b], w(1), None, ALU.mult)
        link(dve, step, ins)
        for seg in segs:
            a, b = seg[0], seg[0] + seg[1]
            ins = V.scalar_tensor_tensor(dst[:, a + 1:b], src[:, a:b - 1], w(0), dst[:, a + 1:b], ALU.mult, ALU.add)
        link(dve, step, ins)
        for seg in segs:
            a, b = seg[0], seg[0] + seg[1]
            ins = V.scalar_tensor_tensor(dst[:, a:b - 1], src[:, a + 1:b], w(2), dst[:, a:b - 1], ALU.mult, ALU.add)
        return ins

    def mlstm_in_dve(dve):
        for k in range(KD):
            dve.wait_ge(tile_read)
            shift3_dve(dve, xmT[:, k, :], xcT[:, k, :], lambda tap: cols("c_conv", 8 * tap + k), BOTH, dve_step)\
                .then_inc(to_act.sem, 1)
        tile_read.skip(dve, 9)

    def mlstm_mid_pe(pe):
        for n in range(KD):
            pe.wait_ge(made)
            w = bdm[n % 2]
            for src, m in ((xmT, 2), (xcT, 1)):
                pe.wait_ge(tile_read)
                for c in range(NC6):
                    p = pe.tiles % 2
                    dst = psum[2 * p + 1][:, P * c:P * c + P] if c < 2 else psum[2 * p][:, P * (c - 2):P * (c - 1)]
                    ins = M.matmul(dst, src[:, n, P * c:P * c + P], w[:, P * m:P * m + P], start=True, stop=True)
                ins.then_inc(prod_act.sem, 1)
                pe.tiles += 1
            pe.wait_ge(tile_read)
            p = pe.tiles % 2
            for m in range(2):
                ins = M.matmul(psum[2 * p + m][:, :], w[:, P * m:P * m + P], xcT[:, n, CTX:T], start=True, stop=True)
            ins.then_inc(prod_act.sem, 1)
            pe.tiles += 1
        pe.wait_ge(made)
        pe.wait_ge(made_act)
        for c in range(NC6):
            for i, r in enumerate((RA, RW, RX, RK)):
                dst = psum[6][:, 32 * c + 8 * i:32 * c + 8 * i + 8].rearrange("p (d h) -> p d h", d=2)
                M.matmul(dst, r[0:64, P * c:P * c + P], ident[0:64, 0:64].rearrange("p (d r) -> p d r", d=2)[:, :, 0:4],
                         start=True, stop=True)
        for u in range(8):
            row = 32 * (u // 4) + u % 4
            ins = M.matmul(psum[7][:, 6 * u:6 * u + 6], ident[0:64, row:row + 1].to_broadcast([64, P]),
                           mrow[0:64, 12:18], start=True, stop=True)
        ins.then_inc(prod.sem, 1)

    def mlstm_mid_act(act):
        r = slice(0, 64)
        act.wait_ge(to_act)
        link(act, act_step, S.activation(RW[r, :], RX[r, :], ACT.Abs))
        S.activation(RW[r, :], RW[r, :], ACT.Exp, scale=-1.0).then_inc(to_dve.sem, 1)
        act.wait_ge(to_act)
        S.activation(RW[r, :], RW[r, :], ACT.Ln).then_inc(to_dve.sem, 1)
        for n in range(KD):
            for what, scale in (("v", 1.0), ("k", C_SCALE)):
                act.wait_ge(prod_act)
                p, dst = act.tiles % 2, vtk if what == "v" else ktk
                S.activation(dst[:, 0:2, P * n:P * n + P], psum[2 * p + 1][:, 0:256].rearrange("p (c f) -> p c f", c=2),
                             ACT.Identity, scale=scale)
                S.activation(dst[:, 2:6, P * n:P * n + P], psum[2 * p][:, :].rearrange("p (c f) -> p c f", c=4),
                             ACT.Identity, scale=scale).then_inc(tile_read.sem, 1)
                act.tiles += 1
            act.wait_ge(prod_act)
            p = act.tiles % 2
            S.activation(qstage(n), psum[2 * p][:, :], ACT.Identity)
            S.activation(kqT[:, n, :], psum[2 * p + 1][:, :], ACT.Identity, scale=C_SCALE).then_inc(tile_read.sem, 1)
            act.tiles += 1
        act.wait_ge(to_act)
        S.activation(RW[r, :], RW[r, :], ACT.Exp, scale=-1.0)
        S.activation(RX[r, :], RX[r, :], ACT.Exp, scale=-1.0)
        S.activation(mrow[r, 12:18], mrow[r, 12:18], ACT.Exp, scale=-1.0)
        S.activation(RK[r, :], RK[r, :], ACT.Exp).then_inc(made_act.sem, 1)

    C_SCALE = 1.0 / 16.0
    def qstage(n):
        return xmT[:, n, CTX:T]

    def mlstm_mid_dve(dve):
        r = slice(0, 64)
        loaded(dve, 9)
        V.tensor_copy(RX[r, :], RX[64:128, :]).then_inc(to_act.sem, 1)
        V.memset(mrow[r, 0:24], 0.0)
        V.memset(RM[r, :], 1.0)
        for h in range(4):
            V.memset(state(0, h), 0.0)
        link(dve, dve_step, V.memset(nvec, 0.0))
        def weights(n):
            for a in range(3):
                ins = V.tensor_tensor(bdm[n % 2][:, P * a:P * a + P].rearrange("p (g o) -> p g o", o=4),
                                      bdw[:, a, n, :].unsqueeze(1).to_broadcast([P, 32, 4]),
                                      diag4.rearrange("p (g o) -> p g o", o=4), ALU.mult)
            ins.then_inc(made.sem, 1)
        weights(0)
        weights(1)
        dve.wait_ge(to_dve)
        V.tensor_scalar(RW[r, :], RW[r, :], 1.0, None, ALU.add).then_inc(to_act.sem, 1)
        dve.wait_ge(to_dve)
        link(dve, dve_step, V.scalar_tensor_tensor(RB[r, :], RX[r, :], 0.0, RW[r, :], ALU.min, ALU.subtract))
        for c in range(NC6):
            for d, q in enumerate((slice(0, 32), slice(32, 64))):
                s = RB[q, P * c:P * c + P]
                o = RM[q, 0:P]
                if d:
                    s = s[:, ::-1]
                ins = V.tensor_tensor_scan(s, o, s, 0.0, ALU.mult, ALU.add)
        link(dve, dve_step, ins)
        link(dve, dve_step, V.tensor_tensor(RA[r, :], RA[r, :], RB[r, :], ALU.subtract))
        for i in range(NC6):
            for d, q in enumerate((slice(0, 32), slice(32, 64))):
                c = mchunk(d, i)
                src, dst = RA[q, P * c:P * c + P], RK[q, P * c:P * c + P]
                if d:
                    src, dst = src[:, ::-1], dst[:, ::-1]
                end = P * c + (0 if d else P - 1)
                link(dve, dve_step, V.tensor_tensor_scan(dst, RM[q, 0:P], src, mrow[q, c:c + 1], ALU.mult, ALU.max))
                link(dve, dve_step, V.tensor_copy(mrow[q, 6 + c:7 + c], RK[q, end:end + 1]))
                if i < NC6 - 1:
                    nx = mchunk(d, i + 1)
                    link(dve, dve_step, V.tensor_tensor(mrow[q, nx:nx + 1], RB[q, end:end + 1], RK[q, end:end + 1],
                                                        ALU.add))
        for n in range(2, KD):
            dve.wait_ge(tile_read, 3)
            weights(n)
        dve.wait_ge(tile_read, 6)
        for h in range(4):
            V.memset(state(1, h), 0.0)
        chunks = lambda t: t[r, :].rearrange("p (c t) -> p c t", c=NC6)
        per = lambda at: mrow[r, at:at + 6].unsqueeze(2).to_broadcast([64, NC6, P])
        link(dve, dve_step, V.tensor_tensor(chunks(RW), chunks(RK), per(0), ALU.subtract))
        link(dve, dve_step, V.tensor_tensor(RX[r, :], RB[r, :], RK[r, :], ALU.add))
        link(dve, dve_step, V.tensor_tensor(mrow[r, 12:18], mrow[r, 6:12], mrow[r, 0:6], ALU.subtract))
        link(dve, dve_step, V.tensor_copy(RM[r, :], RK[r, :]))
        V.tensor_tensor(chunks(RK), chunks(RA), per(6), ALU.subtract).then_inc(to_act.sem, 1)
        V.engine_nop().then_inc(made.sem, 1)
        dve.wait_ge(prod)
        V.tensor_copy(ctk.rearrange("p c q d h -> p (c q d h)"), psum[6][:, 0:192])
        V.tensor_copy(csb.rearrange("p u c -> p (u c)"), psum[7][:, 0:48])

    def mchunk(d, i):
        return i if d == 0 else (1 - i if i < 2 else 7 - i)

    UNITS = [(i, d, h) for i in range(NC6) for d in range(2) for h in range(4)]

    def mlstm_scan_pe(pe):
        def first(u):
            i, d, h = UNITS[u]
            c, b = mchunk(d, i), psum[4 * (u % 2)]
            if c < 2:
                return
            row = 32 * d + h
            M.matmul(b[:, P:2 * P], ident[0:64, row:row + 1].to_broadcast([64, P]), RM[0:64, P * c:P * c + P],
                     start=True, stop=True)
            for a in range(2):
                ins = M.matmul(b[:, 0:P], kqT[:, 2 * h + a, P * (c - 2):P * (c - 1)], q_at(2 * h + a, c),
                               start=(a == 0), stop=(a == 1))
            ins.then_inc(prod.sem, 1)

        def second(u):
            i, d, h = UNITS[u]
            c, b = mchunk(d, i), psum[4 * (u % 2):4 * (u % 2) + 4]
            if u >= 2:
                pe.wait_ge(unit_read)
            pe.wait_ge(made_act)
            v, st = vtk[:, c, 256 * h:256 * h + 256], state(d, h)
            if c >= 2:
                pe.wait_ge(made)
                M.matmul(b[1][:, 0:256], stb[u % 2], v, start=True, stop=True)
                M.matmul(b[3][:, 0:1], stb[u % 2], ones[:, 0:1], start=True, stop=True)
                for a in range(2):
                    M.matmul(b[1][:, 256:512], q_at(2 * h + a, c), st[:, a, :], start=(a == 0), stop=(a == 1))
                for a in range(2):
                    M.matmul(b[3][:, 1:2], q_at(2 * h + a, c), nvec[:, 2 * (4 * d + h) + a:2 * (4 * d + h) + a + 1],
                             start=(a == 0), stop=(a == 1))
            for a in range(2):
                M.matmul(b[2][:, 256 * a:256 * a + 256], kwb[u % 2][:, P * a:P * a + P], v, start=True, stop=True)
            for a in range(2):
                ins = M.matmul(b[3][:, 2 + a:3 + a], kwb[u % 2][:, P * a:P * a + P], ones[:, 0:1], start=True, stop=True)
            ins.then_inc(prod.sem, 1)

        for u in range(len(UNITS) + 1):
            if u < len(UNITS):
                first(u)
            if u:
                second(u - 1)

    def q_at(n, c):
        return xmT[:, n, P * c:P * c + P]

    def mlstm_scan_act(act):
        def first(u):
            i, d, h = UNITS[u]
            c = mchunk(d, i)
            if u >= 2:
                act.wait_ge(unit_read)
            S.activation(kwb[u % 2], ktk[:, c, 256 * h:256 * h + 256], ACT.Identity, scale=ctk[:, c, 3, d, h:h + 1])\
                .then_inc(made_act.sem, 1)
            if c >= 2:
                act.wait_ge(to_act)
                S.activation(eb[u % 2], tb[u % 2], ACT.Exp, bias=ctk[:, c, 0, d, h:h + 1], scale=-1.0)\
                    .then_inc(to_dve.sem, 1)

        def second(u):
            i, d, h = UNITS[u]
            c = mchunk(d, i)
            if c >= 2:
                act.wait_ge(prod_read)
                S.activation(t1b[u % 2], psum[4 * (u % 2) + 1][:, 256:512], ACT.Identity,
                             scale=ctk[:, c, 1, d, h:h + 1]).then_inc(to_dve.sem, 1)

        for u in range(len(UNITS) + 1):
            if u < len(UNITS):
                first(u)
            if u:
                second(u - 1)

    unit_read, prod_read = signal("unit_through"), signal("unit_products_seen")

    def mlstm_scan_dve(dve):
        seen = set()

        def first(u):
            i, d, h = UNITS[u]
            c, b = mchunk(d, i), psum[4 * (u % 2)]
            if c < 2:
                return
            dve.wait_ge(prod)
            V.tensor_tensor(tb[u % 2], b[:, P:2 * P], neg128[d], ALU.subtract).then_inc(to_act.sem, 1)
            dve.wait_ge(to_dve)
            V.tensor_tensor(stb[u % 2], b[:, 0:P], eb[u % 2], ALU.mult).then_inc(made.sem, 1)

        def second(u):
            i, d, h = UNITS[u]
            c, b, m = mchunk(d, i), psum[4 * (u % 2):4 * (u % 2) + 4], 4 * d + h
            dve.wait_ge(prod)
            den = dens[u % 2]
            if c >= 2:
                dve.e.sem_inc(prod_read.sem, 1)
                link(dve, dve_step, V.tensor_copy(den[:, 2:4], b[3][:, 0:2]))
                link(dve, dve_step, V.scalar_tensor_tensor(den[:, 0:1], den[:, 3:4], ctk[:, c, 1, d, h:h + 1], den[:, 2:3],
                                                           ALU.mult, ALU.add))
                link(dve, dve_step, V.tensor_scalar(den[:, 1:2], den[:, 0:1], -1.0, ctk[:, c, 2, d, h:h + 1],
                                                    ALU.mult, ALU.max))
                link(dve, dve_step, V.tensor_tensor(den[:, 0:1], den[:, 0:1], den[:, 1:2], ALU.max))
                link(dve, dve_step, V.reciprocal(den[:, 1:2], den[:, 0:1]))
            V.scalar_tensor_tensor(nvec[:, 2 * m:2 * m + 2], nvec[:, 2 * m:2 * m + 2], csb[:, m, c:c + 1], b[3][:, 2:4],
                                   ALU.mult, ALU.add)
            ins = V.scalar_tensor_tensor(state(d, h), state(d, h), csb[:, m, c:c + 1],
                                         b[2][:, :].rearrange("p (a v) -> p a v", a=2), ALU.mult, ALU.add)
            if c >= 2:
                dve.wait_ge(to_dve)
                link(dve, dve_step, V.tensor_tensor(t1b[u % 2], t1b[u % 2], b[1][:, 0:256], ALU.add))
                dst = hacc[:, c - 2, 256 * h:256 * h + 256]
                if (c, h) in seen:
                    ins = V.scalar_tensor_tensor(dst, t1b[u % 2], den[:, 1:2], dst, ALU.mult, ALU.add)
                else:
                    seen.add((c, h))
                    ins = V.tensor_scalar(dst, t1b[u % 2], den[:, 1:2], None, ALU.mult)
            link(dve, unit_read, ins)

        for u in range(len(UNITS) + 1):
            if u < len(UNITS):
                first(u)
            if u:
                second(u - 1)

    def mlstm_out_pe(pe):
        pe.wait_ge(made)
        for n in range(KD):
            if n >= 2:
                pe.wait_ge(bonus_read)
            for c in range(NL):
                ins = M.matmul(psum[n % 2][:, P * c:P * c + P], hacc[:, c, P * n:P * n + P], ident, start=True, stop=True)
            ins.then_inc(prod.sem, 1)
        bonus_read.skip(pe, 2)

    def mlstm_out_act(act):
        for n in range(KD):
            S.activation(xcT[:, n, CTX:T], xcT[:, n, CTX:T], ACT.Identity, scale=cols("c_skip", n))\
                .then_inc(to_dve.sem, 1)
        act.wait_ge(ms_ready)
        S.activation(mstat, mstat, ACT.Sqrt).then_inc(root_ready.sem, 1)

    def mlstm_out_dve(dve):
        h4 = hacc.rearrange("p c (h v) -> p (c h) v", h=4)
        sq = flat(vtk)[:, 0:NL * D].rearrange("p (m v) -> p m v", v=256)
        link(dve, dve_step, V.tensor_tensor(sq, h4, h4, ALU.mult))
        link(dve, dve_step, V.tensor_reduce(mstat, sq, AX, ALU.add))
        V.tensor_scalar(mstat, mstat, 1.0 / 256, EPS, ALU.mult, ALU.add).then_inc(ms_ready.sem, 1)
        dve.wait_ge(root_ready)
        link(dve, dve_step, V.reciprocal(mstat, mstat))
        V.tensor_tensor(h4, h4, mstat.unsqueeze(2).to_broadcast([P, 16, 256]), ALU.mult).then_inc(made.sem, 1)
        for n in range(KD):
            dve.wait_ge(prod)
            dve.wait_ge(to_dve)
            t = xcT[:, n, CTX:T]
            link(dve, bonus_read, V.scalar_tensor_tensor(t, psum[n % 2][:, :], cols("c_norm", n), t, ALU.mult, ALU.add))
            V.tensor_tensor(zT[:, n, :], t, zT[:, n, :], ALU.mult)

    ysq1 = vtk.rearrange("p c f -> p (c f)").rearrange("p (k t) -> p k t", k=KD)

    droom = Room()
    half = lambda n: droom.take(n * LAT).rearrange("p (k t) -> p k t", k=n)
    qkvT = half(12)
    zaT = half(4)
    ktok, vtok2, oacc = (droom.take(NL * 512).rearrange("p (c h v) -> p c h v", c=NL, h=4) for _ in range(3))
    dmask = droom.take(18 * P)
    incl_d = [dmask[:, 0:P], dmask[:, P:2 * P]]
    neg_d = [dmask[:, 2 * P:3 * P], dmask[:, 3 * P:4 * P]]
    lev_d = [[dmask[:, P * (4 + 7 * d + lv):P * (5 + 7 * d + lv)] for lv in range(7)] for d in range(2)]
    wab = droom.take(KD * 16).rearrange("p (k n) -> p k n", k=KD)
    alog = droom.take(16)
    cols4 = lambda: droom.take(32).rearrange("p (c m) -> p c m", c=NL)
    gl, beta, gx, Gc, Gt, eG, kdc, dl = (cols4() for _ in range(8))
    dstat = droom.take(16)
    drt = droom.take(T)
    d_at = droom.at
    aroom = Room(d_at)
    fraw = [aroom.take(LAT + 4) for _ in range(2)]
    sqb = aroom.take(4 * LAT)
    msb = aroom.take(4 * LAT)
    sroomd = Room(d_at)
    f4 = lambda: sroomd.take(4 * P).rearrange("p (h t) -> p h t", h=4)
    AT, LT, PMd, RHd, STd, KDC, QD, DM, LMd0, LMd1, XD, XTd = ([f4() for _ in range(2)] for _ in range(12))
    LMd = [[LMd0[d], LMd1[d]] for d in range(2)]
    broom = Room(d_at)
    bh = lambda n: broom.take(n * LAT).rearrange("p (k t) -> p k t", k=n)
    gatesT = bh(16)
    zbT = bh(4)
    ccT = qkvT[:, 0:4, :]
    cfsq = qkvT[:, 4:8, :]
    cpad = [broom.take(LAT + 30) for _ in range(4)]
    sgb = [broom.take(LAT) for _ in range(2)]
    vbb = [broom.take(LAT) for _ in range(2)]
    delta_through, val_used = signal("delta_step_through"), signal("values_used")

    def delta_load_sp(sp, l):
        if l == 0:
            sp.e.dma_start(dmask, A["delta_masks"][:, 0:18 * P]).then_inc(extra_in.sem, 16)
        for dst, src in ((wab, A[f"ab_cols{l}"]), (alog, A[f"decay_rows{l}"].partition_broadcast(P))):
            sp.e.dma_start(dst, src).then_inc(extra_in.sem, 16)

    assert aroom.at <= HH_D and HH_D + 2 * L8 <= ARENA and WH_FFN + 4 * D <= ARENA

    def delta_split_act(act, ready, high):
        for k in range(KD):
            if ready:
                act.wait_ge(to_act)
            S.activation(high[:, k, :], hT[:, k, CTX:T], ACT.Identity).then_inc(to_dve.sem, 1)

    def delta_split_dve(dve, high, low):
        for k in range(KD):
            dve.wait_ge(to_dve)
            ins = V.tensor_tensor(low(k), hT[:, k, CTX:T], high[:, k, :].bitcast(F32), ALU.subtract)
        return ins

    def delta_in_pe(pe, l):
        block_starts["delta", l] = pe.items
        loaded(pe, 12 + 2 * l)
        for c in range(NL):
            for k in range(KD):
                ins = M.matmul(psum[6][:, 16 * c:16 * c + 16], hT[:, k, CTX + P * c:CTX + P * c + P], wab[:, k, :],
                               start=(k == 0), stop=(k == KD - 1))
        ins.then_inc(prod.sem, 1)
        split_product_pe(pe, 16, wh_d, part(hh_d, CTX), part(hl_d, CTX), LATENT)

    def delta_in_act(act, l):
        act.wait_ge(to_act)
        link(act, act_step, S.activation(gl, gx, ACT.Abs))
        link(act, act_step, S.activation(gl, gl, ACT.Exp, scale=-1.0))
        S.activation(gl, gl, ACT.Ln, bias=ones[:, 0:1]).then_inc(to_dve.sem, 1)
        link(act, act_step, S.activation(alog[:, 0:8], alog[:, 0:8], ACT.Exp))
        S.activation(beta, psum[6][:, 0:64].rearrange("p (c a m) -> p c a m", c=NL, a=2)[:, :, 1, :], ACT.Sigmoid)\
            .then_inc(to_dve.sem, 1)
        for i in range(13):
            if i < 12:
                act.wait_ge(item_done)
                S.activation(fraw[i % 2][:, 2:2 + LAT], bank_of(act.tiles % 2, LATENT[0]), ACT.Identity)\
                    .then_inc(tile_read.sem, 1)
                act.tiles += 1
            if i:
                act.wait_ge(to_act)
                S.activation(qkvT[:, i - 1, :], qkvT[:, i - 1, :], ACT.Silu)
        tiles_act(act, 4, lambda i, p: S.activation(zaT[:, i, :], bank_of(p, LATENT[0]), ACT.Silu), loop=False)

    def delta_in_dve(dve, l):
        for q in range(2):
            V.memset(fraw[q][:, 0:2], 0.0)
            link(dve, dve_step, V.memset(fraw[q][:, LAT + 2:LAT + 4], 0.0))
        loaded(dve, 12 + 2 * l)
        dve.wait_ge(prod)
        V.tensor_tensor(gx, psum[6][:, 0:64].rearrange("p (c a m) -> p c a m", c=NL, a=2)[:, :, 0, :],
                        alog[:, 8:16].unsqueeze(1).to_broadcast([P, NL, 8]), ALU.add).then_inc(to_act.sem, 1)
        dve.wait_ge(to_dve, 2)
        link(dve, dve_step, V.scalar_tensor_tensor(gl, gx, 0.0, gl, ALU.max, ALU.add))
        link(dve, dve_step, V.scalar_tensor_tensor(gl, gl, -1.0, alog[:, 0:8].unsqueeze(1).to_broadcast([P, NL, 8]),
                                                   ALU.mult, ALU.mult))
        for i in range(12):
            dve.wait_ge(tile_read)
            w = lambda tap: cols("qkv_conv", 12 * (5 * l + tap) + i)
            y = qkvT[:, i, :]
            link(dve, dve_step, V.tensor_scalar(y, fraw[i % 2][:, 0:LAT], w(0), None, ALU.mult))
            for tap in range(1, 5):
                ins = V.scalar_tensor_tensor(y, fraw[i % 2][:, tap:tap + LAT], w(tap), y, ALU.mult, ALU.add)
                if tap < 4:
                    link(dve, dve_step, ins)
                else:
                    ins.then_inc(to_act.sem, 1)
        tile_read.skip(dve, 4)

    def delta_norm_pe(pe):
        for r in range(2):
            pe.wait_ge(sq_ready)
            for j in range(4):
                ins = M.matmul(psum[4 * r + j][:, :], ones, sqb[:, LAT * j:LAT * j + LAT], start=True, stop=True)
            ins.then_inc(sum_ready.sem, 1)

    def delta_norm_act(act):
        for r in range(2):
            if r:
                act.wait_ge(to_act)
            S.activation(sqb, flat(qkvT)[:, 2048 * r:2048 * r + 2048], ACT.Square).then_inc(sq_ready.sem, 1)
            act.wait_ge(ms_ready)
            S.activation(msb, msb, ACT.Sqrt).then_inc(root_ready.sem, 1)

    def delta_norm_dve(dve):
        for r in range(2):
            dve.wait_ge(sum_ready)
            if r == 0:
                V.engine_nop().then_inc(to_act.sem, 1)
            scale = (float(P), P * EPS) if r == 0 else (1.0, EPS)
            for j in range(4):
                ins = V.tensor_scalar(msb[:, LAT * j:LAT * j + LAT], psum[4 * r + j][:, :], scale[0], scale[1],
                                      ALU.mult, ALU.add)
            ins.then_inc(ms_ready.sem, 1)
            dve.wait_ge(root_ready)
            link(dve, dve_step, V.reciprocal(msb, msb))
            t = flat(qkvT)[:, 2048 * r:2048 * r + 2048]
            link(dve, dve_step, V.tensor_tensor(t, t, msb, ALU.mult))

    def delta_turn_pe(pe):
        for c in range(NL):
            for a in range(2):
                for h in range(4):
                    ins = M.matmul(psum[2 * c + a][:, P * h:P * h + P], qkvT[:, 4 + 4 * a + h, P * c:P * c + P], ident,
                                   start=True, stop=True)
            ins.then_inc(prod_act.sem, 1)
        pe.wait_ge(made_act)
        for c in range(NL):
            for d in range(2):
                at = 8 * c + 4 * d
                M.matmul(psum[0][:, at:at + 4], incl_d[d], gl[:, c, 4 * d:4 * d + 4], start=True, stop=True)
                ins = M.matmul(psum[0][:, 64 + at:64 + at + 4], ones, gl[:, c, 4 * d:4 * d + 4], start=True, stop=True)
        ins.then_inc(prod.sem, 1)

    def delta_turn_act(act):
        for c in range(NL):
            act.wait_ge(prod_act)
            b = 2 * c
            ins = S.activation(ktok[:, c], psum[b][:, :].rearrange("p (h v) -> p h v", h=4), ACT.Identity)
            if c == 0:
                ins.then_inc(made_act.sem, 1)
            S.activation(vtok2[:, c], psum[b + 1][:, :].rearrange("p (h v) -> p h v", h=4), ACT.Identity)
        act.wait_ge(to_act)
        link(act, act_step, S.activation(eG, Gc, ACT.Exp))
        link(act, act_step, S.activation(kdc, kdc, ACT.Exp))
        link(act, act_step, S.activation(dl, Gt, ACT.Exp))

    def delta_turn_dve(dve):
        dve.wait_ge(prod)
        link(dve, dve_step, V.tensor_copy(Gc, psum[0][:, 0:32].rearrange("p (c m) -> p c m", c=NL)))
        link(dve, dve_step, V.tensor_copy(Gt, psum[0][:, 64:96].rearrange("p (c m) -> p c m", c=NL)))
        V.tensor_tensor(kdc, Gt, Gc, ALU.subtract).then_inc(to_act.sem, 1)
        link(dve, dve_step, V.tensor_scalar(gx, Gc, -1.0, None, ALU.mult))
        for d in range(2):
            V.memset(STd[d], 0.0)

    def head_mm(dst, lhs, rhs, start=True, stop=True):
        for h in range(4):
            ins = M.matmul(dst[:, P * h:P * h + P], lhs(h), rhs(h), start=start, stop=stop)
        return ins

    def delta_scan_pe(pe):
        B = [[psum[4 * d + i] for i in range(4)] for d in range(2)]
        for i in range(NL):
            for d in range(2):
                c = i if d == 0 else NL - 1 - i
                at = slice(P * c, P * c + P)
                kc, qc = (lambda h: qkvT[:, 4 + h, at]), (lambda h: qkvT[:, h, at])
                if i:
                    pe.wait_ge(delta_through)
                head_mm(B[d][0], lambda h: gl[:, c, 4 * d + h:4 * d + h + 1].to_broadcast([P, P]), lambda h: incl_d[d])\
                    .then_inc(prod_act.sem, 1)
                head_mm(B[d][1], kc, kc)
                head_mm(B[d][2], kc, qc).then_inc(prod.sem, 1)
                head_mm(B[d][3], kc, lambda h: STd[d][:, h, :]).then_inc(prod.sem, 1)
            for lv in range(7):
                for d in range(2):
                    pe.wait_ge(made, 2 if d and lv > 1 else 1)
                    ins = head_mm(B[d][0], lambda h: LMd[d][lv % 2][:, h, :],
                                  (lambda h: ident) if lv == 0 else (lambda h: XD[d][:, h, :]))
                    ins.then_inc((prod if lv == 0 else prod_act).sem, 1)
                if lv == 0:
                    continue
                for d in range(2):
                    pe.wait_ge(made_act)
                    if d and lv > 1:
                        pe.wait_ge(made)
                    if lv < 6:
                        head_mm(B[d][1], lambda h: XTd[d][:, h, :], lambda h: PMd[d][:, h, :]).then_inc(prod.sem, 1)
                    if lv > 4:
                        head_mm(B[d][2], lambda h: PMd[d][:, h, :], lambda h: XTd[d][:, h, :]).then_inc(prod.sem, 1)
            for d in range(2):
                pe.wait_ge(made)
                head_mm(B[d][3], lambda h: XTd[d][:, h, :], lambda h: RHd[d][:, h, :]).then_inc(prod.sem, 1)
            for d in range(2):
                pe.wait_ge(made)
                for h in range(4):
                    hs = slice(P * h, P * h + P)
                    M.matmul(B[d][0][:, hs], QD[d][:, h, :], STd[d][:, h, :], start=True, stop=False)
                    ins = M.matmul(B[d][0][:, hs], AT[d][:, h, :], RHd[d][:, h, :], start=False, stop=True)
                head_mm(B[d][1], lambda h: KDC[d][:, h, :], lambda h: RHd[d][:, h, :]).then_inc(prod.sem, 1)
        delta_through.skip(pe, 2)

    def delta_scan_act(act):
        B = [[psum[4 * d + i] for i in range(4)] for d in range(2)]
        for i in range(NL):
            for d in range(2):
                act.wait_ge(prod_act)
                S.activation(QD[d], B[d][0][:, :].rearrange("p (h t) -> p h t", h=4), ACT.Exp)
                S.activation(DM[d], B[d][0][:, :].rearrange("p (h t) -> p h t", h=4), ACT.Identity)\
                    .then_inc(to_dve.sem, 1)
            for d in range(2):
                c = i if d == 0 else NL - 1 - i
                act.wait_ge(to_act)
                for h in range(4):
                    ins = S.activation(DM[d][:, h, :], DM[d][:, h, :], ACT.Exp, bias=gx[:, c, 4 * d + h:4 * d + h + 1])
                ins.then_inc(to_dve.sem, 1)
            for lv in range(1, 7):
                for d in range(2):
                    act.wait_ge(prod_act)
                    S.activation(PMd[d], B[d][0][:, :].rearrange("p (h t) -> p h t", h=4), ACT.Identity)\
                        .then_inc(made_act.sem, 1)

    def delta_scan_dve(dve):
        B = [[psum[4 * d + i][:, :].rearrange("p (h t) -> p h t", h=4) for i in range(4)] for d in range(2)]
        eye = ident.unsqueeze(1).to_broadcast([P, 4, P])
        every = lambda t, c, d: t[:, c, 4 * d:4 * d + 4].unsqueeze(2).to_broadcast([P, 4, P])
        came = set()
        for i in range(NL):
            for d in range(2):
                c = i if d == 0 else NL - 1 - i
                at = slice(P * c, P * c + P)
                level = lambda lv: lev_d[d][lv].unsqueeze(1).to_broadcast([P, 4, P])
                dve.wait_ge(to_dve)
                V.tensor_tensor(DM[d], DM[d], neg_d[d].unsqueeze(1).to_broadcast([P, 4, P]), ALU.add)\
                    .then_inc(to_act.sem, 1)
            for d in range(2):
                c = i if d == 0 else NL - 1 - i
                level = lambda lv: lev_d[d][lv].unsqueeze(1).to_broadcast([P, 4, P])
                dve.wait_ge(prod, 2)
                dve.wait_ge(to_dve)
                link(dve, dve_step, V.tensor_tensor(LT[d], B[d][1], DM[d], ALU.mult))
                link(dve, dve_step, V.tensor_tensor(LT[d], LT[d], every(beta, c, d), ALU.mult))
                link(dve, dve_step, V.tensor_tensor(LMd[d][0], LT[d], level(0), ALU.mult))
                V.scalar_tensor_tensor(XTd[d], LMd[d][0], -1.0, eye, ALU.mult, ALU.add).then_inc(made.sem, 1)
                V.tensor_tensor(AT[d], B[d][2], DM[d], ALU.mult)
            for lv in range(7):
                for d in range(2):
                    level = lambda lv: lev_d[d][lv].unsqueeze(1).to_broadcast([P, 4, P])
                    if lv < 6:
                        V.tensor_tensor(LMd[d][(lv + 1) % 2], LT[d], level(lv + 1), ALU.mult)
                    dve.wait_ge(prod)
                    if lv == 0:
                        V.scalar_tensor_tensor(XD[d], B[d][0], -1.0, eye, ALU.mult, ALU.add).then_inc(made.sem, 1)
                        continue
                    if lv < 6:
                        link(dve, dve_step, V.tensor_tensor(XD[d], XD[d], B[d][1], ALU.subtract))
                        dve.e.sem_inc(made.sem, 1)
                    if lv <= 4:
                        for q in range(4):
                            at = slice(32 * q, 32 * q + 32)
                            ins = V.transpose(XTd[d][at, :, at], XD[d][at, :, at])
                        ins.then_inc(made.sem, 1)
                    else:
                        if lv < 6:
                            dve.wait_ge(prod)
                        V.tensor_tensor(XTd[d], XTd[d], B[d][2], ALU.subtract).then_inc(made.sem, 1)
                    c = i if d == 0 else NL - 1 - i
                    if lv == 1:
                        V.tensor_tensor(QD[d], QD[d], qkvT[:, 0:4, P * c:P * c + P], ALU.mult)
                    elif lv == 2:
                        V.tensor_tensor(KDC[d], ktok[:, c], every(kdc, c, d), ALU.mult)
                    elif lv == 3:
                        V.tensor_tensor(RHd[d], B[d][3], every(eG, c, d), ALU.mult)
                    elif lv == 5:
                        V.tensor_tensor(RHd[d], vtok2[:, c], RHd[d], ALU.subtract)
            for d in range(2):
                c = i if d == 0 else NL - 1 - i
                dve.wait_ge(prod)
                V.tensor_tensor(RHd[d], B[d][3], every(beta, c, d), ALU.mult).then_inc(made.sem, 1)
            for d in range(2):
                c = i if d == 0 else NL - 1 - i
                dve.wait_ge(prod)
                link(dve, dve_step, V.tensor_tensor(STd[d], STd[d], every(dl, c, d), ALU.mult))
                V.tensor_tensor(STd[d], STd[d], B[d][1], ALU.add)
                if c in came:
                    ins = V.tensor_tensor(oacc[:, c], oacc[:, c], B[d][0], ALU.add)
                else:
                    came.add(c)
                    ins = V.tensor_copy(oacc[:, c], B[d][0])
                link(dve, delta_through, ins)

    def branch_pe(pe, l):
        block_starts["branch", l] = pe.items
        pe.wait_ge(made)
        split_product_pe(pe, 28, wh_d, part(hh_b, CTX), part(hlT), LATENT)

    def branch_act(act, l):
        delta_split_act(act, False, hh_b)
        for i in range(4):
            act.wait_ge(item_done)
            if i >= 2:
                act.wait_ge(val_used)
            S.activation(sgb[i % 2], bank_of(act.tiles % 2, LATENT[0]), ACT.Sigmoid).then_inc(tile_read.sem, 1)
            act.wait_ge(item_done)
            S.activation(vbb[i % 2], bank_of((act.tiles + 1) % 2, LATENT[0]), ACT.Identity).then_inc(tile_read.sem, 1)
            act.tiles += 2
        val_used.skip(act, 2)
        tiles_act(act, 4, lambda i, p: S.activation(zbT[:, i, :], bank_of(p, LATENT[0]), ACT.Silu), loop=False)
        tiles_act(act, 16, lambda i, p: S.activation(gatesT[:, i, :], bank_of(p, LATENT[0]), ACT.Sigmoid,
                                                     bias=cols("gate_b", 16 * l + i)), loop=False)

    def branch_dve(dve, l):
        delta_split_dve(dve, hh_b, lambda k: hlT[:, k, CTX:T]).then_inc(made.sem, 1)
        for q in range(4):
            V.memset(cpad[q][:, 0:15], 0.0)
            link(dve, dve_step, V.memset(cpad[q][:, LAT + 15:LAT + 30], 0.0))
        for i in range(4):
            dve.wait_ge(tile_read, 2)
            ins = V.tensor_tensor(cpad[i][:, 15:15 + LAT], sgb[i % 2], vbb[i % 2], ALU.mult)
            link(dve, val_used, ins)
            y = ccT[:, i, :]
            w = lambda tap: cols("cf_conv", 4 * (31 * l + tap) + i)
            link(dve, dve_step, V.tensor_scalar(y, cpad[i][:, 0:LAT], w(0), cols("cf_conv_b", 4 * l + i),
                                                ALU.mult, ALU.add))
            for tap in range(1, 31):
                link(dve, dve_step, V.scalar_tensor_tensor(y, cpad[i][:, tap:tap + LAT], w(tap), y, ALU.mult, ALU.add))
        tile_read.skip(dve, 20)

    blocks_before = []
    joined = signal("joined")
    ymixT = qkvT[:, 4:12, :]
    osq = broom.take(4 * LAT)
    t2b = [sgb[0], sgb[1]]

    def join_pe(pe):
        for j in range(4):
            ins = M.matmul(psum[4][:, :], ones, ccT[:, j, :], start=(j == 0), stop=(j == 3))
        ins.then_inc(prod.sem, 1)
        pe.wait_ge(sq_ready)
        for j in range(4):
            ins = M.matmul(psum[5][:, :], ones, cfsq[:, j, :], start=(j == 0), stop=(j == 3))
        ins.then_inc(sum_ready.sem, 1)
        pe.wait_ge(made)
        for h in range(4):
            for c in range(NL):
                ins = M.matmul(psum[h][:, P * c:P * c + P], oacc[:, c, h, :], ident, start=True, stop=True)
            ins.then_inc(prod.sem, 1)
        pe.wait_ge(made)
        blocks_before.append(pe.items)
        for n in range(KD):
            slot = pe.items % SLOTS
            if n >= 2:
                pe.wait_ge(joined)
            pe.wait_ge(landed[slot], 16)
            for b, src in enumerate((zaT, ccT)):
                for k in range(4):
                    ins = M.matmul(psum[2 * (n % 2) + b][:, :], ring[slot][:, P * (4 * b + k):P * (4 * b + k) + P],
                                   src[:, k, :], start=(k == 0), stop=(k == 3))
            ins.then_inc(item_done.sem, 1)
            pe.items += 1
        joined.skip(pe, 2)
        pe.wait_ge(made)
        for n in range(KD):
            slot = pe.items % SLOTS
            if n >= 2:
                pe.wait_ge(joined)
            pe.wait_ge(landed[slot], 16)
            for k in range(KD):
                ins = M.matmul(psum[n % 2][:, :], ring[slot][:, P * k:P * k + P], ymixT[:, k, :],
                               start=(k == 0), stop=(k == KD - 1))
            ins.then_inc(item_done.sem, 1)
            pe.items += 1
        joined.skip(pe, 2)

    def join_act(act, l):
        act.wait_ge(to_act)
        S.activation(cfsq, ccT, ACT.Square).then_inc(sq_ready.sem, 1)
        act.wait_ge(ms_ready)
        S.activation(dstat, dstat, ACT.Sqrt).then_inc(root_ready.sem, 1)
        act.wait_ge(ms_ready)
        S.activation(drt[:, 0:LAT], drt[:, 0:LAT], ACT.Sqrt).then_inc(root_ready.sem, 1)
        act.wait_ge(to_act)
        for j in range(4):
            S.activation(ccT[:, j, :], ccT[:, j, :], ACT.Silu, bias=cols("cf_ln_b", 4 * l + j),
                         scale=cols("cf_ln_w", 4 * l + j)).then_inc(to_dve.sem, 1)
        item_done.skip(act, 16)

    def join_dve(dve, l):
        item_done.seen[dve.name] = SLOTS + blocks_before[l]
        mean = drt[:, 0:LAT]
        dve.wait_ge(prod)
        link(dve, dve_step, V.tensor_scalar(mean, psum[4][:, :], 1.0 / 512, None, ALU.mult))
        spread = mean.unsqueeze(1).to_broadcast([P, 4, LAT])
        ins = V.tensor_tensor(ccT, ccT, spread, ALU.subtract)
        link(dve, dve_step, ins)
        V.engine_nop().then_inc(to_act.sem, 1)
        o = oacc.rearrange("p c h v -> p (c h) v")
        sq = osq.rearrange("p (m v) -> p m v", v=P)
        link(dve, dve_step, V.tensor_tensor(sq, o, o, ALU.mult))
        link(dve, dve_step, V.tensor_reduce(dstat, sq, AX, ALU.add))
        V.tensor_scalar(dstat, dstat, 1.0 / P, EPS, ALU.mult, ALU.add).then_inc(ms_ready.sem, 1)
        dve.wait_ge(root_ready)
        link(dve, dve_step, V.reciprocal(dstat, dstat))
        V.tensor_tensor(o, o, dstat.unsqueeze(2).to_broadcast([P, 16, P]), ALU.mult).then_inc(made.sem, 1)
        dve.wait_ge(sum_ready)
        V.tensor_scalar(mean, psum[5][:, :], 1.0 / 512, EPS, ALU.mult, ALU.add).then_inc(ms_ready.sem, 1)
        dve.wait_ge(root_ready)
        link(dve, dve_step, V.reciprocal(mean, mean))
        V.tensor_tensor(ccT, ccT, spread, ALU.mult).then_inc(to_act.sem, 1)
        for h in range(4):
            dve.wait_ge(prod)
            V.scalar_tensor_tensor(zaT[:, h, :], psum[h][:, :], cols("dn_norm", l), zaT[:, h, :], ALU.mult, ALU.mult)
        for j in range(4):
            dve.wait_ge(to_dve)
            ins = V.tensor_tensor(ccT[:, j, :], ccT[:, j, :], zbT[:, j, :], ALU.mult)
        ins.then_inc(made.sem, 1)
        for n in range(KD):
            tile_ready(dve)
            V.tensor_tensor(ymixT[:, n, :], psum[2 * (n % 2)][:, :], gatesT[:, n, :], ALU.mult)
            link(dve, joined, V.tensor_tensor(t2b[n % 2], psum[2 * (n % 2) + 1][:, :], gatesT[:, KD + n, :], ALU.mult))
            ins = V.tensor_tensor(ymixT[:, n, :], ymixT[:, n, :], t2b[n % 2], ALU.add)
        ins.then_inc(made.sem, 1)
        for n in range(KD):
            tile_ready(dve)
            link(dve, joined, V.tensor_tensor(xT[:, n, CTX:T], xT[:, n, CTX:T], psum[n % 2][:, :], ALU.add))
            dve.e.sem_inc(to_act.sem, 1)

    def tile_ready(dve):
        dve.wait_ge(item_done)

    def final_dve(dve):
        rms_dve(dve, LATENT, drt, 1.0 / D)
        for k in range(KD):
            V.scalar_tensor_tensor(hT[:, k, CTX:T], xT[:, k, CTX:T], cols("final_w", k), drt[:, CTX:T],
                                   ALU.mult, ALU.mult)

    block = ctx.enter_context(nc.Block())

    @block.sync
    def _(e):
        sp = Engine("sp", e)
        e.dma_start(vec[:, :], A["vectors"]).then_inc(inputs_in.sem, 16)
        e.dma_start(gen[:, :], A["gen_consts"]).then_inc(inputs_in.sem, 16)
        e.dma_start(xT, A["x_in"]).then_inc(inputs_in.sem, 16)
        weights_sp(sp, A["ada_w0"], 48)
        weights_sp(sp, A["ada_w1"], 48)
        mixer_ab_load_sp(sp)
        weights_sp(sp, A["ab_v"], 4)
        weights_sp(sp, A["ab_in"], 19)
        weights_sp(sp, A["ab_out"], SLOTS)
        for _ in range(6):
            phase(sp)
        e.dma_start(xT, A["x_in"]).then_inc(moved.sem, 16)
        weights_sp(sp, A["ab_out"], 8, start=SLOTS)
        weights_sp(sp, A["ffn_up0"], 2 * KF)
        weights_sp(sp, A["ffn_down0"], 24)
        weights_sp(sp, A["c_in"], SLOTS)
        phase(sp)
        phase(sp)
        mlstm_load_sp(sp)
        weights_sp(sp, A["c_in"], 17, start=SLOTS)
        weights_sp(sp, A["c_out"], 8)
        weights_sp(sp, A["ffn_up1"], 2 * KF)
        weights_sp(sp, A["ffn_down1"], 24)
        for l in range(2):
            weights_sp(sp, A[f"d_in{l}"], SLOTS)
            for _ in range(6):
                phase(sp)
            delta_load_sp(sp, l)
            weights_sp(sp, A[f"d_in{l}"], 16, start=SLOTS)
            weights_sp(sp, A[f"d_branch{l}"], 28)
            weights_sp(sp, A[f"d_join{l}"], 8)
            weights_sp(sp, A[f"d_out{l}"], 8)
        for _ in range(7):
            phase(sp)
        e.dma_start(out, hT[:, :, CTX:T]).then_inc(stored.sem, 16)
        sp.wait_ge(stored, 16)

    @block.tensor
    def _(e):
        pe = Engine("pe", e)
        e.sem_inc(item_done.sem, SLOTS)
        pe.wait_ge(inputs_in, 48)
        pe.wait_ge(made_act)
        rms_pe(pe, lambda k: hT[:, k, :], KD, BOTH)
        ada_pe(pe)
        phase(pe)
        mixer_ab_in_pe(pe)
        phase(pe)
        spatial_pe(pe)
        phase(pe)
        lora_pe(pe)
        phase(pe)
        rwkv_pe(pe)
        phase(pe)
        rwkv_out_pe(pe)
        phase(pe)
        product_pe(pe, 8, mix_in, BOTH)
        rms_pe(pe, sq_l0, KD, BOTH)
        rms_pe(pe, lambda k: hT[:, k, :], KD, BOTH)
        phase(pe)
        ffn_pe(pe, 0, BOTH)
        ffn_down_pe(pe, 0, BOTH)
        rms_pe(pe, lambda k: fsq[:, k, :], KD, BOTH)
        rms_pe(pe, lambda k: hT[:, k, :], KD, BOTH)
        phase(pe)
        mlstm_in_pe(pe)
        phase(pe)
        mlstm_mid_pe(pe)
        phase(pe)
        mlstm_scan_pe(pe)
        phase(pe)
        mlstm_out_pe(pe)
        phase(pe)
        product_pe(pe, 8, lambda k, seg: zT[:, k, :], LATENT)
        rms_pe(pe, lambda k: ysq1[:, k, :], KD, LATENT)
        rms_pe(pe, lambda k: hT[:, k, :], KD, LATENT)
        phase(pe)
        ffn_pe(pe, 1, LATENT)
        ffn_down_pe(pe, 1, LATENT)
        rms_pe(pe, lambda k: fsq[:, k, :], KD, LATENT)
        phase(pe)
        for l in range(2):
            rms_pe(pe, lambda k: hT[:, k, :], KD, LATENT)
            phase(pe)
            delta_in_pe(pe, l)
            phase(pe)
            delta_norm_pe(pe)
            phase(pe)
            delta_turn_pe(pe)
            phase(pe)
            delta_scan_pe(pe)
            phase(pe)
            branch_pe(pe, l)
            phase(pe)
            join_pe(pe)
        rms_pe(pe, lambda k: hT[:, k, :], KD, LATENT)
        phase(pe)

    @block.scalar
    def _(e):
        act = Engine("act", e)
        e.sem_inc(tile_read.sem, 2)
        item_done.skip(act, SLOTS)
        act.wait_ge(inputs_in, 48)
        S.activation(small[:, 0:16], cols("c", 0, 16), ACT.Silu).then_inc(made_act.sem, 1)
        rms_act(act, lambda k: xT[:, k, :], lambda k: hT[:, k, :], KD, BOTH, rtN)
        ada_act(act, ADA_FIRST)
        act.wait_ge(to_act)
        prenorm_act(act, BOTH, 0)
        ada_act(act, ADA_GROUPS - ADA_FIRST)
        phase(act)
        mixer_ab_in_act(act)
        phase(act)
        spatial_act(act)
        phase(act)
        lora_act(act)
        phase(act)
        rwkv_act(act)
        phase(act)
        rwkv_out_act(act)
        phase(act)
        tiles_act(act, 8, keep_squared(yT_l0, sq_l0, BOTH), loop=False)
        root_act(act, BOTH, rtB)
        rms_act(act, lambda k: xT[:, k, :], lambda k: hT[:, k, :], KD, BOTH, frt, added=True)
        prenorm_act(act, BOTH, 3)
        phase(act)
        ffn_act(act, 0, BOTH)
        tiles_act(act, KD, keep_squared(lambda k: hT[:, k, :], lambda k: fsq[:, k, :], BOTH), per=3, loop=False)
        root_act(act, BOTH, frt)
        rms_act(act, lambda k: xT[:, k, :], lambda k: hT[:, k, :], KD, BOTH, frt, added=True)
        prenorm_act(act, BOTH, 0)
        phase(act)
        mlstm_in_act(act)
        phase(act)
        mlstm_mid_act(act)
        phase(act)
        mlstm_scan_act(act)
        phase(act)
        mlstm_out_act(act)
        phase(act)
        tiles_act(act, 8, keep_squared(lambda k: xmT[:, k, :], lambda k: ysq1[:, k, :], LATENT), loop=False)
        root_act(act, LATENT, mrt)
        rms_act(act, lambda k: xT[:, k, :], lambda k: hT[:, k, :], KD, LATENT, frt, added=True)
        prenorm_act(act, LATENT, 3)
        phase(act)
        ffn_act(act, 1, LATENT)
        tiles_act(act, KD, keep_squared(lambda k: hT[:, k, :], lambda k: fsq[:, k, :], LATENT), per=3, loop=False)
        root_act(act, LATENT, frt)
        to_act.skip(act, KD)
        phase(act)
        for l in range(2):
            rms_act(act, lambda k: xT[:, k, :], lambda k: hT[:, k, :], KD, LATENT, drt, added=l > 0)
            delta_split_act(act, True, hh_d)
            phase(act)
            delta_in_act(act, l)
            phase(act)
            delta_norm_act(act)
            phase(act)
            delta_turn_act(act)
            phase(act)
            delta_scan_act(act)
            phase(act)
            branch_act(act, l)
            phase(act)
            join_act(act, l)
        rms_act(act, lambda k: xT[:, k, :], lambda k: hT[:, k, :], KD, LATENT, drt, added=True)
        phase(act)

    @block.vector
    def _(e):
        dve = Engine("dve", e)
        tile_read.skip(dve, 2)
        dve.wait_ge(inputs_in, 48)
        prenorm_dve(dve, BOTH, rtN)
        ada_dve(dve, psum[6], 0, 4 * ADA_FIRST)
        modv_first_dve().then_inc(to_act.sem, 1)
        split_dve(dve, BOTH, hh_ab, to_dve)
        ada_dve(dve, psum[7], 4 * ADA_FIRST, 96)
        modv_dve(dve, 0)
        phase(dve)
        mixer_ab_in_dve(dve)
        phase(dve)
        spatial_dve(dve)
        phase(dve)
        lora_dve(dve)
        phase(dve)
        rwkv_dve(dve)
        phase(dve)
        rwkv_out_dve(dve)
        phase(dve)
        tile_read.skip(dve, 8)
        dve.wait_ge(moved, 16)
        residual_dve(dve, BOTH, yT_l0, rtB, 2)
        prenorm_dve(dve, BOTH, frt)
        split_dve(dve, BOTH, hh_ffn, to_dve)
        phase(dve)
        ffn_dve(dve, 0, BOTH)
        V.drain().then_inc(made.sem, 1)
        tile_read.skip(dve, 8)
        residual_dve(dve, BOTH, lambda k: hT[:, k, :], frt, 5)
        modv_dve(dve, 1)
        prenorm_dve(dve, BOTH, frt)
        split_dve(dve, BOTH, hh_m, to_dve)
        phase(dve)
        mlstm_in_dve(dve)
        phase(dve)
        mlstm_mid_dve(dve)
        phase(dve)
        mlstm_scan_dve(dve)
        phase(dve)
        mlstm_out_dve(dve)
        phase(dve)
        tile_read.skip(dve, 8)
        residual_dve(dve, LATENT, lambda k: xmT[:, k, :], mrt, 2)
        prenorm_dve(dve, LATENT, frt)
        split_dve(dve, LATENT, hh_ffn, to_dve)
        phase(dve)
        ffn_dve(dve, 1, LATENT)
        V.drain().then_inc(made.sem, 1)
        tile_read.skip(dve, 8)
        residual_dve(dve, LATENT, lambda k: hT[:, k, :], frt, 5)
        phase(dve)
        for l in range(2):
            prenorm_dve(dve, LATENT, drt, cols("norm_w", 8 * l, 8))
            delta_split_dve(dve, hh_d, lambda k: hl_d[:, k, :])
            phase(dve)
            delta_in_dve(dve, l)
            phase(dve)
            delta_norm_dve(dve)
            phase(dve)
            delta_turn_dve(dve)
            phase(dve)
            delta_scan_dve(dve)
            phase(dve)
            branch_dve(dve, l)
            phase(dve)
            join_dve(dve, l)
        final_dve(dve)
        phase(dve)

    @block.gpsimd
    def _(e):
        pool = Engine("pool", e)
        def phases(n):
            for _ in range(n):
                phase(pool)

        phases(1)
        split_pool(pool, 23, wh_ab, block_starts["ab"])
        phases(6)
        split_pool(pool, 2 * KF, wh_ffn, block_starts["ffn", 0])
        phases(1)
        split_pool(pool, 17, wh_m, block_starts["mlstm"])
        phases(5)
        split_pool(pool, 2 * KF, wh_ffn, block_starts["ffn", 1])
        phases(1)
        for l in range(2):
            phases(1)
            split_pool(pool, 16, wh_d, block_starts["delta", l])
            phases(4)
            split_pool(pool, 28, wh_d, block_starts["branch", l])
            phases(1)
        phases(1)


def tiles_of(w, n=P):
    import numpy as np
    k, m = w.shape
    return np.ascontiguousarray(w.reshape(k // P, P, m // n, n).transpose(2, 1, 0, 3)).reshape(m // n, P, -1)


def lay_out(I):
    import numpy as np
    r = lambda a: np.asarray(a).reshape(-1, P)
    rows = {"c": np.concatenate([r(I["c"]), r(I["c_ctx"])]), "ada_b": r(I["ada_b"]), "mix_pre": r(I["norm_mix_pre"]),
            "mix_post": r(I["norm_mix_post"]), "ffn_pre": r(I["norm_ffn_pre"]), "ffn_post": r(I["norm_ffn_post"]),
            "ffn_conv": r(I["ffn_conv"]), "ffn_conv_b": r(I["ffn_conv_b"]), "norm_w": r(I["norm_w_2"]),
            "qkv_conv": r(I["qkv_conv_w_2"]), "dn_norm": r(I["dn_norm_w_2"]), "cf_conv": r(I["cf_conv_w_2"]),
            "cf_conv_b": r(I["cf_conv_b_2"]), "cf_ln_w": r(I["cf_ln_w_2"]), "cf_ln_b": r(I["cf_ln_b_2"]),
            "gate_b": r(I["gate_b_2"]), "final_w": r(I["final_norm_w_2"])}
    for name, _ in VECTORS:
        if name not in rows:
            rows[name] = r(I[name])
    L = {"vectors": np.ascontiguousarray(np.concatenate([rows[n] for n, _ in VECTORS]).T),
         "gen_consts": general_constants(), "rwkv_masks": rwkv_constants(), "delta_masks": delta_constants()}
    x = np.concatenate([I["ctx"][0], I["x"][0]]).T
    L["x_in"] = np.ascontiguousarray(x.reshape(KD, P, T).transpose(1, 0, 2))
    w = I["ab_w_in"][0]
    aw = 512
    L["ab_v"] = np.ascontiguousarray(w[:, aw:2 * aw].reshape(4, 2, P, aw).transpose(0, 2, 1, 3)).reshape(4, P, 2 * aw)
    o = 2 * aw + 3 * 512
    L["ab_in"] = tiles_of(np.concatenate([w[:, 0:aw], w[:, o:o + 384], w[:, 2 * aw:o]], 1))
    lora = np.concatenate([I["b_w_up"][0].reshape(P, 512), I["b_a_up"][0].reshape(P, 512), I["b_g_up"][0]], 1)
    L["lora_w"] = np.ascontiguousarray(lora)
    L["a_wsT"] = np.ascontiguousarray(I["a_ws"][0].transpose(2, 0, 1)).reshape(P, 512)
    L["a_bs"] = I["a_bs"][0].reshape(512)
    L["ab_out"] = tiles_of(I["ab_w_out"][0])
    w = I["c_w_in"][0]
    gates = np.zeros((D, 4, 32), w.dtype)
    gates[:, :, 0:4] = w[:, 2 * D:].reshape(D, 4, 4)
    L["c_in"] = tiles_of(np.concatenate([w[:, :2 * D], gates.reshape(D, P)], 1))
    gc = np.zeros((4, 32), w.dtype)
    gc[0:2, 0:4], gc[2:4, 0:4] = I["c_bi"][0], I["c_bf"][0]
    L["gate_cols"] = gc.reshape(P, 1)
    L["c_out"] = tiles_of(I["c_w_out"][0])
    q = np.stack([I["c_wq"][0], I["c_wk"][0], I["c_wv"][0]]).reshape(3, KD, P, 4)
    L["qkv_blocks"] = np.ascontiguousarray(q.transpose(2, 0, 1, 3)).reshape(P, 96)
    for l in range(2):
        w = I["w_in_2"][l]
        L[f"d_in{l}"] = tiles_of(w[:, 0:2048])
        L[f"ab_cols{l}"] = np.ascontiguousarray(w[:, 2048:2064].reshape(KD, P, 16).transpose(1, 0, 2))
        L[f"decay_rows{l}"] = np.concatenate([I["a_log_2"][l].reshape(8), I["dt_bias_2"][l].reshape(8)])
        val, glu, rest = w[:, 2064:2576].reshape(D, 4, P), w[:, 2576:3088].reshape(D, 4, P), w[:, 3088:]
        L[f"d_branch{l}"] = tiles_of(np.concatenate([np.stack([glu, val], 2).reshape(D, 1024), rest], 1))
        both = np.concatenate([I["w_dn_out_2"][l], I["w_cf_out_2"][l]])
        L[f"d_join{l}"] = tiles_of(both)
        L[f"d_out{l}"] = tiles_of(I["w_out_2"][l])
    for l in range(2):
        L[f"ada_w{l}"] = np.ascontiguousarray(I["ada_w"][l].reshape(4, 2, P, 12, 512).transpose(3, 0, 2, 1, 4))\
            .reshape(48, P, 2 * 512)
        up = I["ffn_up"][l].reshape(D, 2, KF, P).transpose(0, 2, 1, 3).reshape(D, 2 * DFF)
        L[f"ffn_up{l}"] = tiles_of(up)
        L[f"ffn_down{l}"] = down_blocks(I["ffn_down"][l])
    return L


def down_blocks(w):
    import numpy as np
    full = np.concatenate([w, np.zeros((2 * P, D), w.dtype)])
    t = tiles_of(full)
    return np.ascontiguousarray(t.reshape(KD, P, 3, 8 * P).transpose(0, 2, 1, 3)).reshape(24, P, 8 * P)


def kernel(**inputs):
    import numpy as np
    import concourse.bacc as bacc
    from concourse.bass_utils import run_bass_kernel_spmd

    nc = bacc.Bacc("TRN2", target_bir_lowering=False, num_devices=1)
    arrays, A = {}, {}
    for name, a in lay_out({n: np.asarray(v) for n, v in inputs.items()}).items():
        a = np.ascontiguousarray(a)
        arrays[f"in_{name}_dram"] = a
        A[name] = nc.dram_tensor(f"in_{name}_dram", a.shape, mybir.dt.from_np(a.dtype), kind="ExternalInput").ap()
    out = nc.dram_tensor("out_0_dram", (P, KD, LAT), F32, kind="ExternalOutput").ap()
    program(nc, A, out)
    r = run_bass_kernel_spmd(nc, [arrays], core_ids=[0])
    got = r.results[0]["out_0_dram"]
    return np.ascontiguousarray(got.transpose(1, 0, 2).reshape(D, LAT).T).reshape(1, LAT, D)
```
